# Optimizing a Trainium2 kernel written in Bass

```python
import math
import jax, jax.numpy as jnp
from jax import lax
import numpy as np

D_MODEL = 1024
BATCH = 1
SEQ = 128
DEPTH = 2
DEC_BATCH = 1
DEC_SEQ = 256
PAST_LEN = 128

GRID_W = 64
D_MIX = D_MODEL
ATT_WIDTH = D_MIX // 4
SSD_WIDTH = 3 * D_MIX // 8
RWKV_WIDTH = D_MIX - ATT_WIDTH - SSD_WIDTH
SSD_HEAD_DIM = 64
SSD_HEADS = SSD_WIDTH // SSD_HEAD_DIM
SSD_GROUPS = 2
SSD_STATE = 64
SSD_CONV = 5
SSD_CHUNK = 128
SSD_CONV_DIM = SSD_WIDTH + 2 * SSD_GROUPS * SSD_STATE
RWKV_HEAD_DIM = 64
RWKV_HEADS = RWKV_WIDTH // RWKV_HEAD_DIM
DECAY_LORA = 64
AAA_LORA = 64
GATE_LORA = 128
RWKV_GN_EPS = 64e-5
ATT_V_DIM = 64
ATT_HEADS = ATT_WIDTH // ATT_V_DIM
ATT_QK_DIM = ATT_V_DIM // 2
ATT_Q_BLOCK = 128
ROPE_BASE = 10000.0
N_GROUPS = 4
EXPERTS_PER_GROUP = 4
N_EXPERTS = N_GROUPS * EXPERTS_PER_GROUP
EXPERT_HIDDEN = D_MODEL // 4
NORM_EPS = 1e-6

IN_WIDTHS = (SSD_CONV_DIM, SSD_WIDTH, 2 * SSD_HEADS,
             RWKV_WIDTH, RWKV_WIDTH, RWKV_WIDTH, DECAY_LORA, AAA_LORA, GATE_LORA,
             ATT_HEADS * 2 * ATT_QK_DIM, ATT_HEADS * 2 * ATT_QK_DIM, ATT_HEADS * ATT_V_DIM)
N_IN = sum(IN_WIDTHS)
IN_SPLITS = tuple(sum(IN_WIDTHS[:i + 1]) for i in range(len(IN_WIDTHS) - 1))

kernel_name = 'hybrid_ssd_rwkv7_diffattn_hmoe_prefix_dit_step'

F32 = jnp.float32

def rmsnorm(x, g, eps=NORM_EPS):
    xf = x.astype(F32)
    y = xf * lax.rsqrt(jnp.mean(xf * xf, axis=-1, keepdims=True) + eps)
    return (y * g.astype(F32)).astype(x.dtype)

def dwconv_centred(x, w, b):
    K = w.shape[0]
    y = lax.conv_general_dilated(x, w[:, None, :].astype(x.dtype), window_strides=(1,),
                                 padding=[(K // 2, K // 2)],
                                 dimension_numbers=('NWC', 'WIO', 'NWC'),
                                 feature_group_count=x.shape[-1])
    return y + b

def segsum(a):
    T = a.shape[-1]
    ae = jnp.broadcast_to(a[..., :, None], a.shape + (T,))
    ae = jnp.where(jnp.tril(jnp.ones((T, T), bool), -1), ae, 0.0)
    ss = jnp.cumsum(ae, axis=-2)
    return jnp.where(jnp.tril(jnp.ones((T, T), bool), 0), ss, -jnp.inf)

def ssd_scan(X, dA, Bh, Ch, init):
    b, s, h, p = X.shape
    n = Bh.shape[-1]
    q = SSD_CHUNK if s % SSD_CHUNK == 0 else s
    c = s // q
    dt = X.dtype
    Xc = X.reshape(b, c, q, h, p)
    Bc = Bh.reshape(b, c, q, h, n)
    Cc = Ch.reshape(b, c, q, h, n)
    A = jnp.transpose(dA.astype(F32).reshape(b, c, q, h), (0, 3, 1, 2))
    A_cs = jnp.cumsum(A, axis=-1)
    L = jnp.exp(segsum(A)).astype(dt)
    y_diag = jnp.einsum('bclhn,bcshn,bhcls,bcshp->bclhp', Cc, Bc, L, Xc)
    decay_states = jnp.exp(A_cs[..., -1:] - A_cs).astype(dt)
    states = jnp.einsum('bclhn,bhcl,bclhp->bchpn', Bc, decay_states, Xc)
    states = jnp.concatenate([init.astype(dt)[:, None], states], axis=1)
    chunk_tot = jnp.pad(A_cs[..., -1], ((0, 0), (0, 0), (1, 0)))
    decay_chunk = jnp.exp(segsum(chunk_tot)).astype(dt)
    new_states = jnp.einsum('bhzc,bchpn->bzhpn', decay_chunk, states)
    states, final = new_states[:, :-1], new_states[:, -1]
    y_off = jnp.einsum('bclhn,bchpn,bhcl->bclhp', Cc, states, jnp.exp(A_cs).astype(dt))
    return (y_diag + y_off).reshape(b, s, h, p), final

def ssd_branch(xbc, z, dt_raw, lp, init):
    xbc = jax.nn.silu(dwconv_centred(xbc, lp['ssd_conv_w'], lp['ssd_conv_b']))
    xs, bm, cm = jnp.split(xbc, [SSD_WIDTH, SSD_WIDTH + SSD_GROUPS * SSD_STATE], axis=-1)
    b, s, _ = xs.shape
    rep = SSD_HEADS // SSD_GROUPS
    xh = xs.reshape(b, s, SSD_HEADS, SSD_HEAD_DIM)
    bh = jnp.repeat(bm.reshape(b, s, SSD_GROUPS, SSD_STATE), rep, axis=2)
    ch = jnp.repeat(cm.reshape(b, s, SSD_GROUPS, SSD_STATE), rep, axis=2)
    dt = jax.nn.softplus(dt_raw.reshape(b, s, 2, SSD_HEADS) + lp['ssd_dt_bias'])
    a = -jnp.exp(lp['ssd_a_log'])
    rev = lambda t: jnp.flip(t, axis=1)
    y_f, s_f = ssd_scan(xh * dt[:, :, 0, :, None], dt[:, :, 0] * a[0], bh, ch, init[:, 0])
    y_b, s_b = ssd_scan(rev(xh * dt[:, :, 1, :, None]), rev(dt[:, :, 1] * a[1]), rev(bh), rev(ch), init[:, 1])
    y = y_f + rev(y_b) + lp['ssd_d'][:, None] * xh
    y = y.reshape(b, s, SSD_WIDTH) * jax.nn.silu(z)
    return rmsnorm(y, lp['ssd_norm_g']), jnp.stack([s_f, s_b], axis=1)

def rwkv_scan(r, w, k, v, kk, kka, s0, reverse):
    dt = s0.dtype
    xs = tuple(jnp.moveaxis(t.astype(dt), 1, 0) for t in (r, w, k, v, kk, kka))

    def step(S, inp):
        r_t, w_t, k_t, v_t, kk_t, kka_t = inp
        sa = jnp.einsum('bhvk,bhk->bhv', S, kk_t)
        S = (S * w_t[:, :, None, :] - sa[..., None] * kka_t[:, :, None, :]
             + v_t[..., None] * k_t[:, :, None, :])
        return S, jnp.einsum('bhvk,bhk->bhv', S, r_t)

    s_final, ys = lax.scan(step, s0, xs, reverse=reverse)
    return jnp.moveaxis(ys, 0, 1), s_final

def rwkv_branch(r, k, v, xw, xa, xg, lp, init):
    b, s, _ = r.shape
    heads = lambda t: t.reshape(b, s, RWKV_HEADS, RWKV_HEAD_DIM)
    g = jax.nn.sigmoid(xg) @ lp['rwkv_g2']
    kk = heads(k * lp['rwkv_kk']).astype(F32)
    kk = (kk * lax.rsqrt(jnp.maximum(jnp.sum(kk * kk, axis=-1, keepdims=True), 1e-24))).astype(k.dtype)
    tw = jnp.tanh(xw)
    ys, finals = [], []
    for d in range(2):
        wl = lp['rwkv_w0'][d] + tw @ lp['rwkv_w2'][d]
        decay = jnp.exp(-jnp.exp(-jax.nn.softplus(-wl) - 0.5))
        a = jax.nn.sigmoid(lp['rwkv_a0'][d] + xa @ lp['rwkv_a2'][d])
        kd = k * (1.0 + (a - 1.0) * lp['rwkv_ka'])
        y, sf = rwkv_scan(heads(r), heads(decay), heads(kd), heads(v), kk, kk * heads(a),
                          init[:, d], reverse=(d == 1))
        ys.append(y)
        finals.append(sf)
    yf = (ys[0] + ys[1]).astype(F32)
    mu = jnp.mean(yf, axis=-1, keepdims=True)
    var = jnp.mean(jnp.square(yf - mu), axis=-1, keepdims=True)
    yn = ((yf - mu) * lax.rsqrt(var + RWKV_GN_EPS)).reshape(b, s, RWKV_WIDTH)
    yn = (yn * lp['rwkv_ln_g'].astype(F32) + lp['rwkv_ln_b'].astype(F32)).astype(r.dtype)
    bonus = jnp.sum(heads(r) * heads(k) * lp['rwkv_rk'], axis=-1, keepdims=True) * heads(v)
    y = (yn + bonus.reshape(b, s, RWKV_WIDTH)) * g
    return y, jnp.stack(finals, axis=1)

def rope_1d(x, pos):
    half = x.shape[-1] // 2
    inv = ROPE_BASE ** (-jnp.arange(half, dtype=F32) / half)
    ang = pos[:, None] * inv[None, :]
    cos = jnp.cos(ang)[None, :, None, None, :].astype(x.dtype)
    sin = jnp.sin(ang)[None, :, None, None, :].astype(x.dtype)
    x1, x2 = x[..., :half], x[..., half:]
    return jnp.concatenate([x1 * cos - x2 * sin, x1 * sin + x2 * cos], axis=-1)

def rope_2d(x, row, col):
    half = x.shape[-1] // 2
    return jnp.concatenate([rope_1d(x[..., :half], row), rope_1d(x[..., half:], col)], axis=-1)

def grid_positions(n_tokens):
    rows = n_tokens // GRID_W
    row = jnp.repeat(jnp.arange(rows, dtype=F32), GRID_W)
    col = jnp.tile(jnp.arange(GRID_W, dtype=F32), rows)
    return row, col

def diff_attend(q, k, v, lam):
    b, s, h, m, d = q.shape
    blk = ATT_Q_BLOCK if s % ATT_Q_BLOCK == 0 else s
    nb = s // blk
    scale = d ** -0.5
    qb = jnp.moveaxis(q.reshape(b, nb, blk, h, m, d), 1, 0)

    def one(qblk):
        sc = jnp.einsum('bqhmd,bkhmd->bhmqk', qblk, k).astype(F32) * scale
        pr = jax.nn.softmax(sc, axis=-1)
        wgt = (pr[:, :, 0] - lam * pr[:, :, 1]).astype(v.dtype)
        return jnp.einsum('bhqk,bkhd->bqhd', wgt, v)

    o = lax.map(one, qb)
    return jnp.moveaxis(o, 0, 1).reshape(b, s, h, v.shape[-1])

def diff_attn_branch(q, k, v, lp, layer, pos, ctx_k, ctx_v):
    b, s, _ = q.shape
    q = rmsnorm(q.reshape(b, s, ATT_HEADS, 2, ATT_QK_DIM), lp['att_qnorm_g'])
    k = rmsnorm(k.reshape(b, s, ATT_HEADS, 2, ATT_QK_DIM), lp['att_knorm_g'])
    v = v.reshape(b, s, ATT_HEADS, ATT_V_DIM)
    if pos is not None:
        q = rope_2d(q, pos[0], pos[1])
        k = rope_2d(k, pos[0], pos[1])
    if ctx_k is None:
        k_all, v_all = k, v
    else:
        k_all = jnp.concatenate([ctx_k.astype(k.dtype), k], axis=1)
        v_all = jnp.concatenate([ctx_v.astype(v.dtype), v], axis=1)
    lam_init = 0.8 - 0.6 * math.exp(-0.3 * layer)
    lv = lp['att_lambda'].astype(F32)
    lam = jnp.exp(jnp.sum(lv[0] * lv[1])) - jnp.exp(jnp.sum(lv[2] * lv[3])) + lam_init
    o = diff_attend(q, k_all, v_all, lam)
    o = rmsnorm(o, lp['att_onorm_g']) * (1.0 - lam_init)
    return o.reshape(b, s, ATT_WIDTH), k, v

def hier_moe(x, lp):
    b, s, d = x.shape
    t = x.reshape(b * s, d)
    gp = jax.nn.softmax((t @ lp['moe_wg'] + lp['moe_bg']).astype(F32), axis=-1)
    g_val, g_idx = lax.top_k(gp, 1)
    el = (t @ lp['moe_we'] + lp['moe_be']).astype(F32).reshape(-1, N_GROUPS, EXPERTS_PER_GROUP)
    el = jnp.take_along_axis(el, g_idx[:, :, None], axis=1)[:, 0]
    e_val, e_idx = lax.top_k(jax.nn.softmax(el, axis=-1), 2)
    e_val = e_val / jnp.sum(e_val, axis=-1, keepdims=True)
    eid = g_idx * EXPERTS_PER_GROUP + e_idx
    gate = jnp.sum(jax.nn.one_hot(eid, N_EXPERTS, dtype=F32) * (g_val * e_val)[..., None], axis=1).astype(x.dtype)
    hid = jax.nn.silu(jnp.einsum('td,edf->tef', t, lp['moe_w1'])) * jnp.einsum('td,edf->tef', t, lp['moe_w3'])
    y = jnp.einsum('tef,efd->td', hid * gate[:, :, None], lp['moe_w2'])
    return y.reshape(b, s, d)

def trunk_layer(x, cond, lp, layer, pos, ssd_init, rwkv_init, ctx_k, ctx_v):
    mod = (jax.nn.silu(cond) @ lp['ada_w'] + lp['ada_b']).reshape(-1, 1, 6 * D_MODEL)
    sh1, sc1, g1, sh2, sc2, g2 = jnp.split(mod, 6, axis=-1)
    h = rmsnorm(x, lp['norm1_g']) * (1.0 + sc1) + sh1
    (xbc, z, dt_raw, r, k, v, xw, xa, xg, qa, ka, va) = jnp.split(h @ lp['w_in'], IN_SPLITS, axis=-1)
    y_ssd, st_ssd = ssd_branch(xbc, z, dt_raw, lp, ssd_init)
    y_rwkv, st_rwkv = rwkv_branch(r, k, v, xw, xa, xg, lp, rwkv_init)
    y_att, k_att, v_att = diff_attn_branch(qa, ka, va, lp, layer, pos, ctx_k, ctx_v)
    x = x + g1 * (jnp.concatenate([y_ssd, y_rwkv, y_att], axis=-1) @ lp['w_out'])
    h = rmsnorm(x, lp['norm2_g']) * (1.0 + sc2) + sh2
    x = x + g2 * hier_moe(h, lp)
    return x, k_att, v_att, st_ssd, st_rwkv

def setup_inputs(seed: int = 0) -> dict:
    key = jax.random.key(seed)
    keys = iter(jax.random.split(key, 64))
    L = DEPTH

    def nrm(shape, scale):
        return jax.random.normal(next(keys), shape, F32) * scale

    dt0 = jnp.exp(jax.random.uniform(next(keys), (L, 2, SSD_HEADS), F32)
                  * (math.log(0.1) - math.log(0.001)) + math.log(0.001))
    return {
        'x_prompt': nrm((BATCH, SEQ, D_MODEL), 1.0),
        'x_sample': nrm((DEC_BATCH, DEC_SEQ, D_MODEL), 1.0),
        'c': nrm((DEC_BATCH, D_MODEL), 1.0),
        'cache_attn_k': nrm((DEC_BATCH, L, PAST_LEN, ATT_HEADS, 2, ATT_QK_DIM), 1.0),
        'cache_attn_v': nrm((DEC_BATCH, L, PAST_LEN, ATT_HEADS, ATT_V_DIM), 1.0),
        'state_ssd': nrm((DEC_BATCH, L, 2, SSD_HEADS, SSD_HEAD_DIM, SSD_STATE), 0.3),
        'state_rwkv': nrm((DEC_BATCH, L, 2, RWKV_HEADS, RWKV_HEAD_DIM, RWKV_HEAD_DIM), 0.3),
        'c_ctx': nrm((D_MODEL,), 1.0),
        'ada_w': nrm((L, D_MODEL, 6 * D_MODEL), 0.5 * D_MODEL ** -0.5),
        'ada_b': nrm((L, 6 * D_MODEL), 0.02),
        'norm1_g': 1.0 + nrm((L, D_MODEL), 0.02),
        'norm2_g': 1.0 + nrm((L, D_MODEL), 0.02),
        'w_in': nrm((L, D_MODEL, N_IN), D_MODEL ** -0.5),
        'ssd_conv_w': nrm((L, SSD_CONV, SSD_CONV_DIM), SSD_CONV ** -0.5),
        'ssd_conv_b': nrm((L, SSD_CONV_DIM), 0.02),
        'ssd_dt_bias': dt0 + jnp.log(-jnp.expm1(-dt0)),
        'ssd_a_log': jnp.log(jax.random.uniform(next(keys), (L, 2, SSD_HEADS), F32, 1.0, 16.0)),
        'ssd_d': 1.0 + nrm((L, SSD_HEADS), 0.1),
        'ssd_norm_g': 1.0 + nrm((L, SSD_WIDTH), 0.02),
        'rwkv_w0': nrm((L, 2, RWKV_WIDTH), 1.0),
        'rwkv_w2': nrm((L, 2, DECAY_LORA, RWKV_WIDTH), 0.1),
        'rwkv_a0': nrm((L, 2, RWKV_WIDTH), 0.5),
        'rwkv_a2': nrm((L, 2, AAA_LORA, RWKV_WIDTH), AAA_LORA ** -0.5),
        'rwkv_g2': nrm((L, GATE_LORA, RWKV_WIDTH), GATE_LORA ** -0.5),
        'rwkv_kk': 0.85 + nrm((L, RWKV_WIDTH), 0.05),
        'rwkv_ka': 1.0 + nrm((L, RWKV_WIDTH), 0.05),
        'rwkv_rk': nrm((L, RWKV_HEADS, RWKV_HEAD_DIM), 0.1),
        'rwkv_ln_g': 1.0 + nrm((L, RWKV_WIDTH), 0.02),
        'rwkv_ln_b': nrm((L, RWKV_WIDTH), 0.02),
        'att_qnorm_g': 1.0 + nrm((L, ATT_QK_DIM), 0.02),
        'att_knorm_g': 1.0 + nrm((L, ATT_QK_DIM), 0.02),
        'att_lambda': nrm((L, 4, ATT_QK_DIM), 0.1),
        'att_onorm_g': 1.0 + nrm((L, ATT_V_DIM), 0.02),
        'w_out': nrm((L, D_MIX, D_MODEL), D_MIX ** -0.5),
        'moe_wg': nrm((L, D_MODEL, N_GROUPS), D_MODEL ** -0.5),
        'moe_bg': nrm((L, N_GROUPS), 0.01),
        'moe_we': nrm((L, D_MODEL, N_EXPERTS), D_MODEL ** -0.5),
        'moe_be': nrm((L, N_EXPERTS), 0.01),
        'moe_w1': nrm((L, N_EXPERTS, D_MODEL, EXPERT_HIDDEN), D_MODEL ** -0.5),
        'moe_w3': nrm((L, N_EXPERTS, D_MODEL, EXPERT_HIDDEN), D_MODEL ** -0.5),
        'moe_w2': nrm((L, N_EXPERTS, EXPERT_HIDDEN, D_MODEL), EXPERT_HIDDEN ** -0.5),
    }

def reference(x_prompt, x_sample, c, cache_attn_k, cache_attn_v, state_ssd, state_rwkv, c_ctx,
              ada_w, ada_b, norm1_g, norm2_g, w_in, ssd_conv_w, ssd_conv_b, ssd_dt_bias, ssd_a_log,
              ssd_d, ssd_norm_g, rwkv_w0, rwkv_w2, rwkv_a0, rwkv_a2, rwkv_g2, rwkv_kk, rwkv_ka, rwkv_rk,
              rwkv_ln_g, rwkv_ln_b, att_qnorm_g, att_knorm_g, att_lambda, att_onorm_g, w_out,
              moe_wg, moe_bg, moe_we, moe_be, moe_w1, moe_w3, moe_w2):
    yp, ys = x_prompt, x_sample
    bp = x_prompt.shape[0]
    pos = grid_positions(x_sample.shape[1])
    new_k, new_v, new_ssd, new_rwkv = [], [], [], []
    for l in range(DEPTH):
        lp = {
            'ada_w': ada_w[l], 'ada_b': ada_b[l], 'norm1_g': norm1_g[l], 'norm2_g': norm2_g[l],
            'w_in': w_in[l], 'ssd_conv_w': ssd_conv_w[l], 'ssd_conv_b': ssd_conv_b[l],
            'ssd_dt_bias': ssd_dt_bias[l], 'ssd_a_log': ssd_a_log[l], 'ssd_d': ssd_d[l],
            'ssd_norm_g': ssd_norm_g[l], 'rwkv_w0': rwkv_w0[l], 'rwkv_w2': rwkv_w2[l],
            'rwkv_a0': rwkv_a0[l], 'rwkv_a2': rwkv_a2[l], 'rwkv_g2': rwkv_g2[l], 'rwkv_kk': rwkv_kk[l],
            'rwkv_ka': rwkv_ka[l], 'rwkv_rk': rwkv_rk[l], 'rwkv_ln_g': rwkv_ln_g[l], 'rwkv_ln_b': rwkv_ln_b[l],
            'att_qnorm_g': att_qnorm_g[l], 'att_knorm_g': att_knorm_g[l], 'att_lambda': att_lambda[l],
            'att_onorm_g': att_onorm_g[l], 'w_out': w_out[l], 'moe_wg': moe_wg[l], 'moe_bg': moe_bg[l],
            'moe_we': moe_we[l], 'moe_be': moe_be[l], 'moe_w1': moe_w1[l], 'moe_w3': moe_w3[l],
            'moe_w2': moe_w2[l],
        }
        zero_ssd = jnp.zeros((bp, 2, SSD_HEADS, SSD_HEAD_DIM, SSD_STATE), x_prompt.dtype)
        zero_rwkv = jnp.zeros((bp, 2, RWKV_HEADS, RWKV_HEAD_DIM, RWKV_HEAD_DIM), x_prompt.dtype)
        yp, k_l, v_l, s_l, r_l = trunk_layer(yp, c_ctx, lp, l, None, zero_ssd, zero_rwkv, None, None)
        new_k.append(k_l)
        new_v.append(v_l)
        new_ssd.append(s_l)
        new_rwkv.append(r_l)
        ys, _, _, _, _ = trunk_layer(ys, c, lp, l, pos, state_ssd[:, l], state_rwkv[:, l],
                                     cache_attn_k[:, l], cache_attn_v[:, l])
    return (yp, ys, jnp.stack(new_k, axis=1), jnp.stack(new_v, axis=1),
            jnp.stack(new_ssd, axis=1), jnp.stack(new_rwkv, axis=1))


_drawn_inputs = setup_inputs


def setup_inputs(seed=0):
    import zlib

    import numpy as np

    out = dict(_drawn_inputs(seed))
    spreads = {}
    factors = {'state_rwkv': 8.0,
     'norm2_g': 3.767,
     'ssd_d': 2.915,
     'ssd_norm_g': 6.606,
     'rwkv_kk': 5.114,
     'rwkv_ln_g': 8.0,
     'rwkv_ln_b': 7.581,
     'att_qnorm_g': 8.0,
     'att_lambda': 3.937,
     'att_onorm_g': 8.0,
     'moe_bg': 5.263,
     'moe_be': 6.675}
    for name, (base, spread) in spreads.items():
        noise = np.random.default_rng([zlib.crc32(name.encode()), seed]).standard_normal(out[name].shape)
        drawn = base * np.exp(spread * noise) if base else spread * noise
        out[name] = __import__('jax').numpy.asarray(drawn.astype(out[name].dtype))
    for name, factor in factors.items():
        out[name] = (out[name] * factor).astype(out[name].dtype)
    return out
```

```python
import math
from contextlib import ExitStack

import numpy as np
import concourse.bass as bass
from concourse import mybir

F32 = mybir.dt.float32
BF16 = mybir.dt.bfloat16
ACT = mybir.ActivationFunctionType
ALU = mybir.AluOpType
AXX = mybir.AxisListType.X

P = 128
D = 1024
KD = D // P
DEPTH = 2
CTX, LAT = 128, 256
NT = CTX + LAT
TT = NT // P
HEADS = 6
NJ = 3
N_IN = 3212
COL = dict(xbc=0, z=640, dt=1024, r=1036, k=1420, v=1804, xw=2188, xa=2252, xg=2316, qa=2444, ka=2700, va=2956)
EXPERTS, HIDDEN = 16, 256
SLOT = KD * 256
RING = 6
G = math.exp(-0.5)
NEG = -1.0e30
PAD = [2, 134, 262]
CONVW = 388
TOF = [0, 132, 260]
TILE_OF = ((0, 1, 2), (0, 2, 1))

IN_SLOTS = [[("xs0", 0), ("xs1", 128)], [("xs2", 256), ("B", 384)], [("C", 512), ("z0", 640)],
            [("z1", 768), ("z2", 896)], [("q0", 2444), ("q1", 2572)], [("k0", 2700), ("k1", 2828)],
            [("va", 2956)], [("r0", 1036), ("r1", 1164)], [("r2", 1292), ("rk0", 1420)],
            [("rk1", 1548), ("rk2", 1676)], [("xwa", 2188), ("xg", 2316)], [("v0", 1804), ("v1", 1932)],
            [("v2", 2060)]]
N_INS = len(IN_SLOTS)
ADA_FIRST, ADA_LATER = 8, 16
IN_SLOT0 = ADA_FIRST
ADA_SLOT0 = IN_SLOT0 + N_INS
LORA_SLOT = ADA_SLOT0 + ADA_LATER
ADA_GROUPS, ADA_EARLY = (ADA_FIRST + ADA_LATER) // 2, ADA_FIRST // 2
OUT_SLOT = LORA_SLOT + 1
PRE_SLOTS = OUT_SLOT + 4
LAYER_SLOTS = PRE_SLOTS + 3 * EXPERTS
assert PRE_SLOTS % RING == 0 and LAYER_SLOTS % RING == 0 and RING == 6

C_ID, C_ONE, C_B32, C_B64, C_UI, C_LI, C_US, C_LS, C_ROT, C_NF, C_NB = (128 * i for i in range(11))
C_LV = 128 * 11
C_LVT = C_LV + 7 * 128
C_COS = C_LVT + 7 * 128
C_SIN = C_COS + LAT
C_SCAN = C_SIN + LAT
C_IOTA = C_SCAN + NT
C_EPS, C_GN, C_KKB = C_IOTA + 4, C_IOTA + 5, C_IOTA + 6
C_N = C_IOTA + 8

ROWS_A = [("conv_w", 25), ("conv_b", 5), ("ssd_g", 3), ("w0", 6), ("a0", 6), ("kk", 3), ("ka", 3), ("rk", 3),
          ("ln_g", 3), ("ln_b", 3), ("qn", 1), ("kn", 1), ("on", 1)]
ROWS_B = [("ada_b", 48), ("n1", 8), ("n2", 8)]
NA = sum(n for _, n in ROWS_A)
NB = sum(n for _, n in ROWS_B)
PAR = {}
_at = 0
for _n, _c in ROWS_A + ROWS_B:
    PAR[_n] = _at
    _at += _c
BC = dict(dt_bias=0, a_log=12, d=24, rbias=30, lam=50, lami=178)
NBC = 180
SH1, SC1, G1, SH2, SC2, G2 = (8 * i for i in range(6))


def shape_constants():
    c = np.zeros((P, C_N), np.float32)
    i, j = np.arange(P)[:, None], np.arange(P)[None, :]
    put = lambda at, m: c.__setitem__((slice(None), slice(at, at + m.shape[1])), m.astype(np.float32))
    put(C_ID, i == j)
    put(C_ONE, np.ones((P, P)))
    put(C_B32, (i // 32 == j // 32) / 32.0)
    put(C_B64, i // 64 == j // 64)
    put(C_UI, i <= j)
    put(C_LI, i >= j)
    put(C_US, i < j)
    put(C_LS, i > j)
    rot = np.zeros((P, P))
    for o in range(P):
        if o % 16 < 8:
            rot[o + 8, o] = -1.0
        else:
            rot[o - 8, o] = 1.0
    put(C_ROT, rot)
    put(C_NF, np.where(i <= j, 0.0, NEG))
    put(C_NB, np.where(i >= j, 0.0, NEG))
    for n in range(7):
        b = 1 << n
        m = (i // (2 * b) == j // (2 * b)) & (i % (2 * b) >= b) & (j % (2 * b) < b)
        put(C_LV + 128 * n, -1.0 * m)
        put(C_LVT + 128 * n, -1.0 * m.T)
    inv = (np.float32(10000.0) ** (-np.arange(8, dtype=np.float32) / 8)).astype(np.float32)
    t = np.arange(LAT)
    row, col = (t // 64).astype(np.float32), (t % 64).astype(np.float32)
    for p in range(P):
        pos = row if p % 32 < 16 else col
        ang = (pos * inv[p % 8]).astype(np.float32)
        c[p, C_COS:C_COS + LAT] = np.cos(ang)
        c[p, C_SIN:C_SIN + LAT] = np.sin(ang)
    c[:, C_SCAN:C_SCAN + NT] = (np.arange(NT) % P != 0)[None, :]
    c[:, C_IOTA:C_IOTA + 4] = [4, 3, 2, 1]
    c[:, C_EPS] = 1e-6
    c[:, C_GN] = 64e-5
    c[:, C_KKB] = 8 * math.log(2.0)
    return c


def layer_constants():
    li = [0.8 - 0.6 * math.exp(-0.3 * l) for l in range(DEPTH)]
    return np.array([[x, 1.0 - x] for x in li], np.float32)


def job_order():
    def ada(q):
        return ([(f"at{q - 1}", "v")] if q > ADA_EARLY else []) + [(f"ar{q}", "a")]

    jobs = [(f"ar{q}", "a") for q in range(ADA_EARLY)]
    jobs += [("sum1", "a"), ("prmA", "v"), ("prmB", "v"), ("sst", "v"), ("rst", "v"), ("kct", "v"), ("ada", "v"), ("dt", "v")]
    for slot in IN_SLOTS:
        for name, _ in slot:
            jobs += [("va0", "a"), ("va1", "a")] if name == "va" else [(name, "a")]
    jobs += [("cs", "v")] + ada(4)
    jobs += [(f"xtr{t}", "a") for t in range(TT)] + ada(5)
    jobs += [(f"lst{t}", "v") for t in range(TT)]
    for t in range(TT):
        jobs += [(f"csr{t}{i}", "a") for i in range(3)]
        jobs += [(f"cb{t}0", "v"), (f"cb{t}1", "v")] + ada(6 + t) + [(f"ya{t}", "v"), (f"yb{t}", "v")]
    jobs += [("sfin0", "a"), ("sfin1", "a")] + ada(9) + [("sn", "a")]
    jobs += [(f"qn{c}", "a") for c in range(4)]
    jobs += [("kout", "a"), ("rot0", "v"), ("rot1", "v")]
    for t in range(TT):
        for j in range(2):
            jobs += [(f"sc{t}{j}{i}", "a") for i in range(4)]
            jobs += [(f"wt{t}{j}0", "a"), (f"wt{t}{j}1", "a"), (f"pv{t}{j}", "v")]
    jobs += [("on0", "a"), ("on1", "a")] + ada(10)
    jobs += [(f"kn{j}", "v") for j in range(NJ)] + ada(11)
    for d in range(2):
        for j in range(NJ):
            jobs += [(f"lw{d}{j}", "a"), (f"la{d}{j}", "a")]
    jobs += [(f"vt{t}", "a") for t in range(TT)] + [(f"at{ADA_GROUPS - 1}", "v")]
    for s in range(3):
        for d in range(2):
            jobs += [(f"bt{s}{d}", "a"), (f"kt{s}{d}", "a")]
        for g in range(4):
            jobs += [(f"{n}{s}{g}", "v") for n in ("L1", "LT", "L2", "M1", "M2")]
        for lv in range(1, 7):
            jobs += [(f"W{s}{lv}{g}", "v") for g in range(4)]
            for g in range(4):
                jobs += ([(f"X{s}{lv}{g}", "a")] if lv < 6 else []) + [(f"T{s}{lv}{g}", "a")]
        jobs += [(f"rh{s}{g}", "v") for g in range(4)]
        jobs += [(f"u{s}{g}", "v") for g in range(4)]
        jobs += [(f"ry{s}{d}", "v") for d in range(2)]
        jobs += [(f"rs{s}{d}", "v") for d in range(2)]
        if s == 0:
            jobs += [("rfin0", "a"), ("rfin1", "a")]
    jobs += [(f"mu{j}", "v") for j in range(NJ)]
    jobs += [(f"var{j}", "a") for j in range(NJ)]
    jobs += [(f"bon{j}", "v") for j in range(NJ)]
    jobs += [(f"gt{j}", "v") for j in range(NJ)]
    jobs += [(f"out{m}", "v") for m in range(KD)]
    jobs += [("sum2", "a"), ("rt", "v")]
    jobs += [(f"gb{e}", "a") for e in range(EXPERTS)]
    jobs += [(f"ytr{c}", "v") for c in range(KD)]
    return jobs


class Job:
    def __init__(self, n, by, count, before):
        self.n, self.by, self.count, self.before = n, by, count, before


def job_table(order):
    table, counts, listed = {}, {"v": 0, "a": 0}, []
    for n, (name, by) in enumerate(order):
        counts[by] += 1
        table[name] = Job(n, by, counts[by], listed[n - 8] if n >= 8 else None)
        listed.append(table[name])
    assert len(table) == len(order)
    return table, counts


PRE = [(f"x{c}", "v") for c in range(KD)] + [("cond", "a")]
POST = [(f"o{t}{h}", "a") for t in range(TT) for h in range(2)]


def build(nc, A, O, consts_d, lconst_d):
    with ExitStack() as ctx:
        def sb(name, n, dt=F32):
            return ctx.enter_context(nc.sbuf_tensor(name, [P, n], dt))

        cst = sb("cst", C_N)
        ring = sb("ring", RING * SLOT)
        x_t = sb("x_t", KD * NT)[:, :].rearrange("p (c t) -> p c t", t=NT)
        h_t = sb("h_t", KD * NT)
        y_t = sb("y_t", KD * NT)
        ar_a = sb("ar_a", 7680)
        ar_b = sb("ar_b", 9216)
        xg = sb("xg", NT)
        rkv = sb("rkv", 9 * NT)[:, :].rearrange("p (c t) -> p c t", t=NT)
        vtok = sb("vtok", TT * NT)[:, :].rearrange("p (t n) -> p t n", t=TT)
        kct = sb("kct", 256)[:, :].rearrange("p (j t) -> p j t", j=2)
        cv = sb("cv", 256)
        par = sb("par", NA + NB)
        bcr = sb("bcr", NBC)
        mod = sb("mod", 96)[:, :].rearrange("p (m s) -> p m s", s=2)
        gs = sb("gs", 32)[:, :].rearrange("p (m s) -> p m s", s=2)
        scond = sb("scond", 16)[:, :].rearrange("p (c s) -> p c s", s=2)
        wrt = sb("wrt", KD * 20)[:, :].rearrange("p (c n) -> p c n", c=KD)
        wdt = sb("wdt", KD * 12)[:, :].rearrange("p (c n) -> p c n", c=KD)
        bktok = sb("bktok", 4 * NT)[:, :].rearrange("p (d w n) -> p d w n", d=2, w=2)
        srk = sb("srk", 384)[:, :].rearrange("p (d j v) -> p d j v", d=2, j=3)
        sri = sb("sri", 384)[:, :].rearrange("p (d j v) -> p d j v", d=2, j=3)
        stg = sb("stg", 1024)
        sml = sb("sml", 420)
        rs = sb("rs", NT)
        zer = sb("zer", 512, BF16)
        ps = ctx.enter_context(nc.psum_tensor("ps", [P, 8, 512], F32))

        def cc(at, n=128):
            return cst[:, at:at + n]

        ident, ones = cc(C_ID), cc(C_ONE)
        slot = lambda k: ring[:, (k % RING) * SLOT:(k % RING + 1) * SLOT]
        slot8 = lambda k: slot(k).rearrange("p (c n) -> p c n", c=KD)
        slot2 = lambda k: slot(k).rearrange("p (c n) -> p c n", c=2)
        hv = h_t[:, :].rearrange("p (c t) -> p c t", t=NT)
        yv = y_t[:, :].rearrange("p (c t) -> p c t", t=NT)

        def col(name, i=0, lo=0, hi=P):
            return par[lo:hi, PAR[name] + i:PAR[name] + i + 1]

        xin = ar_a[:, 0:3 * D].rearrange("p (t d) -> p t d", t=TT)
        st_b = ar_b[:, 7168:9216]
        ini = st_b[0:64, 0:768].rearrange("p (d i g n) -> p d i g n", d=2, i=3, g=2)
        inr = st_b[0:64, 768:1536].rearrange("p (u n) -> p u n", u=12)
        ck = st_b[:, 1536:1792]
        rows_a, rows_b = st_b[0:NA, 1792:1920], st_b[0:NB, 1920:2048]
        ada_row = lambda q: h_t[0:2, 512 * q:512 * q + 512] if q < ADA_EARLY else ar_a[0:2, 6912:7424]
        diff = ar_a[:, 0:1536].rearrange("p (u t) -> p u t", u=12)
        ecs = ar_a[:, 1536:3072].rearrange("p (u t) -> p u t", u=12)
        cdec = ar_a[:, 3072:4608].rearrange("p (u t) -> p u t", u=12)
        gmat = ar_a[:, 4608:5376].rearrange("p (u t) -> p u t", u=6)
        e_at = ar_a[:, 0:1536].rearrange("p (i k) -> p i k", i=4)
        w_at = ar_a[:, 1536:2304].rearrange("p (i k) -> p i k", i=2)
        wt_at = ar_a[:, 2304:3072].rearrange("p (i k) -> p i k", i=2)
        o_at = ar_a[:, 3072:3840].rearrange("p (j t) -> p j t", j=2)
        sq_at = ar_a[:, 3840:5376].rearrange("p (c t) -> p c t", t=NT)
        rs_at = ar_a[:, 5376:6912].rearrange("p (c t) -> p c t", t=NT)
        three = lambda a, k: a[:, 1152 * k:1152 * (k + 1)].rearrange("p (j t) -> p j t", t=NT)
        sig, aa, dd, dx, en, ep = (three(ar_a, k) for k in range(6))
        kkn, kxa = three(h_t, 0), three(h_t, 1)
        unit = lambda a, k: a[:, 1536 * k:1536 * (k + 1)].rearrange("p (g i t) -> p g i t", g=4, i=3)
        m_lt, m_l2, m_m1, m_m2, m_nw = (unit(ar_a, k) for k in range(5))
        m_x, m_xt = unit(h_t, 0), unit(h_t, 1)
        rhs_b = h_t[:, 0:768].rearrange("p (g i v) -> p g i v", g=4, i=3)
        nu_b = h_t[:, 768:1536].rearrange("p (g i v) -> p g i v", g=4, i=3)
        gates = ar_a[:, 0:EXPERTS * NT].rearrange("p (e t) -> p e t", t=NT)
        loc = h_t[:, 0:1152].rearrange("p (t d i v) -> p t d i v", t=3, d=2, i=3)
        sin = h_t[:, 1152:2304].rearrange("p (t d i v) -> p t d i v", t=3, d=2, i=3)
        xwt = h_t[:, 2304:3072].rearrange("p (g d i v) -> p g d i v", g=2, d=2, i=3)
        xbcp = ar_b[:, 0:1960].rearrange("p (c t) -> p c t", t=392)
        conv = ar_b[:, 1960:3900].rearrange("p (c t) -> p c t", t=CONVW)
        zz = ar_b[:, 3900:5052].rearrange("p (c t) -> p c t", t=NT)
        tok = ar_b[:, 5052:6588].rearrange("p (t n) -> p t n", t=TT)
        qk = ar_b[:, 6588:8124].rearrange("p (c t) -> p c t", t=NT)
        vat = ar_b[:, 8124:8892].rearrange("p (t n) -> p t n", t=TT)
        f_al, f_rho, f_be, f_ka = ([three(ar_b, 4 * d + k) for d in range(2)] for k in range(4))
        hid = ar_b[:, 0:1536].rearrange("p (e m t) -> p e m t", e=2, m=2)
        sh = ar_b[:, 1536:2304].rearrange("p (m t) -> p m t", m=2)
        th = ar_b[:, 2304:3072].rearrange("p (m t) -> p m t", m=2)
        ytok = ar_b[:, 3072:6144].rearrange("p (t d) -> p t d", t=TT)
        xwa = yv[:, 3, :]
        sq8 = y_t[:, :].rearrange("p (c t) -> p c t", t=NT)
        dts = sml[:, 0:36].rearrange("p (t u) -> p t u", t=3)
        dta = sml[:, 36:72].rearrange("p (t u) -> p t u", t=3)
        csc = sml[:, 72:144].rearrange("p (w t u) -> p w t u", w=2, t=3)
        wst = sml[:, 144:180].rearrange("p (t u) -> p t u", t=3)
        dec = sml[:, 180:216].rearrange("p (t u) -> p t u", t=3)
        dec2 = sml[:, 216:234].rearrange("p (t d i) -> p t d i", t=3, d=2)
        avl = sml[:, 234:246]
        dcol = sml[:, 246:249]
        lam = sml[:, 249:260]
        s3 = lambda at, n: sml[:, at:at + 3 * n].rearrange("p (t u) -> p t u", t=3)
        nmx, ssm = sml[:, 260:264], sml[:, 264:268]
        mref = sml[:, 268:277]
        pre = [sml[:, 277 + 9 * d:286 + 9 * d].rearrange("p (j t) -> p j t", j=3) for d in range(2)]
        fin = [sml[:, 295 + 9 * d:304 + 9 * d].rearrange("p (j t) -> p j t", j=3) for d in range(2)]
        lg, rg1, rg2, rg3 = s3(0, 20), s3(60, 4), s3(72, 4), s3(84, 16)
        rg4, rg5, rg6 = s3(132, 4), s3(144, 4), s3(156, 4)
        r1, r2, r3, r4, r5 = (s3(168 + 3 * k, 1) for k in range(5))
        gate = s3(190, 16)

        names = ("bank_full emptied_v emptied_a v_chain a_chain par_in bc_in init_in wsmall_in stats_sq mod_ready "
                 "h_part h_ready x_ready conv_raw conv_in conv_done dt_pre dt_sp dt_one cs_pre cs_exp xw_ready s_ready "
                 "csr_read ec_ready d_ready e_ready cd_ready g_ready ssd_y yssd_sq stage_ssd stage_rwkv stage_kv "
                 "lam_pre lam_exp qk_sq qk_rs qk_ready sc_max sc_exp w_ready o_ready att_done kk_sq kk_max kk_rs "
                 "lora_ready decay_pre decay_exp f_ready nw_ready x1_ready s0_ready rwkv_y bon_in gn_c gn_rs y_ready "
                 "x2_ready h2_part h2_ready rt_pre rt_exp gate_ready moe_y moe_tok out_free xin_in rwkv_st zx s_moe "
                 "t_moe t2_moe hp_moe tok_done sn_rs on_rs passed").split()
        S = {n: ctx.enter_context(nc.semaphore(n)) for n in names}
        cleared = [S[n] for n in names if n not in ("par_in", "bc_in", "init_in", "wsmall_in", "xin_in")]
        ring_full = [ctx.enter_context(nc.semaphore(f"ring_full{i}")) for i in range(RING)]
        ring_free = ctx.enter_context(nc.semaphore("ring_free"))
        engine_done = ctx.enter_context(nc.semaphore("engine_done"))
        sp_passed = ctx.enter_context(nc.semaphore("sp_passed"))
        go_on = ctx.enter_context(nc.semaphore("go_on"))
        gone_on = ctx.enter_context(nc.semaphore("gone_on"))
        cst_in = ctx.enter_context(nc.semaphore("cst_in"))
        cst_rest = ctx.enter_context(nc.semaphore("cst_rest"))
        stored = ctx.enter_context(nc.semaphore("stored"))

        table, totals = job_table(job_order())
        pre_table, _ = job_table(PRE)
        post_table, _ = job_table(POST)
        bank = lambda job: ps[:, job.n % 8, :]

        def meet(eng, i):
            eng.sem_inc(engine_done, 1)
            eng.wait_ge(go_on, i + 1)
            eng.sem_inc(gone_on, 1)

        def counter():
            return {}

        def step(eng, counts, ins, name):
            counts[name] = counts.get(name, 0) + 1
            ins.then_inc(S[name], 1)
            eng.wait_ge(S[name], counts[name])

        block = ctx.enter_context(nc.Block())

        @block.sync
        def _(sp):
            sp.dma_start(xin[:, 0, :], A["x_prompt"].rearrange("b t d -> (b t) d")).then_inc(S["xin_in"], 16)
            sp.dma_start(stg[0:8, 0:P], A["c"].rearrange("b (c p) -> (b c) p", p=P)).then_inc(S["xin_in"], 16)
            sp.dma_start(stg[8:16, 0:P], A["c_ctx"].rearrange("(c p) -> c p", p=P)).then_inc(S["xin_in"], 16)
            sp.dma_start(cst[:, 0:P], consts_d[:, 0:P]).then_inc(cst_in, 16)
            sp.dma_start(xin[:, 1:3, :], A["x_sample"].rearrange("b (t p) d -> p (b t) d", p=P)).then_inc(S["xin_in"], 16)
            sp.dma_start(cst[:, P:C_N], consts_d[:, P:C_N]).then_inc(cst_rest, 16)
            with sp.Fori(0, DEPTH) as l:
                before = l * LAYER_SLOTS
                dl = lambda name: A[name][bass.ds(l, 1)]
                at = 0
                srcs = [dl("ssd_conv_w").rearrange("a j (t p) -> (a j t) p", p=P), dl("ssd_conv_b").rearrange("a (t p) -> (a t) p", p=P),
                        dl("ssd_norm_g").rearrange("a (t p) -> (a t) p", p=P), dl("rwkv_w0").rearrange("a d (t p) -> (a d t) p", p=P),
                        dl("rwkv_a0").rearrange("a d (t p) -> (a d t) p", p=P), dl("rwkv_kk").rearrange("a (t p) -> (a t) p", p=P),
                        dl("rwkv_ka").rearrange("a (t p) -> (a t) p", p=P), dl("rwkv_rk").rearrange("a (t h) p -> (a t) (h p)", h=2),
                        dl("rwkv_ln_g").rearrange("a (t p) -> (a t) p", p=P), dl("rwkv_ln_b").rearrange("a (t p) -> (a t) p", p=P)]
                for (name, n), src in zip(ROWS_A, srcs):
                    sp.dma_start(rows_a[at:at + n, :], src).then_inc(S["par_in"], 16)
                    at += n
                for name, rep in (("att_qnorm_g", 4), ("att_knorm_g", 4), ("att_onorm_g", 2)):
                    for r in range(rep):
                        w = P // rep
                        sp.dma_start(rows_a[at:at + 1, r * w:r * w + w], dl(name)).then_inc(S["par_in"], 16)
                    at += 1
                sp.dma_start(rows_b[0:48, :], dl("ada_b").rearrange("a (t p) -> (a t) p", p=P)).then_inc(S["par_in"], 16)
                sp.dma_start(rows_b[48:56, :], dl("norm1_g").rearrange("a (t p) -> (a t) p", p=P)).then_inc(S["par_in"], 16)
                sp.dma_start(rows_b[56:64, :], dl("norm2_g").rearrange("a (t p) -> (a t) p", p=P)).then_inc(S["par_in"], 16)
                for d in range(2):
                    for gg in range(2):
                        sp.dma_start(ini[:, d, :, gg, :], A["state_ssd"][0, bass.ds(l, 1), d, 3 * gg:3 * gg + 3].rearrange("a i p n -> p (a i) n")).then_inc(S["init_in"], 16)
                sp.dma_start(inr, A["state_rwkv"][0, bass.ds(l, 1)].rearrange("a d h p n -> p (a d h) n")).then_inc(S["init_in"], 16)
                sp.dma_start(ck, A["cache_attn_k"][0, bass.ds(l, 1)].rearrange("a t h m k -> (a t) (h m k)")).then_inc(S["init_in"], 16)
                sp.dma_start(cv[:, :], A["cache_attn_v"][0, bass.ds(l, 1)].rearrange("a t h k -> (a t) (h k)")).then_inc(S["init_in"], 16)
                for name, w, src in (("dt_bias", 12, dl("ssd_dt_bias").rearrange("a d h -> (a d h)")),
                                     ("a_log", 12, dl("ssd_a_log").rearrange("a d h -> (a d h)")),
                                     ("d", 6, dl("ssd_d").rearrange("a h -> (a h)")),
                                     ("rbias", 4, dl("moe_bg").rearrange("a h -> (a h)")),
                                     ("be", 16, dl("moe_be").rearrange("a h -> (a h)")),
                                     ("lam", 128, dl("att_lambda").rearrange("a d h -> (a d h)")),
                                     ("lami", 2, lconst_d[bass.ds(l, 1)].rearrange("a h -> (a h)"))):
                    c0 = BC["rbias"] + 4 if name == "be" else BC[name]
                    sp.dma_start(bcr[:, c0:c0 + w], src.partition_broadcast(P)).then_inc(S["bc_in"], 16)
                with nc.allow_non_contiguous_dma(reason="narrow weight columns"):
                    sp.dma_start(wdt, dl("w_in").rearrange("a (c p) n -> p (a c) n", p=P)[:, :, COL["dt"]:COL["dt"] + 12]).then_inc(S["wsmall_in"], 16)
                    sp.dma_start(wrt[:, :, 0:4], dl("moe_wg").rearrange("a (c p) n -> p (a c) n", p=P)).then_inc(S["wsmall_in"], 16)
                    sp.dma_start(wrt[:, :, 4:20], dl("moe_we").rearrange("a (c p) n -> p (a c) n", p=P)).then_inc(S["wsmall_in"], 16)
                for k in range(PRE_SLOTS):
                    sp.wait_ge(ring_free, before + (k + 1))
                    sp.sem_inc(sp_passed, 1)
                    full = ring_full[k % RING]
                    if k < ADA_FIRST or ADA_SLOT0 <= k < LORA_SLOT:
                        n = k if k < ADA_FIRST else k - ADA_SLOT0 + ADA_FIRST
                        sp.dma_start(slot8(k), dl("ada_w").rearrange("a (c p) n -> p (a c) n", p=P)[:, :, 256 * n:256 * n + 256]).then_inc(full, 16)
                    elif k < ADA_SLOT0:
                        parts = IN_SLOTS[k - IN_SLOT0]
                        c0, w = parts[0][1], 256 if len(parts) == 2 or parts[0][0] == "va" else 128
                        sp.dma_start(slot8(k)[:, :, 0:w], dl("w_in").rearrange("a (c p) n -> p (a c) n", p=P)[:, :, c0:c0 + w]).then_inc(full, 16)
                    elif k == LORA_SLOT:
                        for name, lo, hi in (("rwkv_w2", 0, 64), ("rwkv_a2", 64, 128)):
                            sp.dma_start(slot(k)[lo:hi, 0:768].rearrange("p (d n) -> p d n", d=2),
                                         dl(name).rearrange("a d p n -> p (a d) n")).then_inc(full, 16)
                        sp.dma_start(slot(k)[:, 768:1152], dl("rwkv_g2").rearrange("a p n -> p (a n)")).then_inc(full, 16)
                    else:
                        m = k - OUT_SLOT
                        sp.dma_start(slot2(k), dl("w_out").rearrange("a (c p) n -> p (a c) n", p=P)[:, 2 * m:2 * m + 2, :]).then_inc(full, 16)
                with sp.Fori(0, EXPERTS // 2) as j:
                    for e in range(2):
                        for i, name in enumerate(("moe_w1", "moe_w3", "moe_w2")):
                            k = PRE_SLOTS + 3 * e + i
                            src = A[name].rearrange("l e a b -> (l e) a b")[bass.ds(l * EXPERTS + j * 2 + e, 1)]
                            sp.wait_ge(ring_free, before + j * 6 + (k + 1))
                            sp.dma_start(slot8(k) if i < 2 else slot2(k), src.rearrange("a (c p) n -> p (a c) n", p=P)).then_inc(ring_full[k % RING], 16)

        EXTRA = 32

        def ring_value(k):
            v = 16 * (k // RING + 1)
            if k % RING == LORA_SLOT % RING and k >= LORA_SLOT:
                v += EXTRA
            return v

        @block.gpsimd
        def _(g):
            def clear(i):
                g.wait_ge(engine_done, i * 3 + 3)
                g.sem_inc(gone_on, 1)
                for s in cleared:
                    g.sem_clear(s)
                g.sem_inc(go_on, 1)

            g.memset(zer[:, :], 0.0).then_inc(S["zx"], 1)
            g.wait_ge(S["zx"], 1)
            clear(0)
            with g.Fori(0, DEPTH) as l:
                g.wait_ge(S["stage_ssd"], 2)
                so = stg[0:64, 0:768].rearrange("p (d i g n) -> p d i g n", d=2, i=3, g=2)
                for d in range(2):
                    for gg in range(2):
                        g.dma_start(O[4][0, bass.ds(l, 1), d, 3 * gg:3 * gg + 3].rearrange("a i p n -> p (a i) n"), so[:, d, :, gg, :]).then_inc(stored, 16)
                g.wait_ge(S["stage_kv"], 1)
                g.dma_start(O[2][0, bass.ds(l, 1)].rearrange("a t h m k -> (a t) (h m k)"), stg[:, 768:1024]).then_inc(stored, 16)
                g.dma_start(O[3][0, bass.ds(l, 1)].rearrange("a t h k -> (a t) (h k)"), vat[:, 0, :]).then_inc(stored, 16)
                g.wait_ge(stored, l * 128 + 96)
                g.sem_inc(S["out_free"], 1)
                g.wait_ge(S["stage_rwkv"], 2)
                ro = stg[0:64, 0:768].rearrange("p (u n) -> p u n", u=12)
                for d in range(2):
                    g.dma_start(O[5][0, bass.ds(l, 1), d].rearrange("a i p n -> p (a i) n"), ro[:, 6 * d:6 * d + 6, :]).then_inc(stored, 16)
                g.wait_ge(stored, l * 128 + 128)
                clear(l + 1)
            for t in range(TT):
                g.wait_ge(S["tok_done"], 2 * t + 2)
                dst = O[0][0] if t == 0 else O[1][0, 128 * (t - 1):128 * t]
                g.dma_start(dst, xin[:, t, :]).then_inc(stored, 16)
            g.wait_ge(stored, DEPTH * 128 + 48)

        @block.tensor
        def _(pe):
            tb = [pre_table]

            def claim(name):
                job = tb[0][name]
                if job.before is not None:
                    pe.wait_ge(S["emptied_" + job.before.by], job.before.count)
                return bank(job)

            def mm(out, lhsT, rhs, start=True, stop=True):
                return pe.matmul(out, lhsT, rhs, start=start, stop=stop)

            def full(ins):
                ins.then_inc(S["bank_full"], 1)

            def tr(out, in_, n=P):
                return pe.transpose(out, in_, ident[0:n, 0:n])

            pe.sem_inc(ring_free, RING)
            pe.wait_ge(cst_in, 16)
            pe.wait_ge(S["xin_in"], 64)
            for c in range(KD):
                b = claim(f"x{c}")
                for t in range(TT):
                    i = tr(b[:, P * t:P * t + P], xin[:, t, P * c:P * c + P])
                full(i)
            b = claim("cond")
            full(tr(b[:, 0:16], stg[0:16, 0:P], 16))
            pe.wait_ge(cst_rest, 16)
            meet(pe, 0)
            tb[0] = table

            with pe.Fori(0, DEPTH) as l:
                lring = [l * (16 * (LAYER_SLOTS // RING) + (EXTRA if i == LORA_SLOT % RING else 0)) for i in range(RING)]

                def arrived(k):
                    pe.wait_ge(ring_full[k % RING], lring[k % RING] + ring_value(k))

                def used(ins):
                    ins.then_inc(ring_free, 1)

                def ada_rows(q):
                    b = claim(f"ar{q}")
                    for half in range(2):
                        k = 2 * q + half + (0 if q < ADA_EARLY else N_INS)
                        arrived(k)
                        for c in range(KD):
                            i = mm(b[0:2, 256 * half:256 * half + 256], scond[:, c, :], slot8(k)[:, c, :], c == 0, c == KD - 1)
                        if half == 0:
                            used(i)
                    full(i)
                    pe.wait_ge(S["bank_full"], table[f"ar{q}"].n + 1)
                    pe.sem_inc(ring_free, 1)

                def ada_turn(q, b, at):
                    pe.wait_ge(S["emptied_a"], table[f"ar{q}"].count)
                    for m in range(4):
                        i = tr(b[:, at + 2 * m:at + 2 * m + 2], ada_row(q)[:, P * m:P * m + P], 2)
                    return i

                def ada(q):
                    if q > ADA_EARLY:
                        full(ada_turn(q - 1, claim(f"at{q - 1}"), 0))
                    if q < ADA_GROUPS:
                        ada_rows(q)

                for q in range(ADA_EARLY):
                    ada_rows(q)
                b = claim("sum1")
                for c in range(KD):
                    pe.wait_ge(S["stats_sq"], c + 1)
                    i = mm(b[:, 0:NT], ones, sq8[:, c, :], c == 0, c == KD - 1)
                full(i)
                pe.wait_ge(S["par_in"], l * (16 * 23) + 16 * 23)
                pe.sem_inc(S["passed"], 1)
                b = claim("prmA")
                full(tr(b[:, 0:NA], rows_a, NA))
                b = claim("prmB")
                full(tr(b[:, 0:NB], rows_b, NB))
                pe.wait_ge(S["init_in"], l * (16 * 7) + 16 * 7)
                pe.sem_inc(S["passed"], 1)
                b = claim("sst")
                for d in range(2):
                    for i in range(3):
                        src = ini[:, d, i].rearrange("p g n -> p (g n)")
                        o = tr(b[:, 64 * (3 * d + i):64 * (3 * d + i) + 64], src, 64)
                full(o)
                b = claim("rst")
                for d in range(2):
                    for j in range(3):
                        o = tr(b[:, 64 * (3 * d + j):64 * (3 * d + j) + 64], inr[:, 6 * d + 2 * j:6 * d + 2 * j + 2, :].rearrange("p u n -> p (u n)"), 64)
                full(o)
                b = claim("kct")
                for j in range(2):
                    o = tr(b[:, P * j:P * j + P], ck[:, P * j:P * j + P])
                full(o)
                b = claim("ada")
                for q in range(ADA_EARLY):
                    i = ada_turn(q, b, 8 * q)
                full(i)
                pe.wait_ge(S["h_ready"], 16)
                pe.wait_ge(S["wsmall_in"], l * 48 + 48)
                pe.sem_inc(S["passed"], 1)
                b = claim("dt")
                for t in range(TT):
                    for c in range(KD):
                        i = mm(b[:, 12 * t:12 * t + 12], hv[:, c, P * t:P * t + P], wdt[:, c, :], c == 0, c == KD - 1)
                full(i)
                for n, parts in enumerate(IN_SLOTS):
                    k = IN_SLOT0 + n
                    arrived(k)
                    w = slot8(k)
                    if parts[0][0] == "va":
                        for half, ts in ((0, (0, 1)), (1, (2,))):
                            b = claim(f"va{half}")
                            for o, t in enumerate(ts):
                                for c in range(KD):
                                    i = mm(b[:, 256 * o:256 * o + 256], hv[:, c, P * t:P * t + P], w[:, c, :], c == 0, c == KD - 1)
                            if half == 0:
                                full(i)
                    else:
                        for o, (name, _) in enumerate(parts):
                            b = claim(name)
                            for c in range(KD):
                                i = mm(b[:, 0:NT], w[:, c, P * o:P * o + P], hv[:, c, :], c == 0, c == KD - 1)
                            if o < len(parts) - 1:
                                full(i)
                    full(i)
                    pe.wait_ge(S["bank_full"], table[parts[-1][0] if parts[0][0] != "va" else "va1"].n + 1)
                    pe.sem_inc(ring_free, 1)

                pe.wait_ge(S["dt_one"], 1)
                b = claim("cs")
                for d, tri in ((0, C_UI), (1, C_LI)):
                    for t in range(TT):
                        mm(b[:, 12 * t + 6 * d:12 * t + 6 * d + 6], cc(tri), dta[:, t, 6 * d:6 * d + 6])
                full(mm(b[:, 36:72], ones, sml[:, 36:72]))
                ada(4)
                for t in range(TT):
                    if t == 0:
                        pe.wait_ge(S["conv_done"], 5)
                    b = claim(f"xtr{t}")
                    for c in range(4):
                        i = tr(b[:, P * c:P * c + P], conv[:, c, TOF[t]:TOF[t] + P])
                    full(i)
                ada(5)
                for t in range(TT):
                    pe.wait_ge(S["xw_ready"], 4 * t + 4)
                    b = claim(f"lst{t}")
                    for gg in range(2):
                        i = mm(b[64 * gg:64 * gg + 64, 0:384], tok[:, t, 384 + 64 * gg:448 + 64 * gg], xwt[:, gg].rearrange("p d i v -> p (d i v)"))
                    full(i)
                for t in range(TT):
                    for q in range(3):
                        b = claim(f"csr{t}{q}")
                        for o in range(4):
                            u = 4 * q + o
                            i = mm(b[:, P * o:P * o + P], dta[:, t, u:u + 1].to_broadcast([P, P]), cc(C_UI if u < 6 else C_LI))
                        full(i)
                    for gg in range(2):
                        b = claim(f"cb{t}{gg}")
                        r = slice(64 * gg, 64 * gg + 64)
                        full(mm(b[:, 0:P], conv[r, 3, TOF[t]:TOF[t] + P], conv[r, 4, TOF[t]:TOF[t] + P]))
                    ada(6 + t)
                    pe.wait_ge(S["g_ready"], t + 1)
                    if t == 0:
                        pe.wait_ge(S["s_ready"], 1)
                    for gg in range(2):
                        b = claim(f"y{'ab'[gg]}{t}")
                        r = slice(64 * gg, 64 * gg + 64)
                        for hh in range(3):
                            h = 3 * gg + hh
                            o = b[64 * (h % 2):64 * (h % 2) + 64, P * (h // 2):P * (h // 2) + P]
                            mm(o, tok[:, t, 64 * h:64 * h + 64], gmat[:, h, :], True, False)
                            for d in range(2):
                                i = mm(o, sin[r, t, d, hh, :], cdec[r, 6 * d + h, :], False, d == 1)
                        full(i)
                for d in range(2):
                    b = claim(f"sfin{d}")
                    for i in range(3):
                        o = tr(b[0:64, P * i:P * i + P], loc[:, 0, d, i, :])
                    full(o)
                ada(9)
                b = claim("sn")
                for j in range(NJ):
                    pe.wait_ge(S["yssd_sq"], j + 1)
                    i = mm(b[:, 0:NT], ones, rs_at[:, j, :], j == 0, j == NJ - 1)
                full(i)

                pe.wait_ge(S["qk_sq"], 1)
                for c in range(4):
                    b = claim(f"qn{c}")
                    full(mm(b[:, 0:NT], cc(C_B32), sq_at[:, c, :]))
                pe.wait_ge(S["qk_rs"], 4)
                b = claim("kout")
                for j in range(2):
                    i = tr(b[:, P * j:P * j + P], qk[:, 2 + j, 0:P])
                full(i)
                for q in range(2):
                    b = claim(f"rot{q}")
                    for o in range(2):
                        i = mm(b[:, 256 * o:256 * o + 256], cc(C_ROT), qk[:, 2 * q + o, P:NT])
                    full(i)
                pe.wait_ge(S["qk_ready"], 2)
                for t in range(TT):
                    for j in range(2):
                        for i4 in range(4):
                            b = claim(f"sc{t}{j}{i4}")
                            r = slice(32 * i4, 32 * i4 + 32)
                            q = qk[r, j, P * t:P * t + P]
                            if t == 0:
                                i = pe.matmul(b[:, 0:P], q, qk[r, 2 + j, 0:P], start=True, stop=True, tile_position=(32 * i4, 0))
                            else:
                                pe.matmul(b[:, 0:P], q, kct[r, j, :], start=True, stop=True, tile_position=(32 * i4, 0))
                                i = pe.matmul(b[:, P:NT], q, qk[r, 2 + j, P:NT], start=True, stop=True, tile_position=(32 * i4, 0))
                            full(i)
                        nb = 1 if t == 0 else 3
                        for hh in range(2):
                            pe.wait_ge(S["w_ready"], 4 * t + 2 * j + hh + 1)
                            b = claim(f"wt{t}{j}{hh}")
                            for kb in range(nb):
                                i = tr(b[:, P * kb:P * kb + P], w_at[:, hh, P * kb:P * kb + P])
                            full(i)
                        b = claim(f"pv{t}{j}")
                        for hh in range(2):
                            pe.wait_ge(S["emptied_a"], table[f"wt{t}{j}{hh}"].count)
                            h = 2 * j + hh
                            for kb in range(nb):
                                if t == 0:
                                    v = vat[:, 0, 64 * h:64 * h + 64]
                                else:
                                    v = cv[:, 64 * h:64 * h + 64] if kb == 0 else vat[:, kb, 64 * h:64 * h + 64]
                                i = mm(b[64 * hh:64 * hh + 64, 0:P], v, wt_at[:, hh, P * kb:P * kb + P], kb == 0, kb == nb - 1)
                        full(i)
                for j in range(2):
                    pe.wait_ge(S["o_ready"], j + 1)
                    b = claim(f"on{j}")
                    full(mm(b[:, 0:NT], cc(C_B64), sq_at[:, j, :]))

                ada(10)
                pe.wait_ge(S["kk_sq"], 1)
                for j in range(NJ):
                    b = claim(f"kn{j}")
                    full(mm(b[:, 0:NT], cc(C_B64), en[:, j, :]))
                ada(11)
                arrived(LORA_SLOT)
                for d in range(2):
                    for j in range(NJ):
                        lo = slot(LORA_SLOT)[:, 0:768].rearrange("p (d n) -> p d n", d=2)
                        b = claim(f"lw{d}{j}")
                        full(mm(b[:, 0:NT], lo[0:64, d, P * j:P * j + P], xwa[0:64, :]))
                        b = claim(f"la{d}{j}")
                        full(mm(b[:, 0:NT], lo[64:128, d, P * j:P * j + P], xwa[64:128, :]))
                for t in range(TT):
                    b = claim(f"vt{t}")
                    for j in range(NJ):
                        i = tr(b[:, P * j:P * j + P], rkv[:, 6 + j, P * t:P * t + P])
                    full(i)
                ada(12)
                for s in range(3):
                    for d in range(2):
                        t = TILE_OF[d][s]
                        c = slice(P * t, P * t + P)
                        if s == 0:
                            pe.wait_ge(S["f_ready"], 2)
                        for w, f in ((0, f_be), (1, f_ka)):
                            b = claim(f"{'bk'[w]}t{s}{d}")
                            for j in range(NJ):
                                i = tr(b[:, P * j:P * j + P], f[d][:, j, c])
                            full(i)
                    for g4 in range(4):
                        d, par_ = g4 // 2, g4 % 2
                        t = TILE_OF[d][s]
                        c = slice(P * t, P * t + P)
                        r = slice(64 * par_, 64 * par_ + 64)
                        for name, lh, rh in (("L1", f_al, f_be), ("LT", f_be, f_al), ("L2", f_ka, f_al), ("M1", f_be, f_rho), ("M2", f_ka, f_rho)):
                            b = claim(f"{name}{s}{g4}")
                            for j in range(NJ):
                                i = mm(b[:, P * j:P * j + P], lh[d][r, j, c], rh[d][r, j, c])
                            full(i)
                    for lv in range(1, 7):
                        for g4 in range(4):
                            if lv == 1:
                                pe.wait_ge(S["x1_ready"], 2 * (4 * s + g4) + 2)
                            else:
                                pe.wait_ge(S["emptied_a"], table[f"T{s}{lv - 1}{g4}"].count)
                            b = claim(f"W{s}{lv}{g4}")
                            for j in range(NJ):
                                i = mm(b[:, P * j:P * j + P], m_lt[:, g4, j, :], m_x[:, g4, j, :])
                            full(i)
                        for g4 in range(4):
                            pe.wait_ge(S["nw_ready"], 24 * s + 4 * (lv - 1) + g4 + 1)
                            if lv < 6:
                                b = claim(f"X{s}{lv}{g4}")
                                for j in range(NJ):
                                    i = mm(b[:, P * j:P * j + P], m_xt[:, g4, j, :], m_nw[:, g4, j, :])
                                full(i)
                            b = claim(f"T{s}{lv}{g4}")
                            for j in range(NJ):
                                i = mm(b[:, P * j:P * j + P], m_nw[:, g4, j, :], m_xt[:, g4, j, :])
                            full(i)
                    pe.wait_ge(S["s0_ready"], 2 * s + 2)
                    if s == 0:
                        pe.wait_ge(S["emptied_a"], table["vt2"].count)
                    for g4 in range(4):
                        d, par_ = g4 // 2, g4 % 2
                        t = TILE_OF[d][s]
                        c = slice(P * t, P * t + P)
                        r = slice(64 * par_, 64 * par_ + 64)
                        b = claim(f"rh{s}{g4}")
                        for j in range(NJ):
                            h = 2 * j + par_
                            mm(b[:, 64 * j:64 * j + 64], f_al[d][r, j, c], srk[r, d, j, :], True, False)
                            i = mm(b[:, 64 * j:64 * j + 64], m_l2[:, g4, j, :], vtok[:, t, 64 * h:64 * h + 64], False, True)
                        full(i)
                    pe.wait_ge(S["emptied_a"], table[f"T{s}63"].count)
                    for g4 in range(4):
                        pe.wait_ge(S["emptied_v"], table[f"rh{s}{g4}"].count)
                        b = claim(f"u{s}{g4}")
                        for j in range(NJ):
                            i = mm(b[:, 64 * j:64 * j + 64], m_xt[:, g4, j, :], rhs_b[:, g4, j, :])
                        full(i)
                    for d in range(2):
                        pe.wait_ge(S["emptied_v"], table[f"u{s}{2 * d + 1}"].count)
                        t = TILE_OF[d][s]
                        c = slice(P * t, P * t + P)
                        b = claim(f"ry{s}{d}")
                        for par_ in range(2):
                            r = slice(64 * par_, 64 * par_ + 64)
                            for j in range(NJ):
                                h = 2 * j + par_
                                o = b[r, P * j:P * j + P]
                                mm(o, srk[r, d, j, :], f_rho[d][r, j, c], True, False)
                                mm(o, vtok[:, t, 64 * h:64 * h + 64], m_m2[:, 2 * d + par_, j, :], False, False)
                                i = mm(o, nu_b[:, 2 * d + par_, j, :], m_m1[:, 2 * d + par_, j, :], False, True)
                        full(i)
                    for d in range(2):
                        t = TILE_OF[d][s]
                        pe.wait_ge(S["emptied_a"], table[f"kt{s}{d}"].count)
                        b = claim(f"rs{s}{d}")
                        for par_ in range(2):
                            for j in range(NJ):
                                h = 2 * j + par_
                                o = b[64 * par_:64 * par_ + 64, 64 * j:64 * j + 64]
                                mm(o, bktok[:, d, 1, 64 * h:64 * h + 64], vtok[:, t, 64 * h:64 * h + 64], True, False)
                                i = mm(o, bktok[:, d, 0, 64 * h:64 * h + 64], nu_b[:, 2 * d + par_, j, :], False, True)
                        full(i)
                    if s == 0:
                        for d in range(2):
                            pe.wait_ge(S["rwkv_st"], d + 1)
                            b = claim(f"rfin{d}")
                            for j in range(NJ):
                                i = tr(b[0:64, P * j:P * j + P], sri[:, d, j, :])
                            full(i)
                pe.wait_ge(S["rwkv_y"], 1)
                for j in range(NJ):
                    b = claim(f"mu{j}")
                    full(mm(b[:, 0:NT], cc(C_B64), yv[:, 3 + j, :]))
                for j in range(NJ):
                    pe.wait_ge(S["gn_c"], j + 1)
                    b = claim(f"var{j}")
                    full(mm(b[:, 0:NT], cc(C_B64), en[:, j, :]))
                for j in range(NJ):
                    pe.wait_ge(S["bon_in"], j + 1)
                    b = claim(f"bon{j}")
                    full(mm(b[:, 0:NT], cc(C_B64), ep[:, j, :]))
                for j in range(NJ):
                    b = claim(f"gt{j}")
                    full(mm(b[:, 0:NT], slot(LORA_SLOT)[:, 768 + P * j:768 + P * j + P], xg[:, :]))
                pe.wait_ge(S["bank_full"], table["gt2"].n + 1)
                pe.sem_inc(ring_free, 1)

                for q in range(4):
                    arrived(OUT_SLOT + q)
                pe.wait_ge(S["y_ready"], 3)
                pe.wait_ge(S["att_done"], 2)
                for m in range(KD):
                    b = claim(f"out{m}")
                    for c in range(KD):
                        i = mm(b[:, 0:NT], slot2(OUT_SLOT + c // 2)[:, c % 2, P * m:P * m + P], yv[:, c, :], c == 0, c == KD - 1)
                    full(i)
                pe.wait_ge(S["bank_full"], table[f"out{KD - 1}"].n + 1)
                pe.sem_inc(ring_free, 4)
                b = claim("sum2")
                for c in range(KD):
                    pe.wait_ge(S["x2_ready"], c + 1)
                    i = mm(b[:, 0:NT], ones, sq8[:, c, :], c == 0, c == KD - 1)
                full(i)
                pe.wait_ge(S["h2_ready"], 16)
                b = claim("rt")
                for t in range(TT):
                    for c in range(KD):
                        i = mm(b[:, 20 * t:20 * t + 20], hv[:, c, P * t:P * t + P], wrt[:, c, :], c == 0, c == KD - 1)
                full(i)
                pe.wait_ge(S["gate_ready"], 1)
                for e in range(EXPERTS):
                    b = claim(f"gb{e}")
                    for t in range(TT):
                        i = mm(b[:, P * t:P * t + P], gate[:, t, e:e + 1].to_broadcast([P, P]), ident)
                    full(i)
                pe.wait_ge(S["emptied_a"], table[f"gb{EXPERTS - 1}"].count)
                for q in range(6):
                    pe.matmul(ps[:, q, :], zer[:, 0:P], zer[:, :], start=True, stop=False, skip_group_check=True)
                with pe.Fori(0, EXPERTS // 2) as jj:
                    for e in range(2):
                        k = PRE_SLOTS + 3 * e
                        for i3 in range(2):
                            full_at = lring[(k + i3) % RING] + ring_value(k + i3)
                            pe.wait_ge(ring_full[(k + i3) % RING], jj * 16 + full_at)
                            if i3 == 0:
                                w1 = slot8(k).rearrange("p c n -> p c n")
                            else:
                                w3 = slot8(k + 1)
                        for m in range(2):
                            n = 2 * e + m
                            pe.wait_ge(S["s_moe"], jj * 4 + (n + 1))
                            for c in range(KD):
                                i = mm(ps[:, 6, 0:NT], w1[:, c, P * m:P * m + P], hv[:, c, :], c == 0, c == KD - 1)
                            i.then_inc(S["hp_moe"], 1)
                            pe.wait_ge(S["t_moe"], jj * 4 + (n + 1))
                            for c in range(KD):
                                i = mm(ps[:, 7, 0:NT], w3[:, c, P * m:P * m + P], hv[:, c, :], c == 0, c == KD - 1)
                            i.then_inc(S["hp_moe"], 1)
                        pe.wait_ge(S["hp_moe"], jj * 8 + (4 * e + 4))
                        pe.sem_inc(ring_free, 2)
                        full_at = lring[(k + 2) % RING] + ring_value(k + 2)
                        pe.wait_ge(ring_full[(k + 2) % RING], jj * 16 + full_at)
                        w2 = slot2(k + 2)
                        for m in range(2):
                            pe.wait_ge(S["t2_moe"], jj * 4 + (2 * e + m + 1))
                            for t in range(TT):
                                for hf in range(2):
                                    i = pe.matmul(ps[:, 2 * t + hf, :], hid[:, e, m, P * t:P * t + P], w2[:, m, 512 * hf:512 * hf + 512],
                                                  start=False, stop=False, skip_group_check=True)
                        i.then_inc(ring_free, 1)
                for q in range(6):
                    i = pe.matmul(ps[:, q, :], zer[:, 0:P], zer[:, :], start=False, stop=True, skip_group_check=True)
                i.then_inc(S["moe_y"], 1)
                pe.wait_ge(S["moe_tok"], 6)
                for c in range(KD):
                    b = claim(f"ytr{c}")
                    for t in range(TT):
                        i = tr(b[:, P * t:P * t + P], ytok[:, t, P * c:P * c + P])
                    full(i)
                meet(pe, l + 1)
            tb[0] = post_table
            for t in range(TT):
                for hf in range(2):
                    b = claim(f"o{t}{hf}")
                    for c in range(4):
                        i = tr(b[:, P * c:P * c + P], x_t[:, 4 * hf + c, P * t:P * t + P])
                    full(i)

        @block.vector
        def _(v):
            cnt = counter()
            tb = [pre_table]

            def do(ins, name="v_chain"):
                step(v, cnt, ins, name)

            def filled(name):
                v.wait_ge(S["bank_full"], tb[0][name].n + 1)
                return bank(tb[0][name])

            def tell(name):
                cnt[name] = cnt.get(name, 0) + 1
                v.sem_inc(S[name], 1)

            TTT = v.tensor_tensor
            STT = v.scalar_tensor_tensor
            TS = v.tensor_scalar

            def bc3(ap, n, inner):
                return ap.unsqueeze(2).to_broadcast([P, n, inner])

            for c in range(KD):
                do(v.tensor_copy(x_t[:, c, :], filled(f"x{c}")[:, 0:NT]), "emptied_v")
            meet(v, 0)
            cnt.clear()
            tb[0] = table
            seg = ((1, 0, P), (0, P, NT))

            with v.Fori(0, DEPTH) as l:
                for c in range(KD):
                    do(TTT(sq8[:, c, :], x_t[:, c, :], x_t[:, c, :], ALU.mult), "stats_sq")
                b = filled("prmA")
                do(v.tensor_copy(par[:, 0:NA], b[:, 0:NA]), "emptied_v")
                b = filled("prmB")
                do(v.tensor_copy(par[:, NA:NA + NB], b[:, 0:NB]), "emptied_v")
                b = filled("sst")
                do(v.tensor_copy(bktok[:, 0, 0, :], b[:, 0:384]), "emptied_v")
                b = filled("rst")
                do(v.tensor_copy(sri[:, :, :, :].rearrange("p d j v -> p (d j v)"), b[:, 0:384]), "emptied_v")
                b = filled("kct")
                do(v.tensor_copy(kct[:, :, :].rearrange("p j t -> p (j t)"), b[:, 0:256]), "emptied_v")
                v.wait_ge(S["bc_in"], l * (16 * 7) + 16 * 7)
                lv_ = bcr[:, BC["lam"]:BC["lam"] + 128].rearrange("p (a b k) -> p a b k", a=2, b=2)
                tmp = rs[:, 0:64].rearrange("p (a k) -> p a k", a=2)
                do(TTT(tmp, lv_[:, :, 0, :], lv_[:, :, 1, :], ALU.mult))
                do(v.tensor_reduce(lam[:, 0:2], tmp, AXX, ALU.add), "lam_pre")
                def ada_add(name, m0, n):
                    b = filled(name)
                    ab = par[:, PAR["ada_b"] + m0:PAR["ada_b"] + m0 + n]
                    do(TTT(mod[:, m0:m0 + n, :], b[:, 0:2 * n].rearrange("p (m s) -> p m s", s=2), bc3(ab, n, 2), ALU.add), "emptied_v")

                def norm_gain(g0, sc, pn):
                    gn = bc3(par[:, PAR[pn]:PAR[pn] + 8], 8, 2)
                    do(STT(out=gs[:, g0:g0 + 8, :], in0=mod[:, sc:sc + 8, :], scalar=1.0, in1=gn, op0=ALU.add, op1=ALU.mult), "mod_ready")

                def ada_later(q):
                    ada_add(f"at{q}", 4 * q, 4)

                ada_add("ada", 0, 4 * ADA_EARLY)
                norm_gain(0, SC1, "n1")
                v.wait_ge(S["h_part"], 1)
                for c in range(KD):
                    do(TTT(hv[:, c, :], x_t[:, c, :], rs[:, :], ALU.mult), "x_ready")
                v.wait_ge(S["lam_exp"], 2)
                do(TTT(lam[:, 4:5], lam[:, 2:3], lam[:, 3:4], ALU.subtract))
                do(TTT(lam[:, 4:5], lam[:, 4:5], bcr[:, BC["lami"]:BC["lami"] + 1], ALU.add))
                do(TTT(lam[:, 5:6], col("on"), bcr[:, BC["lami"] + 1:BC["lami"] + 2], ALU.mult))
                dd_ = bcr[:, BC["d"]:BC["d"] + 6].rearrange("p (j k) -> p j k", k=2)
                do(v.tensor_copy(dcol[0:64, :], dd_[0:64, :, 0]))
                do(v.tensor_copy(dcol[64:128, :], dd_[64:128, :, 1]))
                b = filled("dt")
                dtb = bcr[:, BC["dt_bias"]:BC["dt_bias"] + 12].unsqueeze(1).to_broadcast([P, 3, 12])
                do(TTT(dts[:, :, :], b[:, 0:36].rearrange("p (t u) -> p t u", t=3), dtb, ALU.add), "emptied_v")
                tell("dt_pre")
                v.wait_ge(S["dt_sp"], 3)
                do(STT(out=dts[:, :, :], in0=dts[:, :, :], scalar=0.0, in1=dta[:, :, :], op0=ALU.max, op1=ALU.add))
                avb = avl.unsqueeze(1).to_broadcast([P, 3, 12])
                do(STT(out=dta[:, :, :], in0=dts[:, :, :], scalar=-1.0, in1=avb, op0=ALU.mult, op1=ALU.mult), "dt_one")
                do(v.memset(xbcp[:, :, 0:2], 0.0))
                do(v.memset(xbcp[:, :, 130:134], 0.0))
                do(v.memset(xbcp[:, :, 390:392], 0.0), "conv_raw")
                for c in range(5):
                    v.wait_ge(S["emptied_a"], table[("xs0", "xs1", "xs2", "B", "C")[c]].count)
                    do(TS(conv[:, c, :], xbcp[:, c, 0:CONVW], col("conv_w", c), None, ALU.mult))
                    for k in range(1, 5):
                        do(STT(out=conv[:, c, :], in0=xbcp[:, c, k:k + CONVW], scalar=col("conv_w", 5 * k + c), in1=conv[:, c, :],
                               op0=ALU.mult, op1=ALU.add), "conv_in" if k == 4 else "v_chain")
                b = filled("cs")
                do(v.tensor_copy(csc[:, :, :, :].rearrange("p w t u -> p (w t u)"), b[:, 0:72]), "emptied_v")
                do(TTT(wst[:, :, :], csc[:, 1], csc[:, 0], ALU.subtract), "cs_pre")
                v.wait_ge(S["cs_exp"], 2)
                do(TTT(wst[:, :, :], wst[:, :, :], dts[:, :, :], ALU.mult))
                for gg in range(2):
                    r = slice(64 * gg, 64 * gg + 64)
                    src = dec[r].rearrange("p t (d h) -> p t d h", d=2)[:, :, :, 3 * gg:3 * gg + 3]
                    do(v.tensor_copy(dec2[r], src))
                do(v.memset(sin[:, 0].rearrange("p d i v -> p (d i v)"), 0.0))
                do(v.tensor_copy(sin[:, 1, 0].rearrange("p i v -> p (i v)"), bktok[:, 0, 0, 0:192]))
                do(v.tensor_copy(sin[:, 2, 1].rearrange("p i v -> p (i v)"), bktok[:, 0, 0, 192:384]))
                ada_later(4)
                for t in range(TT):
                    if t > 0:
                        v.wait_ge(S["bank_full"], table[f"lst{t - 1}"].n + 1)
                    v.wait_ge(S["emptied_a"], table[f"xtr{t}"].count)
                    for gg in range(2):
                        for d in range(2):
                            xs = tok[:, t, 192 * gg:192 * gg + 192].rearrange("p (i v) -> p i v", i=3)
                            do(TTT(xwt[:, gg, d], xs, bc3(wst[:, t, 6 * d + 3 * gg:6 * d + 3 * gg + 3], 3, 64), ALU.mult), "xw_ready")
                    b = filled(f"lst{t}")
                    do(v.tensor_copy(loc[:, t].rearrange("p d i v -> p (d i v)"), b[:, 0:384]), "emptied_v")
                for d, t0, t1 in ((0, 1, 2), (1, 2, 1)):
                    do(TTT(sin[:, t1, d], sin[:, t0, d], bc3(dec2[:, t0, d], 3, 64), ALU.mult))
                    do(TTT(sin[:, t1, d], sin[:, t1, d], loc[:, t0, d], ALU.add), "s_ready" if d == 1 else "v_chain")
                for t in range(TT):
                    if t > 0:
                        v.wait_ge(S["bank_full"], table[f"yb{t - 1}"].n + 1)
                    for q in range(3):
                        b = filled(f"csr{t}{q}")
                        u0 = 4 * q
                        do(TTT(diff[:, u0:u0 + 4, :], b[:, :].rearrange("p (u t) -> p u t", u=4),
                               bc3(csc[:, 0, t, u0:u0 + 4], 4, P), ALU.subtract), "csr_read")
                    for d in range(2):
                        nm = cc(C_NF if d == 0 else C_NB).unsqueeze(1).to_broadcast([P, 6, P])
                        dv = diff[:, 6 * d:6 * d + 6, :]
                        do(STT(out=dv, in0=dv, scalar=0.0, in1=nm, op0=ALU.min, op1=ALU.add), "d_ready")
                    v.wait_ge(S["ec_ready"], 3 * t + 3)
                    for gg in range(2):
                        r = slice(64 * gg, 64 * gg + 64)
                        for d in range(2):
                            u = slice(6 * d + 3 * gg, 6 * d + 3 * gg + 3)
                            cb_ = conv[r, 4, TOF[t]:TOF[t] + P].unsqueeze(1).to_broadcast([64, 3, P])
                            do(TTT(cdec[r, u, :], ecs[r, u, :], cb_, ALU.mult), "cd_ready")
                    v.wait_ge(S["e_ready"], 2 * t + 2)
                    for d in range(2):
                        dv = diff[:, 6 * d:6 * d + 6, :]
                        do(TTT(dv, dv, bc3(dts[:, t, 6 * d:6 * d + 6], 6, P), ALU.mult))
                    do(TTT(gmat[:, :, :], diff[:, 0:6, :], diff[:, 6:12, :], ALU.add))
                    for gg in range(2):
                        b = filled(f"cb{t}{gg}")
                        gv = gmat[:, 3 * gg:3 * gg + 3, :]
                        do(TTT(gv, b[:, 0:P].unsqueeze(1).to_broadcast([P, 3, P]), gv, ALU.mult), "emptied_v")
                    tell("g_ready")
                    ada_later(5 + t)
                    for gg, pieces in ((0, ((0, 0, 128), (1, 0, 64))), (1, ((1, 64, 128), (2, 0, 128)))):
                        b = filled(f"y{'ab'[gg]}{t}")
                        for n, (j, lo, hi) in enumerate(pieces):
                            do(STT(out=yv[lo:hi, j, P * t:P * t + P], in0=conv[lo:hi, j, TOF[t]:TOF[t] + P], scalar=dcol[lo:hi, j:j + 1],
                                   in1=b[lo:hi, P * j:P * j + P], op0=ALU.mult, op1=ALU.add), "emptied_v" if n == 1 else "v_chain")
                for j in range(NJ):
                    do(TTT(yv[:, j, :], yv[:, j, :], zz[:, j, :], ALU.mult), "ssd_y")
                ada_later(8)
                v.wait_ge(S["sn_rs"], 1)
                for j in range(NJ):
                    do(STT(out=yv[:, j, :], in0=yv[:, j, :], scalar=col("ssd_g", j), in1=rs[:, :], op0=ALU.mult, op1=ALU.mult))

                v.wait_ge(S["qk_sq"], 5)
                for c in range(4):
                    do(STT(out=qk[:, c, :], in0=qk[:, c, :], scalar=col("qn" if c < 2 else "kn"), in1=rs_at[:, c, :],
                           op0=ALU.mult, op1=ALU.mult), "qk_rs")
                for q in range(2):
                    b = filled(f"rot{q}")
                    bv = b[:, :].rearrange("p (o t) -> p o t", o=2)
                    sb_, cb_ = (cc(x, LAT).unsqueeze(1).to_broadcast([P, 2, LAT]) for x in (C_SIN, C_COS))
                    tmp = sq_at[:, 0:2, 0:LAT]
                    qv = qk[:, 2 * q:2 * q + 2, P:NT]
                    do(TTT(tmp, bv, sb_, ALU.mult), "emptied_v")
                    do(TTT(qv, qv, cb_, ALU.mult))
                    do(TTT(qv, qv, tmp, ALU.add), "qk_ready")
                sc = 32 ** -0.5
                for t in range(TT):
                    nk = P if t == 0 else NT
                    for j in range(2):
                        for i4 in range(4):
                            b = filled(f"sc{t}{j}{i4}")
                            do(v.tensor_reduce(nmx[:, i4:i4 + 1], b[:, 0:nk], AXX, ALU.max))
                            do(TS(nmx[:, i4:i4 + 1], nmx[:, i4:i4 + 1], -sc, None, ALU.mult), "sc_max")
                        v.wait_ge(S["sc_exp"], 4 * (2 * t + j) + 4)
                        do(v.reciprocal(ssm[:, 0:4], ssm[:, 0:4]))
                        if 2 * t + j > 0:
                            pt, pj = (t, 0) if j == 1 else (t - 1, 1)
                            v.wait_ge(S["bank_full"], table[f"wt{pt}{pj}1"].n + 1)
                        for hh in range(2):
                            e0, e1 = e_at[:, 2 * hh, 0:nk], e_at[:, 2 * hh + 1, 0:nk]
                            do(TS(e1, e1, ssm[:, 2 * hh + 1:2 * hh + 2], lam[:, 4:5], ALU.mult, ALU.mult))
                            do(STT(out=w_at[:, hh, 0:nk], in0=e0, scalar=ssm[:, 2 * hh:2 * hh + 1], in1=e1, op0=ALU.mult, op1=ALU.subtract), "w_ready")
                        b = filled(f"pv{t}{j}")
                        do(v.tensor_copy(o_at[:, j, P * t:P * t + P], b[:, 0:P]), "emptied_v")
                for j in range(2):
                    do(TTT(sq_at[:, j, :], o_at[:, j, :], o_at[:, j, :], ALU.mult), "o_ready")
                for j in range(2):
                    v.wait_ge(S["on_rs"], j + 1)
                    do(STT(out=yv[:, 6 + j, :], in0=o_at[:, j, :], scalar=lam[:, 5:6], in1=rs_at[:, j, :], op0=ALU.mult, op1=ALU.mult), "att_done")

                for j in range(NJ):
                    do(TS(kkn[:, j, :], rkv[:, 3 + j, :], col("kk", j), None, ALU.mult))
                    do(TS(kxa[:, j, :], rkv[:, 3 + j, :], col("ka", j), None, ALU.mult))
                do(TTT(en[:, :, :], kkn[:, :, :], kkn[:, :, :], ALU.mult), "kk_sq")
                ada_later(9)
                for j in range(NJ):
                    b = filled(f"kn{j}")
                    do(TS(ep[:, j, :], b[:, 0:NT], 1e-24, None, ALU.max), "emptied_v")
                tell("kk_max")
                ada_later(10)
                v.wait_ge(S["kk_rs"], 1)
                do(TTT(kkn[:, :, :], kkn[:, :, :], ep[:, :, :], ALU.mult))
                v.wait_ge(S["out_free"], 1)
                rv, kv = rkv[:, 0:3, :], rkv[:, 3:6, :]
                tile3 = lambda a: a[:, :, :].rearrange("p j (t c) -> p (j t) c", c=P)
                for d in range(2):
                    v.wait_ge(S["lora_ready"], 6 * d + 6)
                    for j in range(NJ):
                        do(v.tensor_tensor_scan(dd[:, j, :], cc(C_SCAN, NT), sig[:, j, :], 0.0, ALU.mult, ALU.add))
                    ddt, dxt, sgt = tile3(dd), tile3(dx), tile3(sig)
                    if d == 0:
                        do(v.tensor_copy(mref[:, 0:9], ddt[:, :, 64]))
                    else:
                        do(TTT(mref[:, 0:9], ddt[:, :, 64], sgt[:, :, 64], ALU.subtract))
                    do(TTT(ddt, ddt, bc3(mref, 9, P), ALU.subtract))
                    do(TTT(dx[:, :, :], dd[:, :, :], sig[:, :, :], ALU.subtract), "decay_pre")
                    do(STT(out=sig[:, :, :], in0=aa[:, :, :], scalar=-1.0, in1=kxa[:, :, :], op0=ALU.add, op1=ALU.mult))
                    do(TTT(sig[:, :, :], sig[:, :, :], kv, ALU.add))
                    do(TTT(aa[:, :, :], aa[:, :, :], kkn[:, :, :], ALU.mult))
                    v.wait_ge(S["decay_exp"], 4 * d + 4)
                    do(v.tensor_copy(fin[d].rearrange("p j t -> p (j t)"), tile3(en)[:, :, 127 if d == 0 else 0]))
                    do(TTT(f_ka[d][:, :, :], sig[:, :, :], ep[:, :, :], ALU.mult))
                    do(TTT(f_be[d][:, :, :], aa[:, :, :], ep[:, :, :], ALU.mult))
                    do(TTT(f_rho[d][:, :, :], rv, en[:, :, :], ALU.mult))
                    do(TTT(f_al[d][:, :, :], kkn[:, :, :], dx[:, :, :], ALU.mult), "f_ready")
                ada_later(11)
                norm_gain(8, SC2, "n2")
                for s in range(3):
                    for d in range(2):
                        t = TILE_OF[d][s]
                        pb = bc3(pre[d][:, :, t], 3, 64)
                        if s == 0:
                            do(v.memset(srk[:, d].rearrange("p j v -> p (j v)"), 0.0), "s0_ready")
                        else:
                            src = sri if s == 1 else srk
                            do(TTT(srk[:, d], src[:, d], pb, ALU.mult), "s0_ready")
                    for g4 in range(4):
                        d = g4 // 2
                        tri = {"L1": C_LS, "LT": C_US, "L2": C_US, "M1": C_UI, "M2": C_UI} if d == 0 else \
                              {"L1": C_US, "LT": C_LS, "L2": C_LS, "M1": C_LI, "M2": C_LI}
                        for name, dst in (("L1", m_x), ("LT", m_lt), ("L2", m_l2), ("M1", m_m1), ("M2", m_m2)):
                            b = filled(f"{name}{s}{g4}")
                            mk = cc(tri[name]).unsqueeze(1).to_broadcast([P, 3, P])
                            do(TTT(dst[:, g4], b[:, 0:384].rearrange("p (i t) -> p i t", i=3), mk, ALU.mult), "emptied_v")
                        idb = ident.unsqueeze(1).to_broadcast([P, 3, P])
                        for dst, src, lvl in ((m_x, m_x, C_LV if d == 0 else C_LVT), (m_xt, m_lt, C_LVT if d == 0 else C_LV)):
                            mk = cc(lvl).unsqueeze(1).to_broadcast([P, 3, P])
                            do(TTT(dst[:, g4], src[:, g4], mk, ALU.mult))
                            do(TTT(dst[:, g4], dst[:, g4], idb, ALU.add), "x1_ready")
                    for lv in range(1, 7):
                        for g4 in range(4):
                            d = g4 // 2
                            mk = cc((C_LV if d == 0 else C_LVT) + P * lv).unsqueeze(1).to_broadcast([P, 3, P])
                            b = filled(f"W{s}{lv}{g4}")
                            do(TTT(m_nw[:, g4], b[:, 0:384].rearrange("p (i t) -> p i t", i=3), mk, ALU.mult), "emptied_v")
                            do(TTT(m_nw[:, g4], m_nw[:, g4], ident.unsqueeze(1).to_broadcast([P, 3, P]), ALU.add), "nw_ready")
                    for g4 in range(4):
                        b = filled(f"rh{s}{g4}")
                        do(v.tensor_copy(rhs_b[:, g4], b[:, 0:192].rearrange("p (i v) -> p i v", i=3)), "emptied_v")
                    for g4 in range(4):
                        b = filled(f"u{s}{g4}")
                        do(TS(nu_b[:, g4], b[:, 0:192].rearrange("p (i v) -> p i v", i=3), -1.0, None, ALU.mult), "emptied_v")
                    for d in range(2):
                        t = TILE_OF[d][s]
                        b = filled(f"ry{s}{d}")
                        bv = b[:, 0:384].rearrange("p (j t) -> p j t", j=3)
                        yo = yv[:, 3:6, P * t:P * t + P]
                        if (s == 0 and d == 0) or s == 1:
                            do(v.tensor_copy(yo, bv), "emptied_v")
                        else:
                            do(TTT(yo, bv, yo, ALU.add), "emptied_v")
                    for d in range(2):
                        t = TILE_OF[d][s]
                        b = filled(f"rs{s}{d}")
                        bv = b[:, 0:192].rearrange("p (j v) -> p j v", j=3)
                        do(TTT(srk[:, d], bv, srk[:, d], ALU.add), "emptied_v")
                        do(TTT(srk[:, d], srk[:, d], bc3(fin[d][:, :, t], 3, 64), ALU.mult))
                        if s == 0:
                            do(v.tensor_copy(rs[:, 192 * d:192 * d + 192], sri[:, d].rearrange("p j v -> p (j v)")))
                            do(v.tensor_copy(sri[:, d], srk[:, d]), "rwkv_st")
                    if s == 0:
                        v.wait_ge(S["bank_full"], table["rfin1"].n + 1)
                        do(v.tensor_copy(sri[:, :, :, :].rearrange("p d j v -> p (d j v)"), rs[:, 0:384]))
                tell("rwkv_y")
                for j in range(NJ):
                    b = filled(f"mu{j}")
                    do(STT(out=dd[:, j, :], in0=b[:, 0:NT], scalar=-1.0 / 64, in1=yv[:, 3 + j, :], op0=ALU.mult, op1=ALU.add), "emptied_v")
                    do(TTT(en[:, j, :], dd[:, j, :], dd[:, j, :], ALU.mult), "gn_c")
                for j in range(NJ):
                    do(STT(out=ep[:, j, :], in0=rkv[:, j, :], scalar=col("rk", j), in1=rkv[:, 3 + j, :], op0=ALU.mult, op1=ALU.mult), "bon_in")
                for j in range(NJ):
                    v.wait_ge(S["gn_rs"], j + 1)
                    do(STT(out=dd[:, j, :], in0=dd[:, j, :], scalar=col("ln_g", j), in1=dx[:, j, :], op0=ALU.mult, op1=ALU.mult))
                for j in range(NJ):
                    b = filled(f"bon{j}")
                    do(TTT(sig[:, j, :], b[:, 0:NT], rkv[:, 6 + j, :], ALU.mult), "emptied_v")
                    do(STT(out=dd[:, j, :], in0=dd[:, j, :], scalar=col("ln_b", j), in1=sig[:, j, :], op0=ALU.add, op1=ALU.add))
                for j in range(NJ):
                    b = filled(f"gt{j}")
                    do(TTT(yv[:, 3 + j, :], b[:, 0:NT], dd[:, j, :], ALU.mult), "emptied_v")
                    tell("y_ready")
                for m in range(KD):
                    b = filled(f"out{m}")
                    for n, (st, lo, hi) in enumerate(seg):
                        do(STT(out=x_t[:, m, lo:hi], in0=b[:, lo:hi], scalar=mod[:, G1 + m, st:st + 1], in1=x_t[:, m, lo:hi],
                               op0=ALU.mult, op1=ALU.add), "emptied_v" if n == 1 else "v_chain")
                v.wait_ge(S["bank_full"], table[f"out{KD - 1}"].n + 1)
                for c in range(KD):
                    do(TTT(sq8[:, c, :], x_t[:, c, :], x_t[:, c, :], ALU.mult), "x2_ready")
                v.wait_ge(S["h2_part"], 1)
                for c in range(KD):
                    do(TTT(hv[:, c, :], x_t[:, c, :], rs[:, :], ALU.mult), "x2_ready")
                b = filled("rt")
                rb = bcr[:, BC["rbias"]:BC["rbias"] + 20].unsqueeze(1).to_broadcast([P, 3, 20])
                do(TTT(lg, b[:, 0:60].rearrange("p (t u) -> p t u", t=3), rb, ALU.add), "emptied_v")
                iota = cc(C_IOTA, 4).unsqueeze(1).to_broadcast([P, 3, 4])
                b4 = lambda a: a.to_broadcast([P, 3, 4])

                def first_max(src, top, hot):
                    do(v.tensor_reduce(top, src, AXX, ALU.max))
                    do(TTT(hot, src, b4(top), ALU.is_equal))
                    do(TTT(hot, hot, iota, ALU.mult))
                    do(v.tensor_reduce(r5, hot, AXX, ALU.max))
                    do(TTT(hot, hot, b4(r5), ALU.is_equal))

                g4_, e16 = lg[:, :, 0:4], lg[:, :, 4:20].rearrange("p t (g e) -> p t g e", g=4)
                first_max(g4_, r1, rg1)
                do(TTT(rg2, g4_, b4(r1), ALU.subtract), "rt_pre")
                e3 = rg3.rearrange("p t (g e) -> p t g e", g=4)
                for gg in range(4):
                    do(TTT(e3[:, :, gg, :], e16[:, :, gg, :], b4(rg1[:, :, gg:gg + 1]), ALU.mult))
                do(v.tensor_reduce(rg4, rg3.rearrange("p t (g e) -> p t e g", g=4), AXX, ALU.add))
                first_max(rg4, r2, rg5)
                do(STT(out=rg4, in0=rg5, scalar=NEG, in1=rg4, op0=ALU.mult, op1=ALU.add))
                first_max(rg4, r3, rg6)
                do(TTT(r3, r3, r2, ALU.subtract), "rt_pre")
                v.wait_ge(S["rt_exp"], 2)
                do(v.tensor_reduce(r1, rg2, AXX, ALU.add))
                do(v.reciprocal(r1, r1))
                do(TS(r4, r3, 1.0, None, ALU.add))
                do(v.reciprocal(r4, r4))
                do(TTT(r4, r4, r1, ALU.mult))
                do(TTT(r3, r3, r4, ALU.mult))
                do(TTT(rg5, rg5, b4(r4), ALU.mult))
                do(TTT(rg6, rg6, b4(r3), ALU.mult))
                do(TTT(rg5, rg5, rg6, ALU.add))
                gt_ = gate.rearrange("p t (g e) -> p t g e", g=4)
                for gg in range(4):
                    do(TTT(gt_[:, :, gg, :], rg5, b4(rg1[:, :, gg:gg + 1]), ALU.mult), "gate_ready" if gg == 3 else "v_chain")
                v.wait_ge(S["emptied_a"], table[f"gb{EXPERTS - 1}"].count)
                tell("t_moe")
                with v.Fori(0, EXPERTS // 2) as jj:
                    for e in range(2):
                        for m in range(2):
                            n = 2 * e + m
                            v.wait_ge(S["hp_moe"], jj * 8 + (2 * n + 2))
                            v.wait_ge(S["s_moe"], jj * 4 + (n + 2))
                            TTT(th[:, m, :], ps[:, 7, 0:NT], sh[:, m, :], ALU.mult).then_inc(S["t_moe"], 1)
                            v.wait_ge(S["t_moe"], jj * 4 + (n + 2))
                            TTT(hid[:, e, m, :], th[:, m, :], gates[:, bass.ds(jj * 2 + e, 1), :].rearrange("p a t -> p (a t)"),
                                ALU.mult).then_inc(S["t2_moe"], 1)
                            v.wait_ge(S["t2_moe"], jj * 4 + (n + 1))
                v.wait_ge(S["moe_y"], 1)
                for t in range(TT):
                    for hf in range(2):
                        do(v.tensor_copy(ytok[:, t, 512 * hf:512 * hf + 512], ps[:, 2 * t + hf, :]), "moe_tok")
                for c in range(KD):
                    b = filled(f"ytr{c}")
                    for n, (st, lo, hi) in enumerate(seg):
                        do(STT(out=x_t[:, c, lo:hi], in0=b[:, lo:hi], scalar=mod[:, G2 + c, st:st + 1], in1=x_t[:, c, lo:hi],
                               op0=ALU.mult, op1=ALU.add), "emptied_v" if n == 1 else "v_chain")
                meet(v, l + 1)
                cnt.clear()

        @block.scalar
        def _(a):
            cnt = counter()
            tb = [pre_table]

            def do(ins, name="a_chain"):
                step(a, cnt, ins, name)

            def filled(name):
                a.wait_ge(S["bank_full"], tb[0][name].n + 1)
                return bank(tb[0][name])

            def tell(name):
                cnt[name] = cnt.get(name, 0) + 1
                a.sem_inc(S[name], 1)

            def act(out, in_, f, **kw):
                return a.activation(out, in_, f, **kw)

            def exp_ln_tables():
                a.preload_act_table_set("natural_log_exp_and_others")

            eps = cst[:, C_EPS:C_EPS + 1]
            b = filled("cond")
            do(act(scond[:, :, :], b[:, 0:16].rearrange("p (s c) -> p c s", s=2), ACT.Silu), "emptied_a")
            meet(a, 0)
            cnt.clear()
            tb[0] = table
            with a.Fori(0, DEPTH) as l:
                exp_ln_tables()

                def ada_copy(q):
                    b = filled(f"ar{q}")
                    if q > ADA_EARLY:
                        a.wait_ge(S["bank_full"], table[f"at{q - 1}"].n + 1)
                    do(act(ada_row(q), b[0:2, :], ACT.Copy), "emptied_a")

                for q in range(ADA_EARLY):
                    ada_copy(q)
                a.wait_ge(S["lam_pre"], 1)
                do(act(lam[:, 2:4], lam[:, 0:2], ACT.Exp), "lam_exp")
                do(act(avl, bcr[:, BC["a_log"]:BC["a_log"] + 12], ACT.Exp), "lam_exp")
                b = filled("sum1")
                do(act(rs[:, :], b[:, 0:NT], ACT.Ln, scale=1.0 / D, bias=eps), "emptied_a")
                do(act(rs[:, :], rs[:, :], ACT.Exp, scale=-0.5), "h_part")
                a.wait_ge(S["mod_ready"], 1)
                for c in range(KD):
                    a.wait_ge(S["x_ready"], c + 1)
                    for st, lo, hi in ((1, 0, P), (0, P, NT)):
                        do(act(hv[:, c, lo:hi], hv[:, c, lo:hi], ACT.Identity, scale=gs[:, c, st:st + 1], bias=mod[:, SH1 + c, st:st + 1]), "h_ready")
                a.wait_ge(S["dt_pre"], 1)
                do(act(dta[:, :, :], dts[:, :, :], ACT.Abs), "dt_sp")
                do(act(dta[:, :, :], dta[:, :, :], ACT.Exp, scale=-1.0), "dt_sp")
                do(act(dta[:, :, :], dta[:, :, :], ACT.Ln, bias=1.0), "dt_sp")
                a.wait_ge(S["conv_raw"], 1)
                for slot_ in IN_SLOTS:
                    for name, _ in slot_:
                        if name == "va":
                            b = filled("va0")
                            do(act(vat[:, 0:2, :], b[:, :].rearrange("p (t n) -> p t n", t=2), ACT.Copy), "emptied_a")
                            b = filled("va1")
                            do(act(vat[:, 2, :], b[:, 0:256], ACT.Copy), "emptied_a")
                            continue
                        b = filled(name)
                        if name in ("xs0", "xs1", "xs2", "B", "C"):
                            c = ("xs0", "xs1", "xs2", "B", "C").index(name)
                            do(act(xbcp[:, c, 2:130], b[:, 0:P], ACT.Copy))
                            do(act(xbcp[:, c, 134:390], b[:, P:NT], ACT.Copy), "emptied_a")
                        elif name[0] == "z":
                            do(act(zz[:, int(name[1]), :], b[:, 0:NT], ACT.Silu), "emptied_a")
                        elif name == "xwa":
                            do(act(xwa[0:64, :], b[0:64, 0:NT], ACT.Tanh))
                            do(act(xwa[64:128, :], b[64:128, 0:NT], ACT.Copy), "emptied_a")
                        elif name == "xg":
                            do(act(xg[:, :], b[:, 0:NT], ACT.Sigmoid), "emptied_a")
                        else:
                            if name[0] == "q":
                                dst = qk[:, int(name[1]), :]
                            elif name[0] == "k":
                                dst = qk[:, 2 + int(name[1]), :]
                            else:
                                dst = rkv[:, {"r": 0, "v": 6}[name[0]] + int(name[1]) if name[:2] != "rk" else 3 + int(name[2]), :]
                            do(act(dst, b[:, 0:NT], ACT.Copy), "emptied_a")
                for c in range(5):
                    a.wait_ge(S["conv_in"], c + 1)
                    do(act(conv[:, c, :], conv[:, c, :], ACT.Silu, bias=col("conv_b", c)), "conv_done")
                exp_ln_tables()
                a.wait_ge(S["cs_pre"], 1)
                do(act(wst[:, :, :], wst[:, :, :], ACT.Exp), "cs_exp")
                do(act(dec[:, :, :], csc[:, 1], ACT.Exp), "cs_exp")
                ada_copy(4)
                for t in range(TT):
                    b = filled(f"xtr{t}")
                    do(act(tok[:, t, :], b[:, :], ACT.Copy), "emptied_a")
                ada_copy(5)
                for t in range(TT):
                    if t > 0:
                        a.wait_ge(S["cd_ready"], 4 * t)
                    for q in range(3):
                        b = filled(f"csr{t}{q}")
                        a.wait_ge(S["csr_read"], 3 * t + q + 1)
                        do(act(ecs[:, 4 * q:4 * q + 4, :], b[:, :].rearrange("p (u t) -> p u t", u=4), ACT.Exp), "emptied_a")
                        tell("ec_ready")
                    for d in range(2):
                        a.wait_ge(S["d_ready"], 2 * t + d + 1)
                        dv = diff[:, 6 * d:6 * d + 6, :]
                        do(act(dv, dv, ACT.Exp), "e_ready")
                    ada_copy(6 + t)
                for d in range(2):
                    b = filled(f"sfin{d}")
                    do(act(stg[0:64, 384 * d:384 * d + 384], b[0:64, 0:384], ACT.Copy), "emptied_a")
                    tell("stage_ssd")
                for j in range(NJ):
                    a.wait_ge(S["ssd_y"], j + 1)
                    do(act(rs_at[:, j, :], yv[:, j, :], ACT.Square), "yssd_sq")
                ada_copy(9)
                b = filled("sn")
                do(act(rs[:, :], b[:, 0:NT], ACT.Ln, scale=1.0 / 384, bias=eps), "emptied_a")
                do(act(rs[:, :], rs[:, :], ACT.Exp, scale=-0.5), "sn_rs")
                do(act(sq_at[:, :, :], qk[:, :, :], ACT.Square), "qk_sq")
                for c in range(4):
                    b = filled(f"qn{c}")
                    do(act(rs_at[:, c, :], b[:, 0:NT], ACT.Ln, bias=eps), "emptied_a")
                    do(act(rs_at[:, c, :], rs_at[:, c, :], ACT.Exp, scale=-0.5), "qk_sq")
                b = filled("kout")
                do(act(stg[:, 768:1024], b[:, 0:256], ACT.Copy), "emptied_a")
                tell("stage_kv")
                sc = 32 ** -0.5
                for t in range(TT):
                    nk = P if t == 0 else NT
                    for j in range(2):
                        if 2 * t + j > 0:
                            a.wait_ge(S["w_ready"], 2 * (2 * t + j))
                        for i4 in range(4):
                            b = filled(f"sc{t}{j}{i4}")
                            a.wait_ge(S["sc_max"], 4 * (2 * t + j) + i4 + 1)
                            do(act(e_at[:, i4, 0:nk], b[:, 0:nk], ACT.Exp, scale=sc, bias=nmx[:, i4:i4 + 1], accum_out=ssm[:, i4:i4 + 1]), "emptied_a")
                            tell("sc_exp")
                        for hh in range(2):
                            b = filled(f"wt{t}{j}{hh}")
                            do(act(wt_at[:, hh, 0:nk], b[:, 0:nk], ACT.Copy), "emptied_a")
                for j in range(2):
                    b = filled(f"on{j}")
                    do(act(rs_at[:, j, :], b[:, 0:NT], ACT.Ln, scale=1.0 / 64, bias=eps), "emptied_a")
                    do(act(rs_at[:, j, :], rs_at[:, j, :], ACT.Exp, scale=-0.5), "on_rs")
                ada_copy(10)
                a.wait_ge(S["kk_max"], 1)
                do(act(ep[:, :, :], ep[:, :, :], ACT.Ln, scale=65536.0))
                do(act(ep[:, :, :], ep[:, :, :], ACT.Exp, scale=-0.5, bias=cst[:, C_KKB:C_KKB + 1]), "kk_rs")
                ada_copy(11)
                for d in range(2):
                    if d == 1:
                        a.wait_ge(S["f_ready"], 1)
                    for j in range(NJ):
                        b = filled(f"lw{d}{j}")
                        do(act(sig[:, j, :], b[:, 0:NT], ACT.Sigmoid, bias=col("w0", 3 * d + j)), "emptied_a")
                        tell("lora_ready")
                        b = filled(f"la{d}{j}")
                        do(act(aa[:, j, :], b[:, 0:NT], ACT.Sigmoid, bias=col("a0", 3 * d + j)), "emptied_a")
                        tell("lora_ready")
                    exp_ln_tables()
                    a.wait_ge(S["decay_pre"], d + 1)
                    pr = pre[d].rearrange("p j t -> p (j t)")
                    if d == 0:
                        do(act(pr, mref[:, 0:9], ACT.Exp, scale=-G), "decay_exp")
                        do(act(en[:, :, :], dd[:, :, :], ACT.Exp, scale=-G), "decay_exp")
                        do(act(ep[:, :, :], dd[:, :, :], ACT.Exp, scale=G), "decay_exp")
                        do(act(dx[:, :, :], dx[:, :, :], ACT.Exp, scale=-G), "decay_exp")
                    else:
                        do(act(pr, dd[:, :, :].rearrange("p j (t c) -> p (j t) c", c=P)[:, :, 127], ACT.Exp, scale=-G), "decay_exp")
                        do(act(en[:, :, :], dx[:, :, :], ACT.Exp, scale=G), "decay_exp")
                        do(act(ep[:, :, :], dx[:, :, :], ACT.Exp, scale=-G), "decay_exp")
                        do(act(dx[:, :, :], dd[:, :, :], ACT.Exp, scale=G), "decay_exp")
                for t in range(TT):
                    b = filled(f"vt{t}")
                    do(act(vtok[:, t, :], b[:, 0:NT], ACT.Copy), "emptied_a")
                for s in range(3):
                    if s > 0:
                        a.wait_ge(S["bank_full"], table[f"rs{s - 1}1"].n + 1)
                    for d in range(2):
                        for w in range(2):
                            b = filled(f"{'bk'[w]}t{s}{d}")
                            do(act(bktok[:, d, w, :], b[:, 0:NT], ACT.Copy), "emptied_a")
                    for lv in range(1, 7):
                        for g4 in range(4):
                            if lv < 6:
                                b = filled(f"X{s}{lv}{g4}")
                                do(act(m_x[:, g4], b[:, 0:384].rearrange("p (i t) -> p i t", i=3), ACT.Copy), "emptied_a")
                            b = filled(f"T{s}{lv}{g4}")
                            do(act(m_xt[:, g4], b[:, 0:384].rearrange("p (i t) -> p i t", i=3), ACT.Copy), "emptied_a")
                    if s == 0:
                        a.wait_ge(S["out_free"], 1)
                        for d in range(2):
                            b = filled(f"rfin{d}")
                            do(act(stg[0:64, 384 * d:384 * d + 384], b[0:64, 0:384], ACT.Copy), "emptied_a")
                            tell("stage_rwkv")
                for j in range(NJ):
                    b = filled(f"var{j}")
                    do(act(dx[:, j, :], b[:, 0:NT], ACT.Ln, scale=1.0 / 64, bias=cst[:, C_GN:C_GN + 1]), "emptied_a")
                    do(act(dx[:, j, :], dx[:, j, :], ACT.Exp, scale=-0.5), "gn_rs")
                a.wait_ge(S["mod_ready"], 2)
                b = filled("sum2")
                do(act(rs[:, :], b[:, 0:NT], ACT.Ln, scale=1.0 / D, bias=eps), "emptied_a")
                do(act(rs[:, :], rs[:, :], ACT.Exp, scale=-0.5), "h2_part")
                for c in range(KD):
                    a.wait_ge(S["x2_ready"], KD + c + 1)
                    for st, lo, hi in ((1, 0, P), (0, P, NT)):
                        do(act(hv[:, c, lo:hi], hv[:, c, lo:hi], ACT.Identity, scale=gs[:, 8 + c, st:st + 1], bias=mod[:, SH2 + c, st:st + 1]), "h2_ready")
                a.wait_ge(S["rt_pre"], 2)
                do(act(rg2, rg2, ACT.Exp), "rt_exp")
                do(act(r3, r3, ACT.Exp), "rt_exp")
                for e in range(EXPERTS):
                    b = filled(f"gb{e}")
                    do(act(gates[:, e, :], b[:, 0:NT], ACT.Copy), "emptied_a")
                tell("s_moe")
                with a.Fori(0, EXPERTS // 2) as jj:
                    for e in range(2):
                        for m in range(2):
                            n = 2 * e + m
                            a.wait_ge(S["hp_moe"], jj * 8 + (2 * n + 1))
                            act(sh[:, m, :], ps[:, 6, 0:NT], ACT.Silu).then_inc(S["s_moe"], 1)
                meet(a, l + 1)
                cnt.clear()
            tb[0] = post_table
            for t in range(TT):
                for hf in range(2):
                    b = filled(f"o{t}{hf}")
                    do(act(xin[:, t, 512 * hf:512 * hf + 512], b[:, :], ACT.Copy), "emptied_a")
                    tell("tok_done")


_OUTS = [(1, CTX, D), (1, LAT, D), (1, DEPTH, CTX, 4, 2, 32), (1, DEPTH, CTX, 4, 64), (1, DEPTH, 2, HEADS, 64, 64), (1, DEPTH, 2, HEADS, 64, 64)]


def kernel(**inputs):
    import numpy as _np
    import concourse.bacc as _bacc
    from concourse import mybir as _mybir
    from concourse.bass_utils import run_bass_kernel_spmd as _run

    nc = _bacc.Bacc("TRN2", target_bir_lowering=False, num_devices=1)
    arrays, aps = {}, {}
    for name, value in inputs.items():
        value = _np.ascontiguousarray(value)
        arrays["in_" + name] = value
        aps[name] = nc.dram_tensor("in_" + name, value.shape, _mybir.dt.float32, kind="ExternalInput").ap()
    arrays["shape_constants"] = shape_constants()
    arrays["layer_constants"] = layer_constants()
    consts = nc.dram_tensor("shape_constants", (P, C_N), _mybir.dt.float32, kind="ExternalInput").ap()
    lconst = nc.dram_tensor("layer_constants", (DEPTH, 2), _mybir.dt.float32, kind="ExternalInput").ap()
    outs = [nc.dram_tensor(f"out_{i}", s, _mybir.dt.float32, kind="ExternalOutput").ap() for i, s in enumerate(_OUTS)]
    build(nc, aps, outs, consts, lconst)
    r = _run(nc, [arrays], core_ids=[0])
    return tuple(r.results[0][f"out_{i}"] for i in range(len(_OUTS)))
```

```python
import math
from contextlib import ExitStack

import numpy as np
import concourse.bass as bass
from concourse import mybir

F32 = mybir.dt.float32
BF16 = mybir.dt.bfloat16
F32R = mybir.dt.float32r
ACT = mybir.ActivationFunctionType
ALU = mybir.AluOpType
AXX = mybir.AxisListType.X

P = 128
D = 1024
KD = D // P
DEPTH = 2
CTX, LAT = 128, 256
NT = CTX + LAT
TT = NT // P
HEADS = 6
NJ = 3
N_IN = 3212
COL = dict(xbc=0, z=640, dt=1024, r=1036, k=1420, v=1804, xw=2188, xa=2252, xg=2316, qa=2444, ka=2700, va=2956)
EXPERTS, HIDDEN = 16, 256
SLOT = KD * 256
RING = 6
G = math.exp(-0.5)
NEG = -1.0e30
PAD = [2, 134, 262]
CONVW = 388
TOF = [0, 132, 260]
TILE_OF = ((0, 1, 2), (0, 2, 1))

IN_SLOTS = [[("xs0", 0), ("xs1", 128)], [("xs2", 256), ("B", 384)], [("C", 512), ("z0", 640)],
            [("z1", 768), ("z2", 896)], [("q0", 2444), ("q1", 2572)], [("k0", 2700), ("k1", 2828)],
            [("va", 2956)], [("r0", 1036), ("r1", 1164)], [("r2", 1292), ("rk0", 1420)],
            [("rk1", 1548), ("rk2", 1676)], [("xwa", 2188), ("xg", 2316)], [("v0", 1804), ("v1", 1932)],
            [("v2", 2060)]]
N_INS = len(IN_SLOTS)
ADA_FIRST, ADA_LATER = 8, 16
IN_SLOT0 = ADA_FIRST
ADA_SLOT0 = IN_SLOT0 + N_INS
LORA_SLOT = ADA_SLOT0 + ADA_LATER
ADA_GROUPS, ADA_EARLY = (ADA_FIRST + ADA_LATER) // 2, ADA_FIRST // 2
OUT_SLOT = LORA_SLOT + 1
PRE_SLOTS = OUT_SLOT + 4
LAYER_SLOTS = PRE_SLOTS + 3 * EXPERTS
assert PRE_SLOTS % RING == 0 and LAYER_SLOTS % RING == 0 and RING == 6

C_ID, C_ONE, C_B32, C_B64, C_UI, C_LI, C_US, C_LS, C_ROT, C_NF, C_NB = (128 * i for i in range(11))
C_LV = 128 * 11
C_LVT = C_LV + 7 * 128
C_COS = C_LVT + 7 * 128
C_SIN = C_COS + LAT
C_SCAN = C_SIN + LAT
C_IOTA = C_SCAN + NT
C_EPS, C_GN, C_KKB = C_IOTA + 4, C_IOTA + 5, C_IOTA + 6
C_N = C_IOTA + 8

ROWS_A = [("conv_w", 25), ("conv_b", 5), ("ssd_g", 3), ("w0", 6), ("a0", 6), ("kk", 3), ("ka", 3), ("rk", 3),
          ("ln_g", 3), ("ln_b", 3), ("qn", 1), ("kn", 1), ("on", 1)]
ROWS_B = [("ada_b", 48), ("n1", 8), ("n2", 8)]
NA = sum(n for _, n in ROWS_A)
NB = sum(n for _, n in ROWS_B)
PAR = {}
_at = 0
for _n, _c in ROWS_A + ROWS_B:
    PAR[_n] = _at
    _at += _c
BC = dict(dt_bias=0, a_log=12, d=24, rbias=30, lam=50, lami=178)
NBC = 180
SH1, SC1, G1, SH2, SC2, G2 = (8 * i for i in range(6))


def shape_constants():
    c = np.zeros((P, C_N), np.float32)
    i, j = np.arange(P)[:, None], np.arange(P)[None, :]
    put = lambda at, m: c.__setitem__((slice(None), slice(at, at + m.shape[1])), m.astype(np.float32))
    put(C_ID, i == j)
    put(C_ONE, np.ones((P, P)))
    put(C_B32, (i // 32 == j // 32) / 32.0)
    put(C_B64, i // 64 == j // 64)
    put(C_UI, i <= j)
    put(C_LI, i >= j)
    put(C_US, i < j)
    put(C_LS, i > j)
    rot = np.zeros((P, P))
    for o in range(P):
        if o % 16 < 8:
            rot[o + 8, o] = -1.0
        else:
            rot[o - 8, o] = 1.0
    put(C_ROT, rot)
    put(C_NF, np.where(i <= j, 0.0, NEG))
    put(C_NB, np.where(i >= j, 0.0, NEG))
    for n in range(7):
        b = 1 << n
        m = (i // (2 * b) == j // (2 * b)) & (i % (2 * b) >= b) & (j % (2 * b) < b)
        put(C_LV + 128 * n, -1.0 * m)
        put(C_LVT + 128 * n, -1.0 * m.T)
    inv = (np.float32(10000.0) ** (-np.arange(8, dtype=np.float32) / 8)).astype(np.float32)
    t = np.arange(LAT)
    row, col = (t // 64).astype(np.float32), (t % 64).astype(np.float32)
    for p in range(P):
        pos = row if p % 32 < 16 else col
        ang = (pos * inv[p % 8]).astype(np.float32)
        c[p, C_COS:C_COS + LAT] = np.cos(ang)
        c[p, C_SIN:C_SIN + LAT] = np.sin(ang)
    c[:, C_SCAN:C_SCAN + NT] = (np.arange(NT) % P != 0)[None, :]
    c[:, C_IOTA:C_IOTA + 4] = [4, 3, 2, 1]
    c[:, C_EPS] = 1e-6
    c[:, C_GN] = 64e-5
    c[:, C_KKB] = 8 * math.log(2.0)
    return c


def layer_constants():
    li = [0.8 - 0.6 * math.exp(-0.3 * l) for l in range(DEPTH)]
    return np.array([[x, 1.0 - x] for x in li], np.float32)


def job_order():
    def ada(q):
        return ([(f"at{q - 1}", "v")] if q > ADA_EARLY else []) + [(f"ar{q}", "a")]

    jobs = [(f"ar{q}", "a") for q in range(ADA_EARLY)]
    jobs += [("sum1", "a"), ("prmA", "v"), ("prmB", "v"), ("sst", "v"), ("rst", "v"), ("kct", "v"), ("ada", "v"), ("dt", "v")]
    for slot in IN_SLOTS:
        for name, _ in slot:
            jobs += [("va0", "a"), ("va1", "a")] if name == "va" else [(name, "a")]
    jobs += [("cs", "v")] + ada(4)
    jobs += [(f"xtr{t}", "a") for t in range(TT)] + ada(5)
    jobs += [(f"lst{t}", "v") for t in range(TT)]
    for t in range(TT):
        jobs += [(f"csr{t}{i}", "a") for i in range(3)]
        jobs += [(f"cb{t}0", "v"), (f"cb{t}1", "v")] + ada(6 + t) + [(f"ya{t}", "v"), (f"yb{t}", "v")]
    jobs += [("sfin0", "a"), ("sfin1", "a")] + ada(9) + [("sn", "a")]
    jobs += [(f"qn{c}", "a") for c in range(4)]
    jobs += [("kout", "a"), ("rot0", "v"), ("rot1", "v")]
    for u in range(2 * TT + 1):
        if u < 2 * TT:
            jobs += [(f"sc{u // 2}{u % 2}{i}", "a") for i in range(4)]
        if u > 0:
            t, j = divmod(u - 1, 2)
            jobs += [(f"wt{t}{j}0", "a"), (f"wt{t}{j}1", "a"), (f"pv{t}{j}", "v")]
    jobs += [("on0", "a"), ("on1", "a")]
    jobs += [(f"kn{j}", "v") for j in range(NJ)]
    for d in range(2):
        for j in range(NJ):
            jobs += [(f"lw{d}{j}", "a"), (f"la{d}{j}", "a")]
        jobs += ada(10 + d)
    jobs += [(f"vt{t}", "a") for t in range(TT)] + [(f"at{ADA_GROUPS - 1}", "v")]
    for s in range(3):
        for d in range(2):
            jobs += [(f"bt{s}{d}", "a"), (f"kt{s}{d}", "a")]
        for g in range(4):
            jobs += [(f"L1{s}{g}", "v"), (f"LT{s}{g}", "v")] + [(f"{n}{s}{g}", "a") for n in ("L2", "M1", "M2")]
        for lv in range(1, 7):
            jobs += [(f"W{s}{lv}{g}", "v") for g in range(4)]
            for g in range(4):
                jobs += ([(f"X{s}{lv}{g}", "a")] if lv < 6 else []) + [(f"T{s}{lv}{g}", "a")]
        jobs += [(f"rh{s}{g}", "v") for g in range(4)]
        jobs += [(f"u{s}{g}", "v") for g in range(4)]
        jobs += [(f"ry{s}{d}", "v") for d in range(2)]
        jobs += [(f"rs{s}{d}", "v") for d in range(2)]
        if s == 0:
            jobs += [("rfin0", "a"), ("rfin1", "a")]
    jobs += [(f"mu{j}", "v") for j in range(NJ)]
    jobs += [(f"var{j}", "a") for j in range(NJ)]
    jobs += [(f"bon{j}", "v") for j in range(NJ)]
    jobs += [(f"gt{j}", "v") for j in range(NJ)]
    jobs += [(f"out{m}", "v") for m in range(KD)]
    jobs += [("sum2", "a"), ("rtr", "v"), ("rt", "v")]
    jobs += [(f"gb{e}", "a") for e in range(EXPERTS)]
    jobs += [(f"ytr{c}", "v") for c in range(KD)]
    return jobs


class Job:
    def __init__(self, n, by, count, before):
        self.n, self.by, self.count, self.before = n, by, count, before


def job_table(order):
    table, counts, listed = {}, {"v": 0, "a": 0}, []
    for n, (name, by) in enumerate(order):
        counts[by] += 1
        table[name] = Job(n, by, counts[by], listed[n - 8] if n >= 8 else None)
        listed.append(table[name])
    assert len(table) == len(order)
    return table, counts


PRE = [(f"x{c}", "v") for c in range(KD)] + [("cond", "a")]
POST = [(f"o{t}{h}", "a") for t in range(TT) for h in range(2)]


def build(nc, A, O, consts_d, lconst_d):
    with ExitStack() as ctx:
        def sb(name, n, dt=F32):
            return ctx.enter_context(nc.sbuf_tensor(name, [P, n], dt))

        twice = [("ring", RING * SLOT), ("h_t", KD * NT), ("y_t", KD * NT), ("rkv", 9 * NT), ("ar_b", 9216), ("ar_a", 7680)]
        with ExitStack() as first:
            ring, h_t, y_t, rkv_f, ar_b, ar_a = [first.enter_context(nc.sbuf_tensor(name, [P, n], F32)) for name, n in twice]
        ring_r, h_r, y_r, rkv_r, ar_br, ar_ar = [ctx.enter_context(nc.sbuf_tensor(name + "_r", [P, n], F32R)) for name, n in twice]
        cst = sb("cst", C_N)
        x_t = sb("x_t", KD * NT)[:, :].rearrange("p (c t) -> p c t", t=NT)
        xg = sb("xg", NT)
        rkv = rkv_f[:, :].rearrange("p (c t) -> p c t", t=NT)
        vtok = sb("vtok", TT * NT)[:, :].rearrange("p (t n) -> p t n", t=TT)
        kct = sb("kct", 256)[:, :].rearrange("p (j t) -> p j t", j=2)
        cv = sb("cv", 256)
        par = sb("par", NA + NB)
        bcr = sb("bcr", NBC)
        mod = sb("mod", 96)[:, :].rearrange("p (m s) -> p m s", s=2)
        gs = sb("gs", 32)[:, :].rearrange("p (m s) -> p m s", s=2)
        scond = sb("scond", 16)[:, :].rearrange("p (c s) -> p c s", s=2)
        wrt = sb("wrt", KD * 20)[:, :].rearrange("p (c n) -> p c n", c=KD)
        wdt = sb("wdt", KD * 12)[:, :].rearrange("p (c n) -> p c n", c=KD)
        bktok = sb("bktok", 4 * NT)[:, :].rearrange("p (d w n) -> p d w n", d=2, w=2)
        xwa = bktok[:, 1, 0, :]
        srk = sb("srk", 384)[:, :].rearrange("p (d j v) -> p d j v", d=2, j=3)
        sri = sb("sri", 384)[:, :].rearrange("p (d j v) -> p d j v", d=2, j=3)
        stg = sb("stg", 1024)
        sml = sb("sml", 420)
        rs = sb("rs", NT)
        zer = sb("zer", 512, BF16)
        ps = ctx.enter_context(nc.psum_tensor("ps", [P, 8, 512], F32))

        def cc(at, n=128):
            return cst[:, at:at + n]

        ident, ones = cc(C_ID), cc(C_ONE)
        slot = lambda k: ring[:, (k % RING) * SLOT:(k % RING + 1) * SLOT]
        slot8 = lambda k: slot(k).rearrange("p (c n) -> p c n", c=KD)
        slot2 = lambda k: slot(k).rearrange("p (c n) -> p c n", c=2)
        hv = h_t[:, :].rearrange("p (c t) -> p c t", t=NT)
        yv = y_t[:, :].rearrange("p (c t) -> p c t", t=NT)

        def col(name, i=0, lo=0, hi=P):
            return par[lo:hi, PAR[name] + i:PAR[name] + i + 1]

        xin = ar_a[:, 0:3 * D].rearrange("p (t d) -> p t d", t=TT)
        st_b = ar_b[:, 7168:9216]
        ini = st_b[0:64, 0:768].rearrange("p (d i g n) -> p d i g n", d=2, i=3, g=2)
        inr = st_b[0:64, 768:1536].rearrange("p (u n) -> p u n", u=12)
        ck = st_b[:, 1536:1792]
        rows_a, rows_b = st_b[0:NA, 1792:1920], st_b[0:NB, 1920:2048]
        ada_row = lambda q: h_t[0:2, 512 * q:512 * q + 512] if q < ADA_EARLY else ar_a[0:2, 6912:7424]
        diff = ar_a[:, 0:1536].rearrange("p (u t) -> p u t", u=12)
        ecs = ar_a[:, 1536:3072].rearrange("p (u t) -> p u t", u=12)
        cdec = ar_a[:, 3072:4608].rearrange("p (u t) -> p u t", u=12)
        gmat = ar_a[:, 4608:5376].rearrange("p (u t) -> p u t", u=6)
        e_at2 = [ar_a[:, at:at + 1536].rearrange("p (i k) -> p i k", i=4) for at in (0, 3840)]
        w_at = ar_a[:, 1536:2304].rearrange("p (i k) -> p i k", i=2)
        wt_at = ar_a[:, 2304:3072].rearrange("p (i k) -> p i k", i=2)
        o_at = ar_a[:, 3072:3840].rearrange("p (j t) -> p j t", j=2)
        sq_at = ar_a[:, 3840:5376].rearrange("p (c t) -> p c t", t=NT)
        rs_at = ar_a[:, 5376:6912].rearrange("p (c t) -> p c t", t=NT)
        three = lambda a, k: a[:, 1152 * k:1152 * (k + 1)].rearrange("p (j t) -> p j t", t=NT)
        sig, aa, dd, dx, en, ep = (three(ar_a, k) for k in range(6))
        kkn, kxa = three(h_t, 0), three(h_t, 1)
        unit = lambda a, k: a[:, 1536 * k:1536 * (k + 1)].rearrange("p (g i t) -> p g i t", g=4, i=3)
        m_lt, m_l2, m_m1, m_m2, m_nw = (unit(ar_a, k) for k in range(5))
        m_x, m_xt = unit(h_t, 0), unit(h_t, 1)
        rhs_b = h_t[:, 0:768].rearrange("p (g i v) -> p g i v", g=4, i=3)
        nu_b = h_t[:, 768:1536].rearrange("p (g i v) -> p g i v", g=4, i=3)
        lg_rows = ar_b[0:20, 2304:2688]
        sq2 = ar_b[:, 0:3072].rearrange("p (c t) -> p c t", t=NT)
        gates = ar_a[:, 0:EXPERTS * NT].rearrange("p (e t) -> p e t", t=NT)
        loc = h_t[:, 0:1152].rearrange("p (t d i v) -> p t d i v", t=3, d=2, i=3)
        sin = h_t[:, 1152:2304].rearrange("p (t d i v) -> p t d i v", t=3, d=2, i=3)
        xwt = h_t[:, 2304:3072].rearrange("p (g d i v) -> p g d i v", g=2, d=2, i=3)
        xbcp = ar_b[:, 0:1960].rearrange("p (c t) -> p c t", t=392)
        conv = ar_b[:, 1960:3900].rearrange("p (c t) -> p c t", t=CONVW)
        zz = ar_b[:, 3900:5052].rearrange("p (c t) -> p c t", t=NT)
        tok = ar_b[:, 5052:6588].rearrange("p (t n) -> p t n", t=TT)
        qk = ar_b[:, 6588:8124].rearrange("p (c t) -> p c t", t=NT)
        vat = ar_b[:, 8124:8892].rearrange("p (t n) -> p t n", t=TT)
        f_al, f_rho, f_be, f_ka = ([three(ar_b, 4 * d + k) for d in range(2)] for k in range(4))
        hid_hi = ar_br[:, 0:768].rearrange("p (m t) -> p m t", m=2)
        hid_lo = ar_br[:, 768:1536].rearrange("p (m t) -> p m t", m=2)
        sh = ar_b[:, 1536:2304].rearrange("p (m t) -> p m t", m=2)
        th = ar_b[:, 2304:3072].rearrange("p (m t) -> p m t", m=2)
        h_hi = ar_br[:, 3072:6144].rearrange("p (c t) -> p c t", t=NT)
        h_lo = h_r[:, :].rearrange("p (c t) -> p c t", t=NT)
        w_hi = [[y_r[:, 0:1024], y_r[:, 1024:2048]], [rkv_r[:, 0:1024], rkv_r[:, 1024:2048]],
                [y_r[:, 2048:3072], rkv_r[:, 2048:3072]]]
        w_lo = lambda k: ring_r[:, (k % RING) * SLOT:(k % RING + 1) * SLOT]
        ytok = ar_a[:, 0:TT * D].rearrange("p (t d) -> p t d", t=TT)
        hin_hi = ar_ar[:, 0:3072].rearrange("p (c t) -> p c t", t=NT)
        hin_lo = ar_ar[:, 3072:6144].rearrange("p (c t) -> p c t", t=NT)
        w_in_hi = [[ar_ar[:, 6144:7168], y_r[:, 0:1024]], [y_r[:, 1024:2048], y_r[:, 2048:3072]]]

        def in_width(n):
            parts = IN_SLOTS[n]
            return 256 if len(parts) == 2 or parts[0][0] == "va" else 128

        def in_parts(n):
            k, w = IN_SLOT0 + n, in_width(n)
            tiles = lambda ap: ap.rearrange("p (c n) -> p c n", c=KD)
            return ([tiles(x)[:, 4 * hf:4 * hf + 4, 0:w] for hf in range(2)] if x is not None else
                    [a[:, 0:4 * w].rearrange("p (c n) -> p c n", c=4) for a in w_in_hi[n % 2]] for x in (slot(k), None, w_lo(k)))

        sq8 = y_t[:, :].rearrange("p (c t) -> p c t", t=NT)
        dts = sml[:, 0:36].rearrange("p (t u) -> p t u", t=3)
        dta = sml[:, 36:72].rearrange("p (t u) -> p t u", t=3)
        csc = sml[:, 72:144].rearrange("p (w t u) -> p w t u", w=2, t=3)
        wst = sml[:, 144:180].rearrange("p (t u) -> p t u", t=3)
        dec = sml[:, 180:216].rearrange("p (t u) -> p t u", t=3)
        dec2 = sml[:, 216:234].rearrange("p (t d i) -> p t d i", t=3, d=2)
        avl = sml[:, 234:246]
        dcol = sml[:, 246:249]
        lam = sml[:, 249:260]
        s3 = lambda at, n: sml[:, at:at + 3 * n].rearrange("p (t u) -> p t u", t=3)
        nmx2, ssm2 = (sml[:, 260:264], sml[:, 313:317]), (sml[:, 264:268], sml[:, 317:321])
        mref = sml[:, 268:277]
        pre = [sml[:, 277 + 9 * d:286 + 9 * d].rearrange("p (j t) -> p j t", j=3) for d in range(2)]
        fin = [sml[:, 295 + 9 * d:304 + 9 * d].rearrange("p (j t) -> p j t", j=3) for d in range(2)]
        lg, rg1, rg2, rg3 = s3(0, 20), s3(60, 4), s3(72, 4), s3(84, 16)
        rg4, rg5, rg6 = s3(132, 4), s3(144, 4), s3(156, 4)
        r1, r2, r3, r4, r5 = (s3(168 + 3 * k, 1) for k in range(5))
        gate = s3(190, 16)

        names = ("bank_full emptied_v emptied_a v_chain a_chain par_in bc_in init_in wsmall_in stats_sq mod_ready "
                 "h_part h_ready x_ready conv_raw conv_in conv_done dt_pre dt_sp dt_one cs_pre cs_exp xw_ready s_ready "
                 "csr_read ec_ready d_ready e_ready cd_ready g_ready ssd_y yssd_sq stage_ssd stage_rwkv stage_kv "
                 "lam_pre lam_exp qk_sq qk_rs qk_ready sc_max sc_exp w_ready o_ready att_done kk_sq kk_max kk_rs "
                 "lora_ready decay_pre decay_exp f_ready nw_ready x1_ready s0_ready rwkv_y bon_in gn_c gn_rs y_ready "
                 "x2_ready h2_part h2_ready rt_pre rt_exp gate_ready moe_y moe_tok out_free xin_in rwkv_st zx s_moe "
                 "t_moe t2_moe hp_moe hi_moe lo_moe hhi_moe hlo_moe hc_ready hc2_ready kx_ready rho_ready hhi_in hlo_in hi_in lo_in mask_in mask_done hid_moe tok_done sn_rs on_rs passed").split()
        S = {n: ctx.enter_context(nc.semaphore(n)) for n in names}
        cleared = [S[n] for n in names if n not in ("par_in", "bc_in", "init_in", "wsmall_in", "xin_in")]
        ring_full = [ctx.enter_context(nc.semaphore(f"ring_full{i}")) for i in range(RING)]
        ring_free = ctx.enter_context(nc.semaphore("ring_free"))
        engine_done = ctx.enter_context(nc.semaphore("engine_done"))
        sp_passed = ctx.enter_context(nc.semaphore("sp_passed"))
        go_on = ctx.enter_context(nc.semaphore("go_on"))
        gone_on = ctx.enter_context(nc.semaphore("gone_on"))
        cst_in = ctx.enter_context(nc.semaphore("cst_in"))
        cst_rest = ctx.enter_context(nc.semaphore("cst_rest"))
        stored = ctx.enter_context(nc.semaphore("stored"))

        table, totals = job_table(job_order())
        pre_table, _ = job_table(PRE)
        post_table, _ = job_table(POST)
        bank = lambda job: ps[:, job.n % 8, :]

        def meet(eng, i):
            eng.sem_inc(engine_done, 1)
            eng.wait_ge(go_on, i + 1)
            eng.sem_inc(gone_on, 1)

        def counter():
            return {}

        def step(eng, counts, ins, name):
            counts[name] = counts.get(name, 0) + 1
            ins.then_inc(S[name], 1)
            eng.wait_ge(S[name], counts[name])

        block = ctx.enter_context(nc.Block())

        @block.sync
        def _(sp):
            sp.dma_start(xin[:, 0, :], A["x_prompt"].rearrange("b t d -> (b t) d")).then_inc(S["xin_in"], 16)
            sp.dma_start(stg[0:8, 0:P], A["c"].rearrange("b (c p) -> (b c) p", p=P)).then_inc(S["xin_in"], 16)
            sp.dma_start(stg[8:16, 0:P], A["c_ctx"].rearrange("(c p) -> c p", p=P)).then_inc(S["xin_in"], 16)
            sp.dma_start(cst[:, 0:P], consts_d[:, 0:P]).then_inc(cst_in, 16)
            sp.dma_start(xin[:, 1:3, :], A["x_sample"].rearrange("b (t p) d -> p (b t) d", p=P)).then_inc(S["xin_in"], 16)
            with sp.Fori(0, DEPTH) as l:
                before = l * LAYER_SLOTS
                dl = lambda name: A[name][bass.ds(l, 1)]
                def small_inputs():
                    at = 0
                    srcs = [dl("ssd_conv_w").rearrange("a j (t p) -> (a j t) p", p=P), dl("ssd_conv_b").rearrange("a (t p) -> (a t) p", p=P),
                            dl("ssd_norm_g").rearrange("a (t p) -> (a t) p", p=P), dl("rwkv_w0").rearrange("a d (t p) -> (a d t) p", p=P),
                            dl("rwkv_a0").rearrange("a d (t p) -> (a d t) p", p=P), dl("rwkv_kk").rearrange("a (t p) -> (a t) p", p=P),
                            dl("rwkv_ka").rearrange("a (t p) -> (a t) p", p=P), dl("rwkv_rk").rearrange("a (t h) p -> (a t) (h p)", h=2),
                            dl("rwkv_ln_g").rearrange("a (t p) -> (a t) p", p=P), dl("rwkv_ln_b").rearrange("a (t p) -> (a t) p", p=P)]
                    for (name, n), src in zip(ROWS_A, srcs):
                        sp.dma_start(rows_a[at:at + n, :], src).then_inc(S["par_in"], 16)
                        at += n
                    for name, rep in (("att_qnorm_g", 4), ("att_knorm_g", 4), ("att_onorm_g", 2)):
                        for r in range(rep):
                            w = P // rep
                            sp.dma_start(rows_a[at:at + 1, r * w:r * w + w], dl(name)).then_inc(S["par_in"], 16)
                        at += 1
                    sp.dma_start(rows_b[0:48, :], dl("ada_b").rearrange("a (t p) -> (a t) p", p=P)).then_inc(S["par_in"], 16)
                    sp.dma_start(rows_b[48:56, :], dl("norm1_g").rearrange("a (t p) -> (a t) p", p=P)).then_inc(S["par_in"], 16)
                    sp.dma_start(rows_b[56:64, :], dl("norm2_g").rearrange("a (t p) -> (a t) p", p=P)).then_inc(S["par_in"], 16)
                    for d in range(2):
                        for gg in range(2):
                            sp.dma_start(ini[:, d, :, gg, :], A["state_ssd"][0, bass.ds(l, 1), d, 3 * gg:3 * gg + 3].rearrange("a i p n -> p (a i) n")).then_inc(S["init_in"], 16)
                    sp.dma_start(inr, A["state_rwkv"][0, bass.ds(l, 1)].rearrange("a d h p n -> p (a d h) n")).then_inc(S["init_in"], 16)
                    sp.dma_start(ck, A["cache_attn_k"][0, bass.ds(l, 1)].rearrange("a t h m k -> (a t) (h m k)")).then_inc(S["init_in"], 16)
                    sp.dma_start(cv[:, :], A["cache_attn_v"][0, bass.ds(l, 1)].rearrange("a t h k -> (a t) (h k)")).then_inc(S["init_in"], 16)
                    for name, w, src in (("dt_bias", 12, dl("ssd_dt_bias").rearrange("a d h -> (a d h)")),
                                         ("a_log", 12, dl("ssd_a_log").rearrange("a d h -> (a d h)")),
                                         ("d", 6, dl("ssd_d").rearrange("a h -> (a h)")),
                                         ("rbias", 4, dl("moe_bg").rearrange("a h -> (a h)")),
                                         ("be", 16, dl("moe_be").rearrange("a h -> (a h)")),
                                         ("lam", 128, dl("att_lambda").rearrange("a d h -> (a d h)")),
                                         ("lami", 2, lconst_d[bass.ds(l, 1)].rearrange("a h -> (a h)"))):
                        c0 = BC["rbias"] + 4 if name == "be" else BC[name]
                        sp.dma_start(bcr[:, c0:c0 + w], src.partition_broadcast(P)).then_inc(S["bc_in"], 16)
                    with nc.allow_non_contiguous_dma(reason="narrow weight columns"):
                        sp.dma_start(wdt, dl("w_in").rearrange("a (c p) n -> p (a c) n", p=P)[:, :, COL["dt"]:COL["dt"] + 12]).then_inc(S["wsmall_in"], 16)
                        sp.dma_start(wrt[:, :, 0:4], dl("moe_wg").rearrange("a (c p) n -> p (a c) n", p=P)).then_inc(S["wsmall_in"], 16)
                        sp.dma_start(wrt[:, :, 4:20], dl("moe_we").rearrange("a (c p) n -> p (a c) n", p=P)).then_inc(S["wsmall_in"], 16)

                for k in range(PRE_SLOTS):
                    if k == 2:
                        small_inputs()
                    sp.wait_ge(ring_free, before + (k + 1))
                    sp.sem_inc(sp_passed, 1)
                    full = ring_full[k % RING]
                    if k < ADA_FIRST or ADA_SLOT0 <= k < LORA_SLOT:
                        n = k if k < ADA_FIRST else k - ADA_SLOT0 + ADA_FIRST
                        sp.dma_start(slot8(k), dl("ada_w").rearrange("a (c p) n -> p (a c) n", p=P)[:, :, 256 * n:256 * n + 256]).then_inc(full, 16)
                    elif k < ADA_SLOT0:
                        parts = IN_SLOTS[k - IN_SLOT0]
                        c0, w = parts[0][1], in_width(k - IN_SLOT0)
                        sp.dma_start(slot8(k)[:, :, 0:w], dl("w_in").rearrange("a (c p) n -> p (a c) n", p=P)[:, :, c0:c0 + w]).then_inc(full, 16)
                    elif k == LORA_SLOT:
                        for name, lo, hi in (("rwkv_w2", 0, 64), ("rwkv_a2", 64, 128)):
                            sp.dma_start(slot(k)[lo:hi, 0:768].rearrange("p (d n) -> p d n", d=2),
                                         dl(name).rearrange("a d p n -> p (a d) n")).then_inc(full, 16)
                        sp.dma_start(slot(k)[:, 768:1152], dl("rwkv_g2").rearrange("a p n -> p (a n)")).then_inc(full, 16)
                    else:
                        m = k - OUT_SLOT
                        sp.dma_start(slot2(k), dl("w_out").rearrange("a (c p) n -> p (a c) n", p=P)[:, 2 * m:2 * m + 2, :]).then_inc(full, 16)
                with sp.Fori(0, EXPERTS // 2) as j:
                    for e in range(2):
                        for i, name in enumerate(("moe_w1", "moe_w3", "moe_w2")):
                            k = PRE_SLOTS + 3 * e + i
                            src = A[name].rearrange("l e a b -> (l e) a b")[bass.ds(l * EXPERTS + j * 2 + e, 1)]
                            sp.wait_ge(ring_free, before + j * 6 + (k + 1))
                            sp.dma_start(slot8(k) if i < 2 else slot2(k), src.rearrange("a (c p) n -> p (a c) n", p=P)).then_inc(ring_full[k % RING], 16)

        EXTRA = 32

        def ring_value(k):
            v = 16 * (k // RING + 1)
            if k % RING == LORA_SLOT % RING and k >= LORA_SLOT:
                v += EXTRA
            return v

        def lring(l, i):
            return l * (16 * (LAYER_SLOTS // RING) + (EXTRA if i == LORA_SLOT % RING else 0))

        @block.gpsimd
        def _(g):
            def clear(i):
                g.wait_ge(engine_done, i * 3 + 3)
                g.sem_inc(gone_on, 1)
                for s in cleared:
                    g.sem_clear(s)
                g.sem_inc(go_on, 1)

            def mask_step(s):
                for g4 in range(4):
                    up = g4 < 2
                    for n, (dst, mk) in enumerate(((m_l2, C_US if up else C_LS), (m_m1, C_UI if up else C_LI), (m_m2, C_UI if up else C_LI))):
                        g.wait_ge(S["mask_in"], 12 * s + 3 * g4 + n + 1)
                        g.tensor_tensor(dst[:, g4], dst[:, g4], cc(mk).unsqueeze(1).to_broadcast([P, 3, P]), ALU.mult).then_inc(S["mask_done"], 1)

            g.memset(zer[:, :], 0.0).then_inc(S["zx"], 1)
            g.wait_ge(S["zx"], 1)
            clear(0)
            with g.Fori(0, DEPTH) as l:
                g.wait_ge(S["stage_ssd"], 2)
                so = stg[0:64, 0:768].rearrange("p (d i g n) -> p d i g n", d=2, i=3, g=2)
                for d in range(2):
                    for gg in range(2):
                        g.dma_start(O[4][0, bass.ds(l, 1), d, 3 * gg:3 * gg + 3].rearrange("a i p n -> p (a i) n"), so[:, d, :, gg, :]).then_inc(stored, 16)
                g.wait_ge(S["stage_kv"], 1)
                g.dma_start(O[2][0, bass.ds(l, 1)].rearrange("a t h m k -> (a t) (h m k)"), stg[:, 768:1024]).then_inc(stored, 16)
                g.dma_start(O[3][0, bass.ds(l, 1)].rearrange("a t h k -> (a t) (h k)"), vat[:, 0, :]).then_inc(stored, 16)
                g.wait_ge(stored, l * 128 + 96)
                g.sem_inc(S["out_free"], 1)
                for d in range(2):
                    g.wait_ge(S["decay_exp"], 4 * d + 4)
                    g.tensor_tensor(f_rho[d][:, :, :], rkv[:, 0:3, :], en[:, :, :], ALU.mult).then_inc(S["rho_ready"], 1)
                mask_step(0)
                g.wait_ge(S["stage_rwkv"], 2)
                ro = stg[0:64, 0:768].rearrange("p (u n) -> p u n", u=12)
                for d in range(2):
                    g.dma_start(O[5][0, bass.ds(l, 1), d].rearrange("a i p n -> p (a i) n"), ro[:, 6 * d:6 * d + 6, :]).then_inc(stored, 16)
                mask_step(1)
                mask_step(2)
                g.wait_ge(stored, l * 128 + 128)
                clear(l + 1)
            for t in range(TT):
                g.wait_ge(S["tok_done"], 2 * t + 2)
                dst = O[0][0] if t == 0 else O[1][0, 128 * (t - 1):128 * t]
                g.dma_start(dst, xin[:, t, :]).then_inc(stored, 16)
            g.wait_ge(stored, DEPTH * 128 + 48)

        @block.tensor
        def _(pe):
            tb = [pre_table]

            def claim(name):
                job = tb[0][name]
                if job.before is not None:
                    pe.wait_ge(S["emptied_" + job.before.by], job.before.count)
                return bank(job)

            def mm(out, lhsT, rhs, start=True, stop=True):
                return pe.matmul(out, lhsT, rhs, start=start, stop=stop)

            def mm3(out, lhi, llo, rhi, rlo, start, stop):
                pe.matmul(out, lhi, rhi, start=start, stop=False)
                pe.matmul(out, lhi, rlo, start=False, stop=False)
                return pe.matmul(out, llo, rhi, start=False, stop=stop)

            def full(ins):
                ins.then_inc(S["bank_full"], 1)

            def tr(out, in_, n=P):
                return pe.transpose(out, in_, ident[0:n, 0:n])

            pe.sem_inc(ring_free, RING)
            pe.wait_ge(cst_in, 16)
            pe.wait_ge(S["xin_in"], 64)
            for c in range(KD):
                b = claim(f"x{c}")
                for t in range(TT):
                    i = tr(b[:, P * t:P * t + P], xin[:, t, P * c:P * c + P])
                full(i)
            b = claim("cond")
            full(tr(b[:, 0:16], stg[0:16, 0:P], 16))
            pe.wait_ge(cst_rest, 16)
            meet(pe, 0)
            tb[0] = table

            with pe.Fori(0, DEPTH) as l:
                def arrived(k):
                    pe.wait_ge(ring_full[k % RING], lring(l, k % RING) + ring_value(k))

                def used(ins):
                    ins.then_inc(ring_free, 1)

                def ada_rows(q):
                    b = claim(f"ar{q}")
                    for half in range(2):
                        k = 2 * q + half + (0 if q < ADA_EARLY else N_INS)
                        arrived(k)
                        for c in range(KD):
                            i = mm(b[0:2, 256 * half:256 * half + 256], scond[:, c, :], slot8(k)[:, c, :], c == 0, c == KD - 1)
                        if half == 0:
                            used(i)
                    full(i)
                    pe.wait_ge(S["bank_full"], table[f"ar{q}"].n + 1)
                    pe.sem_inc(ring_free, 1)

                def ada_turn(q, b, at):
                    pe.wait_ge(S["emptied_a"], table[f"ar{q}"].count)
                    for m in range(4):
                        i = tr(b[:, at + 2 * m:at + 2 * m + 2], ada_row(q)[:, P * m:P * m + P], 2)
                    return i

                def ada(q):
                    if q > ADA_EARLY:
                        full(ada_turn(q - 1, claim(f"at{q - 1}"), 0))
                    if q < ADA_GROUPS:
                        ada_rows(q)

                for q in range(ADA_EARLY):
                    ada_rows(q)
                b = claim("sum1")
                for c in range(KD):
                    pe.wait_ge(S["stats_sq"], c + 1)
                    i = mm(b[:, 0:NT], ones, sq8[:, c, :], c == 0, c == KD - 1)
                full(i)
                pe.wait_ge(S["par_in"], l * (16 * 23) + 16 * 23)
                pe.sem_inc(S["passed"], 1)
                b = claim("prmA")
                full(tr(b[:, 0:NA], rows_a, NA))
                b = claim("prmB")
                full(tr(b[:, 0:NB], rows_b, NB))
                pe.wait_ge(S["init_in"], l * (16 * 7) + 16 * 7)
                pe.sem_inc(S["passed"], 1)
                b = claim("sst")
                for d in range(2):
                    for i in range(3):
                        src = ini[:, d, i].rearrange("p g n -> p (g n)")
                        o = tr(b[:, 64 * (3 * d + i):64 * (3 * d + i) + 64], src, 64)
                full(o)
                b = claim("rst")
                for d in range(2):
                    for j in range(3):
                        o = tr(b[:, 64 * (3 * d + j):64 * (3 * d + j) + 64], inr[:, 6 * d + 2 * j:6 * d + 2 * j + 2, :].rearrange("p u n -> p (u n)"), 64)
                full(o)
                b = claim("kct")
                for j in range(2):
                    o = tr(b[:, P * j:P * j + P], ck[:, P * j:P * j + P])
                full(o)
                b = claim("ada")
                for q in range(ADA_EARLY):
                    i = ada_turn(q, b, 8 * q)
                full(i)
                pe.wait_ge(S["h_ready"], KD)
                pe.wait_ge(S["hc_ready"], KD)
                pe.wait_ge(S["wsmall_in"], l * 48 + 48)
                pe.sem_inc(S["passed"], 1)
                b = claim("dt")
                for t in range(TT):
                    for c in range(KD):
                        i = mm(b[:, 12 * t:12 * t + 12], hv[:, c, P * t:P * t + P], wdt[:, c, :], c == 0, c == KD - 1)
                full(i)
                for n, parts in enumerate(IN_SLOTS):
                    if n == 0:
                        pe.wait_ge(S["hlo_in"], 1)
                    pe.wait_ge(S["lo_in"], 2 * n + 2)
                    _, whi, wlo = in_parts(n)
                    if parts[0][0] == "va":
                        for half, ts in ((0, (0, 1)), (1, (2,))):
                            b = claim(f"va{half}")
                            for o, t in enumerate(ts):
                                for c in range(KD):
                                    i = mm3(b[:, 256 * o:256 * o + 256], hin_hi[:, c, P * t:P * t + P], hin_lo[:, c, P * t:P * t + P],
                                            whi[c // 4][:, c % 4, :], wlo[c // 4][:, c % 4, :], c == 0, c == KD - 1)
                            if half == 0:
                                full(i)
                    else:
                        for o, (name, _) in enumerate(parts):
                            b = claim(name)
                            for c in range(KD):
                                i = mm3(b[:, 0:NT], whi[c // 4][:, c % 4, P * o:P * o + P], wlo[c // 4][:, c % 4, P * o:P * o + P],
                                        hin_hi[:, c, :], hin_lo[:, c, :], c == 0, c == KD - 1)
                            if o < len(parts) - 1:
                                full(i)
                    full(i)
                    pe.wait_ge(S["bank_full"], table[parts[-1][0] if parts[0][0] != "va" else "va1"].n + 1)
                    pe.sem_inc(ring_free, 1)

                pe.wait_ge(S["dt_one"], 1)
                b = claim("cs")
                for d, tri in ((0, C_UI), (1, C_LI)):
                    for t in range(TT):
                        mm(b[:, 12 * t + 6 * d:12 * t + 6 * d + 6], cc(tri), dta[:, t, 6 * d:6 * d + 6])
                full(mm(b[:, 36:72], ones, sml[:, 36:72]))
                ada(4)
                for t in range(TT):
                    if t == 0:
                        pe.wait_ge(S["conv_done"], 5)
                    b = claim(f"xtr{t}")
                    for c in range(4):
                        i = tr(b[:, P * c:P * c + P], conv[:, c, TOF[t]:TOF[t] + P])
                    full(i)
                ada(5)
                for t in range(TT):
                    pe.wait_ge(S["xw_ready"], 4 * t + 4)
                    b = claim(f"lst{t}")
                    for gg in range(2):
                        i = mm(b[64 * gg:64 * gg + 64, 0:384], tok[:, t, 384 + 64 * gg:448 + 64 * gg], xwt[:, gg].rearrange("p d i v -> p (d i v)"))
                    full(i)
                for t in range(TT):
                    for q in range(3):
                        b = claim(f"csr{t}{q}")
                        for o in range(4):
                            u = 4 * q + o
                            i = mm(b[:, P * o:P * o + P], dta[:, t, u:u + 1].to_broadcast([P, P]), cc(C_UI if u < 6 else C_LI))
                        full(i)
                    for gg in range(2):
                        b = claim(f"cb{t}{gg}")
                        r = slice(64 * gg, 64 * gg + 64)
                        full(mm(b[:, 0:P], conv[r, 3, TOF[t]:TOF[t] + P], conv[r, 4, TOF[t]:TOF[t] + P]))
                    ada(6 + t)
                    pe.wait_ge(S["g_ready"], t + 1)
                    if t == 0:
                        pe.wait_ge(S["s_ready"], 1)
                    for gg in range(2):
                        b = claim(f"y{'ab'[gg]}{t}")
                        r = slice(64 * gg, 64 * gg + 64)
                        for hh in range(3):
                            h = 3 * gg + hh
                            o = b[64 * (h % 2):64 * (h % 2) + 64, P * (h // 2):P * (h // 2) + P]
                            mm(o, tok[:, t, 64 * h:64 * h + 64], gmat[:, h, :], True, False)
                            for d in range(2):
                                i = mm(o, sin[r, t, d, hh, :], cdec[r, 6 * d + h, :], False, d == 1)
                        full(i)
                for d in range(2):
                    b = claim(f"sfin{d}")
                    for i in range(3):
                        o = tr(b[0:64, P * i:P * i + P], loc[:, 0, d, i, :])
                    full(o)
                ada(9)
                b = claim("sn")
                for j in range(NJ):
                    pe.wait_ge(S["yssd_sq"], j + 1)
                    i = mm(b[:, 0:NT], ones, rs_at[:, j, :], j == 0, j == NJ - 1)
                full(i)

                pe.wait_ge(S["qk_sq"], 1)
                for c in range(4):
                    b = claim(f"qn{c}")
                    full(mm(b[:, 0:NT], cc(C_B32), sq_at[:, c, :]))
                pe.wait_ge(S["qk_rs"], 4)
                b = claim("kout")
                for j in range(2):
                    i = tr(b[:, P * j:P * j + P], qk[:, 2 + j, 0:P])
                full(i)
                for q in range(2):
                    b = claim(f"rot{q}")
                    for o in range(2):
                        i = mm(b[:, 256 * o:256 * o + 256], cc(C_ROT), qk[:, 2 * q + o, P:NT])
                    full(i)
                pe.wait_ge(S["qk_ready"], 2)
                def scores(t, j):
                    for i4 in range(4):
                        b = claim(f"sc{t}{j}{i4}")
                        r = slice(32 * i4, 32 * i4 + 32)
                        q = qk[r, j, P * t:P * t + P]
                        if t == 0:
                            i = pe.matmul(b[:, 0:P], q, qk[r, 2 + j, 0:P], start=True, stop=True, tile_position=(32 * i4, 0))
                        else:
                            pe.matmul(b[:, 0:P], q, kct[r, j, :], start=True, stop=True, tile_position=(32 * i4, 0))
                            i = pe.matmul(b[:, P:NT], q, qk[r, 2 + j, P:NT], start=True, stop=True, tile_position=(32 * i4, 0))
                        full(i)

                def weighted_values(t, j):
                    nb = 1 if t == 0 else 3
                    for hh in range(2):
                        pe.wait_ge(S["w_ready"], 4 * t + 2 * j + hh + 1)
                        b = claim(f"wt{t}{j}{hh}")
                        for kb in range(nb):
                            i = tr(b[:, P * kb:P * kb + P], w_at[:, hh, P * kb:P * kb + P])
                        full(i)
                    b = claim(f"pv{t}{j}")
                    for hh in range(2):
                        pe.wait_ge(S["emptied_a"], table[f"wt{t}{j}{hh}"].count)
                        h = 2 * j + hh
                        for kb in range(nb):
                            if t == 0:
                                v = vat[:, 0, 64 * h:64 * h + 64]
                            else:
                                v = cv[:, 64 * h:64 * h + 64] if kb == 0 else vat[:, kb, 64 * h:64 * h + 64]
                            i = mm(b[64 * hh:64 * hh + 64, 0:P], v, wt_at[:, hh, P * kb:P * kb + P], kb == 0, kb == nb - 1)
                    full(i)

                scores(0, 0)
                for u in range(2 * TT):
                    if u + 1 < 2 * TT:
                        scores((u + 1) // 2, (u + 1) % 2)
                    weighted_values(u // 2, u % 2)
                for j in range(2):
                    pe.wait_ge(S["o_ready"], j + 1)
                    b = claim(f"on{j}")
                    full(mm(b[:, 0:NT], cc(C_B64), sq_at[:, j, :]))

                pe.wait_ge(S["kk_sq"], 1)
                for j in range(NJ):
                    b = claim(f"kn{j}")
                    full(mm(b[:, 0:NT], cc(C_B64), en[:, j, :]))
                arrived(LORA_SLOT)
                for d in range(2):
                    for j in range(NJ):
                        lo = slot(LORA_SLOT)[:, 0:768].rearrange("p (d n) -> p d n", d=2)
                        b = claim(f"lw{d}{j}")
                        full(mm(b[:, 0:NT], lo[0:64, d, P * j:P * j + P], xwa[0:64, :]))
                        b = claim(f"la{d}{j}")
                        full(mm(b[:, 0:NT], lo[64:128, d, P * j:P * j + P], xwa[64:128, :]))
                    ada(10 + d)
                for t in range(TT):
                    b = claim(f"vt{t}")
                    for j in range(NJ):
                        i = tr(b[:, P * j:P * j + P], rkv[:, 6 + j, P * t:P * t + P])
                    full(i)
                ada(12)
                for s in range(3):
                    for d in range(2):
                        t = TILE_OF[d][s]
                        c = slice(P * t, P * t + P)
                        if s == 0:
                            pe.wait_ge(S["f_ready"], 2)
                            pe.wait_ge(S["rho_ready"], 2)
                        for w, f in ((0, f_be), (1, f_ka)):
                            b = claim(f"{'bk'[w]}t{s}{d}")
                            for j in range(NJ):
                                i = tr(b[:, P * j:P * j + P], f[d][:, j, c])
                            full(i)
                    for g4 in range(4):
                        d, par_ = g4 // 2, g4 % 2
                        t = TILE_OF[d][s]
                        c = slice(P * t, P * t + P)
                        r = slice(64 * par_, 64 * par_ + 64)
                        for name, lh, rh in (("L1", f_al, f_be), ("LT", f_be, f_al), ("L2", f_ka, f_al), ("M1", f_be, f_rho), ("M2", f_ka, f_rho)):
                            b = claim(f"{name}{s}{g4}")
                            for j in range(NJ):
                                i = mm(b[:, P * j:P * j + P], lh[d][r, j, c], rh[d][r, j, c])
                            full(i)
                    for lv in range(1, 7):
                        for g4 in range(4):
                            if lv == 1:
                                pe.wait_ge(S["x1_ready"], 2 * (4 * s + g4) + 2)
                            else:
                                pe.wait_ge(S["emptied_a"], table[f"T{s}{lv - 1}{g4}"].count)
                            b = claim(f"W{s}{lv}{g4}")
                            for j in range(NJ):
                                i = mm(b[:, P * j:P * j + P], m_lt[:, g4, j, :], m_x[:, g4, j, :])
                            full(i)
                        for g4 in range(4):
                            pe.wait_ge(S["nw_ready"], 24 * s + 4 * (lv - 1) + g4 + 1)
                            if lv < 6:
                                b = claim(f"X{s}{lv}{g4}")
                                for j in range(NJ):
                                    i = mm(b[:, P * j:P * j + P], m_xt[:, g4, j, :], m_nw[:, g4, j, :])
                                full(i)
                            b = claim(f"T{s}{lv}{g4}")
                            for j in range(NJ):
                                i = mm(b[:, P * j:P * j + P], m_nw[:, g4, j, :], m_xt[:, g4, j, :])
                            full(i)
                    pe.wait_ge(S["s0_ready"], 2 * s + 2)
                    if s == 0:
                        pe.wait_ge(S["emptied_a"], table["vt2"].count)
                    pe.wait_ge(S["mask_done"], 12 * s + 12)
                    for g4 in range(4):
                        d, par_ = g4 // 2, g4 % 2
                        t = TILE_OF[d][s]
                        c = slice(P * t, P * t + P)
                        r = slice(64 * par_, 64 * par_ + 64)
                        b = claim(f"rh{s}{g4}")
                        for j in range(NJ):
                            h = 2 * j + par_
                            mm(b[:, 64 * j:64 * j + 64], f_al[d][r, j, c], srk[r, d, j, :], True, False)
                            i = mm(b[:, 64 * j:64 * j + 64], m_l2[:, g4, j, :], vtok[:, t, 64 * h:64 * h + 64], False, True)
                        full(i)
                    pe.wait_ge(S["emptied_a"], table[f"T{s}63"].count)
                    for g4 in range(4):
                        pe.wait_ge(S["emptied_v"], table[f"rh{s}{g4}"].count)
                        b = claim(f"u{s}{g4}")
                        for j in range(NJ):
                            i = mm(b[:, 64 * j:64 * j + 64], m_xt[:, g4, j, :], rhs_b[:, g4, j, :])
                        full(i)
                    for d in range(2):
                        pe.wait_ge(S["emptied_v"], table[f"u{s}{2 * d + 1}"].count)
                        t = TILE_OF[d][s]
                        c = slice(P * t, P * t + P)
                        b = claim(f"ry{s}{d}")
                        for par_ in range(2):
                            r = slice(64 * par_, 64 * par_ + 64)
                            for j in range(NJ):
                                h = 2 * j + par_
                                o = b[r, P * j:P * j + P]
                                mm(o, srk[r, d, j, :], f_rho[d][r, j, c], True, False)
                                mm(o, vtok[:, t, 64 * h:64 * h + 64], m_m2[:, 2 * d + par_, j, :], False, False)
                                i = mm(o, nu_b[:, 2 * d + par_, j, :], m_m1[:, 2 * d + par_, j, :], False, True)
                        full(i)
                    for d in range(2):
                        t = TILE_OF[d][s]
                        pe.wait_ge(S["emptied_a"], table[f"kt{s}{d}"].count)
                        b = claim(f"rs{s}{d}")
                        for par_ in range(2):
                            for j in range(NJ):
                                h = 2 * j + par_
                                o = b[64 * par_:64 * par_ + 64, 64 * j:64 * j + 64]
                                mm(o, bktok[:, d, 1, 64 * h:64 * h + 64], vtok[:, t, 64 * h:64 * h + 64], True, False)
                                i = mm(o, bktok[:, d, 0, 64 * h:64 * h + 64], nu_b[:, 2 * d + par_, j, :], False, True)
                        full(i)
                    if s == 0:
                        for d in range(2):
                            pe.wait_ge(S["rwkv_st"], d + 1)
                            b = claim(f"rfin{d}")
                            for j in range(NJ):
                                i = tr(b[0:64, P * j:P * j + P], sri[:, d, j, :])
                            full(i)
                pe.wait_ge(S["rwkv_y"], 1)
                for j in range(NJ):
                    b = claim(f"mu{j}")
                    full(mm(b[:, 0:NT], cc(C_B64), yv[:, 3 + j, :]))
                for j in range(NJ):
                    pe.wait_ge(S["gn_c"], j + 1)
                    b = claim(f"var{j}")
                    full(mm(b[:, 0:NT], cc(C_B64), en[:, j, :]))
                for j in range(NJ):
                    pe.wait_ge(S["bon_in"], j + 1)
                    b = claim(f"bon{j}")
                    full(mm(b[:, 0:NT], cc(C_B64), ep[:, j, :]))
                for j in range(NJ):
                    b = claim(f"gt{j}")
                    full(mm(b[:, 0:NT], slot(LORA_SLOT)[:, 768 + P * j:768 + P * j + P], xg[:, :]))
                pe.wait_ge(S["bank_full"], table["gt2"].n + 1)
                pe.sem_inc(ring_free, 1)

                for q in range(4):
                    arrived(OUT_SLOT + q)
                pe.wait_ge(S["y_ready"], 3)
                pe.wait_ge(S["att_done"], 2)
                for m in range(KD):
                    b = claim(f"out{m}")
                    for c in range(KD):
                        i = mm(b[:, 0:NT], slot2(OUT_SLOT + c // 2)[:, c % 2, P * m:P * m + P], yv[:, c, :], c == 0, c == KD - 1)
                    full(i)
                pe.wait_ge(S["bank_full"], table[f"out{KD - 1}"].n + 1)
                pe.sem_inc(ring_free, 4)
                b = claim("sum2")
                for c in range(KD):
                    pe.wait_ge(S["x2_ready"], c + 1)
                    i = mm(b[:, 0:NT], ones, sq2[:, c, :], c == 0, c == KD - 1)
                full(i)
                b = claim("rtr")
                for c in range(KD):
                    pe.wait_ge(S["h2_ready"], c + 1)
                    pe.wait_ge(S["hc2_ready"], c + 1)
                    i = mm(b[0:20, 0:NT], wrt[:, c, :], hv[:, c, :], c == 0, c == KD - 1)
                full(i)
                pe.wait_ge(S["emptied_v"], table["rtr"].count)
                b = claim("rt")
                for t in range(TT):
                    i = tr(b[:, 20 * t:20 * t + 20], lg_rows[:, P * t:P * t + P], 20)
                full(i)
                pe.wait_ge(S["gate_ready"], 1)
                for e in range(EXPERTS):
                    b = claim(f"gb{e}")
                    for t in range(TT):
                        i = mm(b[:, P * t:P * t + P], gate[:, t, e:e + 1].to_broadcast([P, P]), ident)
                    full(i)
                pe.wait_ge(S["emptied_a"], table[f"gb{EXPERTS - 1}"].count)
                pe.wait_ge(S["hlo_moe"], 1)
                for q in range(6):
                    pe.matmul(ps[:, q, :], zer[:, 0:P], zer[:, :], start=True, stop=False, skip_group_check=True)
                with pe.Fori(0, EXPERTS // 2) as jj:
                    for e in range(2):
                        k = PRE_SLOTS + 3 * e
                        w = [w_lo(k + i3) for i3 in range(3)]
                        for m in range(2):
                            n = 2 * e + m
                            for i3, read in ((0, "s_moe"), (1, "t_moe")):
                                if m == 0:
                                    pe.wait_ge(S["lo_moe"], jj * 6 + (3 * e + i3 + 1))
                                pe.wait_ge(S[read], jj * 4 + (n + 1))
                                for c in range(KD):
                                    whi = w_hi[i3][c // 4][:, 256 * (c % 4) + P * m:256 * (c % 4) + P * m + P]
                                    wlo = w[i3][:, 256 * c + P * m:256 * c + P * m + P]
                                    i = mm3(ps[:, 6 + i3, 0:NT], whi, wlo, h_hi[:, c, :], h_lo[:, c, :], c == 0, c == KD - 1)
                                i.then_inc(S["hp_moe"], 1)
                        pe.wait_ge(S["hp_moe"], jj * 8 + (4 * e + 4))
                        pe.sem_inc(ring_free, 2)
                        pe.wait_ge(S["lo_moe"], jj * 6 + (3 * e + 3))
                        for m in range(2):
                            pe.wait_ge(S["t2_moe"], jj * 4 + (2 * e + m + 1))
                            for t in range(TT):
                                for hf in range(2):
                                    lh = [x[:, m, P * t:P * t + P] for x in (hid_hi, hid_lo)]
                                    rh = [w_hi[2][m][:, 512 * hf:512 * hf + 512], w[2][:, 1024 * m + 512 * hf:1024 * m + 512 * hf + 512]]
                                    for x, y in ((0, 0), (0, 1), (1, 0)):
                                        i = pe.matmul(ps[:, 2 * t + hf, :], lh[x], rh[y], start=False, stop=False, skip_group_check=True)
                        i.then_inc(ring_free, 1)
                for q in range(6):
                    i = pe.matmul(ps[:, q, :], zer[:, 0:P], zer[:, :], start=False, stop=True, skip_group_check=True)
                i.then_inc(S["moe_y"], 1)
                pe.wait_ge(S["moe_tok"], 6)
                for c in range(KD):
                    b = claim(f"ytr{c}")
                    for t in range(TT):
                        i = tr(b[:, P * t:P * t + P], ytok[:, t, P * c:P * c + P])
                    full(i)
                meet(pe, l + 1)
            tb[0] = post_table
            for t in range(TT):
                for hf in range(2):
                    b = claim(f"o{t}{hf}")
                    for c in range(4):
                        i = tr(b[:, P * c:P * c + P], x_t[:, 4 * hf + c, P * t:P * t + P])
                    full(i)

        @block.vector
        def _(v):
            cnt = counter()
            tb = [pre_table]

            def do(ins, name="v_chain"):
                step(v, cnt, ins, name)

            def filled(name):
                v.wait_ge(S["bank_full"], tb[0][name].n + 1)
                return bank(tb[0][name])

            def tell(name):
                cnt[name] = cnt.get(name, 0) + 1
                v.sem_inc(S[name], 1)

            TTT = v.tensor_tensor
            STT = v.scalar_tensor_tensor
            TS = v.tensor_scalar

            def bc3(ap, n, inner):
                return ap.unsqueeze(2).to_broadcast([P, n, inner])

            for c in range(KD):
                do(v.tensor_copy(x_t[:, c, :], filled(f"x{c}")[:, 0:NT]), "emptied_v")
            meet(v, 0)
            cnt.clear()
            tb[0] = table
            seg = ((1, 0, P), (0, P, NT))

            with v.Fori(0, DEPTH) as l:
                for c in range(KD):
                    do(TTT(sq8[:, c, :], x_t[:, c, :], x_t[:, c, :], ALU.mult), "stats_sq")
                b = filled("prmA")
                do(v.tensor_copy(par[:, 0:NA], b[:, 0:NA]), "emptied_v")
                b = filled("prmB")
                do(v.tensor_copy(par[:, NA:NA + NB], b[:, 0:NB]), "emptied_v")
                b = filled("sst")
                do(v.tensor_copy(bktok[:, 0, 0, :], b[:, 0:384]), "emptied_v")
                b = filled("rst")
                do(v.tensor_copy(sri[:, :, :, :].rearrange("p d j v -> p (d j v)"), b[:, 0:384]), "emptied_v")
                b = filled("kct")
                do(v.tensor_copy(kct[:, :, :].rearrange("p j t -> p (j t)"), b[:, 0:256]), "emptied_v")
                v.wait_ge(S["bc_in"], l * (16 * 7) + 16 * 7)
                lv_ = bcr[:, BC["lam"]:BC["lam"] + 128].rearrange("p (a b k) -> p a b k", a=2, b=2)
                tmp = rs[:, 0:64].rearrange("p (a k) -> p a k", a=2)
                do(TTT(tmp, lv_[:, :, 0, :], lv_[:, :, 1, :], ALU.mult))
                do(v.tensor_reduce(lam[:, 0:2], tmp, AXX, ALU.add), "lam_pre")
                def ada_add(name, m0, n):
                    b = filled(name)
                    ab = par[:, PAR["ada_b"] + m0:PAR["ada_b"] + m0 + n]
                    do(TTT(mod[:, m0:m0 + n, :], b[:, 0:2 * n].rearrange("p (m s) -> p m s", s=2), bc3(ab, n, 2), ALU.add), "emptied_v")

                def norm_gain(g0, sc, pn):
                    gn = bc3(par[:, PAR[pn]:PAR[pn] + 8], 8, 2)
                    do(STT(out=gs[:, g0:g0 + 8, :], in0=mod[:, sc:sc + 8, :], scalar=1.0, in1=gn, op0=ALU.add, op1=ALU.mult), "mod_ready")

                def ada_later(q):
                    ada_add(f"at{q}", 4 * q, 4)

                ada_add("ada", 0, 4 * ADA_EARLY)
                norm_gain(0, SC1, "n1")
                v.wait_ge(S["h_part"], 1)
                for c in range(KD):
                    do(TTT(hv[:, c, :], x_t[:, c, :], rs[:, :], ALU.mult), "x_ready")
                    do(TS(hv[:, c, 0:P], hv[:, c, 0:P], gs[:, c, 1:2], mod[:, SH1 + c, 1:2], ALU.mult, ALU.add), "hc_ready")
                v.wait_ge(S["hhi_in"], 1)
                do(TTT(hin_lo, hv, hin_hi, ALU.subtract), "hlo_in")

                def split_lo(n):
                    w, whi, wlo = in_parts(n)
                    for hf in range(2):
                        v.wait_ge(S["hi_in"], 2 * n + hf + 1)
                        do(TTT(wlo[hf], w[hf], whi[hf], ALU.subtract), "lo_in")

                split_lo(0)
                split_lo(1)
                v.wait_ge(S["lam_exp"], 2)
                do(TTT(lam[:, 4:5], lam[:, 2:3], lam[:, 3:4], ALU.subtract))
                do(TTT(lam[:, 4:5], lam[:, 4:5], bcr[:, BC["lami"]:BC["lami"] + 1], ALU.add))
                do(TTT(lam[:, 5:6], col("on"), bcr[:, BC["lami"] + 1:BC["lami"] + 2], ALU.mult))
                dd_ = bcr[:, BC["d"]:BC["d"] + 6].rearrange("p (j k) -> p j k", k=2)
                do(v.tensor_copy(dcol[0:64, :], dd_[0:64, :, 0]))
                do(v.tensor_copy(dcol[64:128, :], dd_[64:128, :, 1]))
                b = filled("dt")
                dtb = bcr[:, BC["dt_bias"]:BC["dt_bias"] + 12].unsqueeze(1).to_broadcast([P, 3, 12])
                do(TTT(dts[:, :, :], b[:, 0:36].rearrange("p (t u) -> p t u", t=3), dtb, ALU.add), "emptied_v")
                tell("dt_pre")
                v.wait_ge(S["dt_sp"], 3)
                do(STT(out=dts[:, :, :], in0=dts[:, :, :], scalar=0.0, in1=dta[:, :, :], op0=ALU.max, op1=ALU.add))
                avb = avl.unsqueeze(1).to_broadcast([P, 3, 12])
                do(STT(out=dta[:, :, :], in0=dts[:, :, :], scalar=-1.0, in1=avb, op0=ALU.mult, op1=ALU.mult), "dt_one")
                do(v.memset(xbcp[:, :, 0:2], 0.0))
                do(v.memset(xbcp[:, :, 130:134], 0.0))
                do(v.memset(xbcp[:, :, 390:392], 0.0), "conv_raw")
                for n in range(2, N_INS):
                    split_lo(n)
                    c = n - 2
                    if c >= 5:
                        continue
                    v.wait_ge(S["emptied_a"], table[("xs0", "xs1", "xs2", "B", "C")[c]].count)
                    do(TS(conv[:, c, :], xbcp[:, c, 0:CONVW], col("conv_w", c), None, ALU.mult))
                    for k in range(1, 5):
                        do(STT(out=conv[:, c, :], in0=xbcp[:, c, k:k + CONVW], scalar=col("conv_w", 5 * k + c), in1=conv[:, c, :],
                               op0=ALU.mult, op1=ALU.add), "conv_in" if k == 4 else "v_chain")
                b = filled("cs")
                do(v.tensor_copy(csc[:, :, :, :].rearrange("p w t u -> p (w t u)"), b[:, 0:72]), "emptied_v")
                do(TTT(wst[:, :, :], csc[:, 1], csc[:, 0], ALU.subtract), "cs_pre")
                v.wait_ge(S["cs_exp"], 2)
                do(TTT(wst[:, :, :], wst[:, :, :], dts[:, :, :], ALU.mult))
                for gg in range(2):
                    r = slice(64 * gg, 64 * gg + 64)
                    src = dec[r].rearrange("p t (d h) -> p t d h", d=2)[:, :, :, 3 * gg:3 * gg + 3]
                    do(v.tensor_copy(dec2[r], src))
                do(v.memset(sin[:, 0].rearrange("p d i v -> p (d i v)"), 0.0))
                do(v.tensor_copy(sin[:, 1, 0].rearrange("p i v -> p (i v)"), bktok[:, 0, 0, 0:192]))
                do(v.tensor_copy(sin[:, 2, 1].rearrange("p i v -> p (i v)"), bktok[:, 0, 0, 192:384]))
                ada_later(4)
                for t in range(TT):
                    if t > 0:
                        v.wait_ge(S["bank_full"], table[f"lst{t - 1}"].n + 1)
                    v.wait_ge(S["emptied_a"], table[f"xtr{t}"].count)
                    for gg in range(2):
                        for d in range(2):
                            xs = tok[:, t, 192 * gg:192 * gg + 192].rearrange("p (i v) -> p i v", i=3)
                            do(TTT(xwt[:, gg, d], xs, bc3(wst[:, t, 6 * d + 3 * gg:6 * d + 3 * gg + 3], 3, 64), ALU.mult), "xw_ready")
                    b = filled(f"lst{t}")
                    do(v.tensor_copy(loc[:, t].rearrange("p d i v -> p (d i v)"), b[:, 0:384]), "emptied_v")
                for d, t0, t1 in ((0, 1, 2), (1, 2, 1)):
                    do(TTT(sin[:, t1, d], sin[:, t0, d], bc3(dec2[:, t0, d], 3, 64), ALU.mult))
                    do(TTT(sin[:, t1, d], sin[:, t1, d], loc[:, t0, d], ALU.add), "s_ready" if d == 1 else "v_chain")
                for t in range(TT):
                    if t > 0:
                        v.wait_ge(S["bank_full"], table[f"yb{t - 1}"].n + 1)
                    for q in range(3):
                        b = filled(f"csr{t}{q}")
                        u0 = 4 * q
                        do(TTT(diff[:, u0:u0 + 4, :], b[:, :].rearrange("p (u t) -> p u t", u=4),
                               bc3(csc[:, 0, t, u0:u0 + 4], 4, P), ALU.subtract), "csr_read")
                    for d in range(2):
                        nm = cc(C_NF if d == 0 else C_NB).unsqueeze(1).to_broadcast([P, 6, P])
                        dv = diff[:, 6 * d:6 * d + 6, :]
                        do(STT(out=dv, in0=dv, scalar=0.0, in1=nm, op0=ALU.min, op1=ALU.add), "d_ready")
                    v.wait_ge(S["ec_ready"], 3 * t + 3)
                    for gg in range(2):
                        r = slice(64 * gg, 64 * gg + 64)
                        for d in range(2):
                            u = slice(6 * d + 3 * gg, 6 * d + 3 * gg + 3)
                            cb_ = conv[r, 4, TOF[t]:TOF[t] + P].unsqueeze(1).to_broadcast([64, 3, P])
                            do(TTT(cdec[r, u, :], ecs[r, u, :], cb_, ALU.mult), "cd_ready")
                    v.wait_ge(S["e_ready"], 2 * t + 2)
                    for d in range(2):
                        dv = diff[:, 6 * d:6 * d + 6, :]
                        do(TTT(dv, dv, bc3(dts[:, t, 6 * d:6 * d + 6], 6, P), ALU.mult))
                    do(TTT(gmat[:, :, :], diff[:, 0:6, :], diff[:, 6:12, :], ALU.add))
                    for gg in range(2):
                        b = filled(f"cb{t}{gg}")
                        gv = gmat[:, 3 * gg:3 * gg + 3, :]
                        do(TTT(gv, b[:, 0:P].unsqueeze(1).to_broadcast([P, 3, P]), gv, ALU.mult), "emptied_v")
                    tell("g_ready")
                    ada_later(5 + t)
                    for gg, pieces in ((0, ((0, 0, 128), (1, 0, 64))), (1, ((1, 64, 128), (2, 0, 128)))):
                        b = filled(f"y{'ab'[gg]}{t}")
                        for n, (j, lo, hi) in enumerate(pieces):
                            do(STT(out=yv[lo:hi, j, P * t:P * t + P], in0=conv[lo:hi, j, TOF[t]:TOF[t] + P], scalar=dcol[lo:hi, j:j + 1],
                                   in1=b[lo:hi, P * j:P * j + P], op0=ALU.mult, op1=ALU.add), "emptied_v" if n == 1 else "v_chain")
                for j in range(NJ):
                    do(TTT(yv[:, j, :], yv[:, j, :], zz[:, j, :], ALU.mult), "ssd_y")
                ada_later(8)
                v.wait_ge(S["sn_rs"], 1)
                for j in range(NJ):
                    do(STT(out=yv[:, j, :], in0=yv[:, j, :], scalar=col("ssd_g", j), in1=rs[:, :], op0=ALU.mult, op1=ALU.mult))

                v.wait_ge(S["qk_sq"], 5)
                for c in range(4):
                    do(STT(out=qk[:, c, :], in0=qk[:, c, :], scalar=col("qn" if c < 2 else "kn"), in1=rs_at[:, c, :],
                           op0=ALU.mult, op1=ALU.mult), "qk_rs")
                for q in range(2):
                    b = filled(f"rot{q}")
                    bv = b[:, :].rearrange("p (o t) -> p o t", o=2)
                    sb_, cb_ = (cc(x, LAT).unsqueeze(1).to_broadcast([P, 2, LAT]) for x in (C_SIN, C_COS))
                    tmp = sq_at[:, 0:2, 0:LAT]
                    qv = qk[:, 2 * q:2 * q + 2, P:NT]
                    do(TTT(tmp, bv, sb_, ALU.mult), "emptied_v")
                    do(TTT(qv, qv, cb_, ALU.mult))
                    do(TTT(qv, qv, tmp, ALU.add), "qk_ready")
                sc = 32 ** -0.5

                def score_max(u):
                    t, j = divmod(u, 2)
                    nmx = nmx2[u % 2]
                    for i4 in range(4):
                        b = filled(f"sc{t}{j}{i4}")
                        do(v.tensor_reduce(nmx[:, i4:i4 + 1], b[:, 0:P if t == 0 else NT], AXX, ALU.max))
                        do(TS(nmx[:, i4:i4 + 1], nmx[:, i4:i4 + 1], -sc, None, ALU.mult), "sc_max")

                def weights(u):
                    t, j = divmod(u, 2)
                    nk = P if t == 0 else NT
                    e_at, ssm = e_at2[u % 2], ssm2[u % 2]
                    v.wait_ge(S["sc_exp"], 4 * u + 4)
                    do(v.reciprocal(ssm[:, 0:4], ssm[:, 0:4]))
                    if u > 0:
                        v.wait_ge(S["bank_full"], table[f"wt{(u - 1) // 2}{(u - 1) % 2}1"].n + 1)
                    for hh in range(2):
                        e0, e1 = e_at[:, 2 * hh, 0:nk], e_at[:, 2 * hh + 1, 0:nk]
                        do(TS(e1, e1, ssm[:, 2 * hh + 1:2 * hh + 2], lam[:, 4:5], ALU.mult, ALU.mult))
                        do(STT(out=w_at[:, hh, 0:nk], in0=e0, scalar=ssm[:, 2 * hh:2 * hh + 1], in1=e1, op0=ALU.mult, op1=ALU.subtract), "w_ready")

                def values_out(u):
                    t, j = divmod(u, 2)
                    b = filled(f"pv{t}{j}")
                    do(v.tensor_copy(o_at[:, j, P * t:P * t + P], b[:, 0:P]), "emptied_v")

                score_max(0)
                for u in range(2 * TT):
                    weights(u)
                    if u + 1 < 2 * TT:
                        score_max(u + 1)
                    values_out(u)
                for j in range(2):
                    do(TTT(sq_at[:, j, :], o_at[:, j, :], o_at[:, j, :], ALU.mult), "o_ready")
                for j in range(2):
                    v.wait_ge(S["on_rs"], j + 1)
                    do(STT(out=yv[:, 6 + j, :], in0=o_at[:, j, :], scalar=lam[:, 5:6], in1=rs_at[:, j, :], op0=ALU.mult, op1=ALU.mult), "att_done")

                for j in range(NJ):
                    b = filled(f"kn{j}")
                    do(TS(ep[:, j, :], b[:, 0:NT], 1e-24, None, ALU.max), "emptied_v")
                tell("kk_max")
                v.wait_ge(S["kk_rs"], 1)
                v.wait_ge(S["kx_ready"], NJ)
                do(TTT(kkn[:, :, :], kkn[:, :, :], ep[:, :, :], ALU.mult))
                v.wait_ge(S["out_free"], 1)
                kv = rkv[:, 3:6, :]
                tile3 = lambda a: a[:, :, :].rearrange("p j (t c) -> p (j t) c", c=P)
                for d in range(2):
                    v.wait_ge(S["lora_ready"], 6 * d + 6)
                    for j in range(NJ):
                        do(v.tensor_tensor_scan(dd[:, j, :], cc(C_SCAN, NT), sig[:, j, :], 0.0, ALU.mult, ALU.add))
                    ddt, dxt, sgt = tile3(dd), tile3(dx), tile3(sig)
                    if d == 0:
                        do(v.tensor_copy(mref[:, 0:9], ddt[:, :, 64]))
                    else:
                        do(TTT(mref[:, 0:9], ddt[:, :, 64], sgt[:, :, 64], ALU.subtract))
                    do(TTT(ddt, ddt, bc3(mref, 9, P), ALU.subtract))
                    do(TTT(dx[:, :, :], dd[:, :, :], sig[:, :, :], ALU.subtract), "decay_pre")
                    ada_later(9 + d)
                    do(STT(out=sig[:, :, :], in0=aa[:, :, :], scalar=-1.0, in1=kxa[:, :, :], op0=ALU.add, op1=ALU.mult))
                    do(TTT(sig[:, :, :], sig[:, :, :], kv, ALU.add))
                    do(TTT(aa[:, :, :], aa[:, :, :], kkn[:, :, :], ALU.mult))
                    v.wait_ge(S["decay_exp"], 4 * d + 4)
                    do(v.tensor_copy(fin[d].rearrange("p j t -> p (j t)"), tile3(en)[:, :, 127 if d == 0 else 0]))
                    do(TTT(f_ka[d][:, :, :], sig[:, :, :], ep[:, :, :], ALU.mult))
                    do(TTT(f_be[d][:, :, :], aa[:, :, :], ep[:, :, :], ALU.mult))
                    do(TTT(f_al[d][:, :, :], kkn[:, :, :], dx[:, :, :], ALU.mult), "f_ready")
                ada_later(11)
                norm_gain(8, SC2, "n2")
                for s in range(3):
                    for d in range(2):
                        t = TILE_OF[d][s]
                        pb = bc3(pre[d][:, :, t], 3, 64)
                        if s == 0:
                            do(v.memset(srk[:, d].rearrange("p j v -> p (j v)"), 0.0), "s0_ready")
                        else:
                            src = sri if s == 1 else srk
                            do(TTT(srk[:, d], src[:, d], pb, ALU.mult), "s0_ready")
                    for g4 in range(4):
                        d = g4 // 2
                        strict = cc(C_US if d == 0 else C_LS).unsqueeze(1).to_broadcast([P, 3, P])
                        idb = ident.unsqueeze(1).to_broadcast([P, 3, P])
                        for name, dst, lvl in (("L1", m_x, C_LV if d == 0 else C_LVT), ("LT", m_xt, C_LVT if d == 0 else C_LV)):
                            b = filled(f"{name}{s}{g4}")[:, 0:384].rearrange("p (i t) -> p i t", i=3)
                            mk = cc(lvl).unsqueeze(1).to_broadcast([P, 3, P])
                            if name == "LT":
                                do(TTT(m_lt[:, g4], b, strict, ALU.mult))
                            do(TTT(dst[:, g4], b, mk, ALU.mult), "emptied_v")
                            do(TTT(dst[:, g4], dst[:, g4], idb, ALU.add), "x1_ready")
                    for lv in range(1, 7):
                        for g4 in range(4):
                            d = g4 // 2
                            mk = cc((C_LV if d == 0 else C_LVT) + P * lv).unsqueeze(1).to_broadcast([P, 3, P])
                            b = filled(f"W{s}{lv}{g4}")
                            do(TTT(m_nw[:, g4], b[:, 0:384].rearrange("p (i t) -> p i t", i=3), mk, ALU.mult), "emptied_v")
                            do(TTT(m_nw[:, g4], m_nw[:, g4], ident.unsqueeze(1).to_broadcast([P, 3, P]), ALU.add), "nw_ready")
                    for g4 in range(4):
                        b = filled(f"rh{s}{g4}")
                        do(v.tensor_copy(rhs_b[:, g4], b[:, 0:192].rearrange("p (i v) -> p i v", i=3)), "emptied_v")
                    for g4 in range(4):
                        b = filled(f"u{s}{g4}")
                        do(TS(nu_b[:, g4], b[:, 0:192].rearrange("p (i v) -> p i v", i=3), -1.0, None, ALU.mult), "emptied_v")
                    for d in range(2):
                        t = TILE_OF[d][s]
                        b = filled(f"ry{s}{d}")
                        bv = b[:, 0:384].rearrange("p (j t) -> p j t", j=3)
                        yo = yv[:, 3:6, P * t:P * t + P]
                        if (s == 0 and d == 0) or s == 1:
                            do(v.tensor_copy(yo, bv), "emptied_v")
                        else:
                            do(TTT(yo, bv, yo, ALU.add), "emptied_v")
                    for d in range(2):
                        t = TILE_OF[d][s]
                        b = filled(f"rs{s}{d}")
                        bv = b[:, 0:192].rearrange("p (j v) -> p j v", j=3)
                        do(TTT(srk[:, d], bv, srk[:, d], ALU.add), "emptied_v")
                        do(TTT(srk[:, d], srk[:, d], bc3(fin[d][:, :, t], 3, 64), ALU.mult))
                        if s == 0:
                            do(v.tensor_copy(rs[:, 192 * d:192 * d + 192], sri[:, d].rearrange("p j v -> p (j v)")))
                            do(v.tensor_copy(sri[:, d], srk[:, d]), "rwkv_st")
                    if s == 0:
                        v.wait_ge(S["bank_full"], table["rfin1"].n + 1)
                        do(v.tensor_copy(sri[:, :, :, :].rearrange("p d j v -> p (d j v)"), rs[:, 0:384]))
                tell("rwkv_y")
                for j in range(NJ):
                    b = filled(f"mu{j}")
                    do(STT(out=dd[:, j, :], in0=b[:, 0:NT], scalar=-1.0 / 64, in1=yv[:, 3 + j, :], op0=ALU.mult, op1=ALU.add), "emptied_v")
                    do(TTT(en[:, j, :], dd[:, j, :], dd[:, j, :], ALU.mult), "gn_c")
                for j in range(NJ):
                    do(STT(out=ep[:, j, :], in0=rkv[:, j, :], scalar=col("rk", j), in1=rkv[:, 3 + j, :], op0=ALU.mult, op1=ALU.mult), "bon_in")
                for j in range(NJ):
                    v.wait_ge(S["gn_rs"], j + 1)
                    do(STT(out=dd[:, j, :], in0=dd[:, j, :], scalar=col("ln_g", j), in1=dx[:, j, :], op0=ALU.mult, op1=ALU.mult))
                for j in range(NJ):
                    b = filled(f"bon{j}")
                    do(TTT(sig[:, j, :], b[:, 0:NT], rkv[:, 6 + j, :], ALU.mult), "emptied_v")
                    do(STT(out=dd[:, j, :], in0=dd[:, j, :], scalar=col("ln_b", j), in1=sig[:, j, :], op0=ALU.add, op1=ALU.add))
                for j in range(NJ):
                    b = filled(f"gt{j}")
                    do(TTT(yv[:, 3 + j, :], b[:, 0:NT], dd[:, j, :], ALU.mult), "emptied_v")
                    tell("y_ready")
                for m in range(KD):
                    b = filled(f"out{m}")
                    for n, (st, lo, hi) in enumerate(seg):
                        do(STT(out=x_t[:, m, lo:hi], in0=b[:, lo:hi], scalar=mod[:, G1 + m, st:st + 1], in1=x_t[:, m, lo:hi],
                               op0=ALU.mult, op1=ALU.add), "emptied_v" if n == 1 else "v_chain")
                    do(TTT(sq2[:, m, :], x_t[:, m, :], x_t[:, m, :], ALU.mult), "x2_ready")
                v.wait_ge(S["h2_part"], 1)
                for c in range(KD):
                    do(TTT(hv[:, c, :], x_t[:, c, :], rs[:, :], ALU.mult), "x2_ready")
                    do(TS(hv[:, c, 0:P], hv[:, c, 0:P], gs[:, 8 + c, 1:2], mod[:, SH2 + c, 1:2], ALU.mult, ALU.add), "hc2_ready")
                b = filled("rtr")
                do(v.tensor_copy(lg_rows, b[0:20, 0:NT]), "emptied_v")
                b = filled("rt")
                rb = bcr[:, BC["rbias"]:BC["rbias"] + 20].unsqueeze(1).to_broadcast([P, 3, 20])
                do(TTT(lg, b[:, 0:60].rearrange("p (t u) -> p t u", t=3), rb, ALU.add), "emptied_v")
                iota = cc(C_IOTA, 4).unsqueeze(1).to_broadcast([P, 3, 4])
                b4 = lambda a: a.to_broadcast([P, 3, 4])

                def first_max(src, top, hot):
                    do(v.tensor_reduce(top, src, AXX, ALU.max))
                    do(TTT(hot, src, b4(top), ALU.is_equal))
                    do(TTT(hot, hot, iota, ALU.mult))
                    do(v.tensor_reduce(r5, hot, AXX, ALU.max))
                    do(TTT(hot, hot, b4(r5), ALU.is_equal))

                g4_, e16 = lg[:, :, 0:4], lg[:, :, 4:20].rearrange("p t (g e) -> p t g e", g=4)
                first_max(g4_, r1, rg1)
                do(TTT(rg2, g4_, b4(r1), ALU.subtract), "rt_pre")
                e3 = rg3.rearrange("p t (g e) -> p t g e", g=4)
                for gg in range(4):
                    do(TTT(e3[:, :, gg, :], e16[:, :, gg, :], b4(rg1[:, :, gg:gg + 1]), ALU.mult))
                do(v.tensor_reduce(rg4, rg3.rearrange("p t (g e) -> p t e g", g=4), AXX, ALU.add))
                first_max(rg4, r2, rg5)
                do(STT(out=rg4, in0=rg5, scalar=NEG, in1=rg4, op0=ALU.mult, op1=ALU.add))
                first_max(rg4, r3, rg6)
                do(TTT(r3, r3, r2, ALU.subtract), "rt_pre")
                v.wait_ge(S["rt_exp"], 2)
                do(v.tensor_reduce(r1, rg2, AXX, ALU.add))
                do(v.reciprocal(r1, r1))
                do(TS(r4, r3, 1.0, None, ALU.add))
                do(v.reciprocal(r4, r4))
                do(TTT(r4, r4, r1, ALU.mult))
                do(TTT(r3, r3, r4, ALU.mult))
                do(TTT(rg5, rg5, b4(r4), ALU.mult))
                do(TTT(rg6, rg6, b4(r3), ALU.mult))
                do(TTT(rg5, rg5, rg6, ALU.add))
                gt_ = gate.rearrange("p t (g e) -> p t g e", g=4)
                for gg in range(4):
                    do(TTT(gt_[:, :, gg, :], rg5, b4(rg1[:, :, gg:gg + 1]), ALU.mult), "gate_ready" if gg == 3 else "v_chain")
                v.wait_ge(S["hhi_moe"], 1)
                do(TTT(h_lo, hv, h_hi, ALU.subtract), "hlo_moe")
                v.wait_ge(S["emptied_a"], table[f"gb{EXPERTS - 1}"].count)
                tell("t_moe")
                with v.Fori(0, EXPERTS // 2) as jj:
                    for e in range(2):
                        for i3 in range(3):
                            k = PRE_SLOTS + 3 * e + i3
                            v.wait_ge(S["hi_moe"], jj * 12 + (6 * e + 2 * i3 + 2))
                            for hf in range(2):
                                part = slice(1024 * hf, 1024 * hf + 1024)
                                i = TTT(w_lo(k)[:, part], slot(k)[:, part], w_hi[i3][hf], ALU.subtract)
                            i.then_inc(S["lo_moe"], 1)
                        for m in range(2):
                            n = 2 * e + m
                            v.wait_ge(S["hp_moe"], jj * 8 + (2 * n + 2))
                            v.wait_ge(S["s_moe"], jj * 4 + (n + 2))
                            TTT(th[:, m, :], ps[:, 7, 0:NT], sh[:, m, :], ALU.mult).then_inc(S["t_moe"], 1)
                            v.wait_ge(S["t_moe"], jj * 4 + (n + 2))
                            TTT(th[:, m, :], th[:, m, :], gates[:, bass.ds(jj * 2 + e, 1), :].rearrange("p a t -> p (a t)"),
                                ALU.mult).then_inc(S["hid_moe"], 1)
                            v.wait_ge(S["hid_moe"], jj * 8 + (2 * n + 1))
                            v.tensor_copy(hid_hi[:, m, :], th[:, m, :]).then_inc(S["hid_moe"], 1)
                            v.wait_ge(S["hid_moe"], jj * 8 + (2 * n + 2))
                            TTT(hid_lo[:, m, :], th[:, m, :], hid_hi[:, m, :], ALU.subtract).then_inc(S["t2_moe"], 1)
                            v.wait_ge(S["t2_moe"], jj * 4 + (n + 1))
                v.wait_ge(S["moe_y"], 1)
                for t in range(TT):
                    for hf in range(2):
                        do(v.tensor_copy(ytok[:, t, 512 * hf:512 * hf + 512], ps[:, 2 * t + hf, :]), "moe_tok")
                for c in range(KD):
                    b = filled(f"ytr{c}")
                    for n, (st, lo, hi) in enumerate(seg):
                        do(STT(out=x_t[:, c, lo:hi], in0=b[:, lo:hi], scalar=mod[:, G2 + c, st:st + 1], in1=x_t[:, c, lo:hi],
                               op0=ALU.mult, op1=ALU.add), "emptied_v" if n == 1 else "v_chain")
                meet(v, l + 1)
                cnt.clear()

        @block.scalar
        def _(a):
            cnt = counter()
            tb = [pre_table]

            def do(ins, name="a_chain"):
                step(a, cnt, ins, name)

            def filled(name):
                a.wait_ge(S["bank_full"], tb[0][name].n + 1)
                return bank(tb[0][name])

            def tell(name):
                cnt[name] = cnt.get(name, 0) + 1
                a.sem_inc(S[name], 1)

            def act(out, in_, f, **kw):
                return a.activation(out, in_, f, **kw)

            def exp_ln_tables():
                a.preload_act_table_set("natural_log_exp_and_others")

            eps = cst[:, C_EPS:C_EPS + 1]
            a.dma_start(cst[:, P:C_N], consts_d[:, P:C_N]).then_inc(cst_rest, 16)
            b = filled("cond")
            do(act(scond[:, :, :], b[:, 0:16].rearrange("p (s c) -> p c s", s=2), ACT.Silu), "emptied_a")
            meet(a, 0)
            cnt.clear()
            tb[0] = table
            with a.Fori(0, DEPTH) as l:
                exp_ln_tables()

                def ada_copy(q):
                    b = filled(f"ar{q}")
                    if q > ADA_EARLY:
                        a.wait_ge(S["bank_full"], table[f"at{q - 1}"].n + 1)
                    do(act(ada_row(q), b[0:2, :], ACT.Copy), "emptied_a")

                for q in range(ADA_EARLY):
                    ada_copy(q)
                a.wait_ge(S["lam_pre"], 1)
                do(act(lam[:, 2:4], lam[:, 0:2], ACT.Exp), "lam_exp")
                do(act(avl, bcr[:, BC["a_log"]:BC["a_log"] + 12], ACT.Exp), "lam_exp")
                b = filled("sum1")
                do(act(rs[:, :], b[:, 0:NT], ACT.Ln, scale=1.0 / D, bias=eps), "emptied_a")
                do(act(rs[:, :], rs[:, :], ACT.Exp, scale=-0.5), "h_part")
                a.wait_ge(S["mod_ready"], 1)
                for c in range(KD):
                    a.wait_ge(S["x_ready"], c + 1)
                    do(act(hv[:, c, P:NT], hv[:, c, P:NT], ACT.Identity, scale=gs[:, c, 0:1], bias=mod[:, SH1 + c, 0:1]), "h_ready")
                a.wait_ge(S["hc_ready"], KD)
                do(act(hin_hi, hv, ACT.Copy), "hhi_in")

                def split_hi(n):
                    k = IN_SLOT0 + n
                    a.wait_ge(ring_full[k % RING], lring(l, k % RING) + ring_value(k))
                    a.sem_inc(S["passed"], 1)
                    if n >= 2:
                        a.wait_ge(ring_free, l * LAYER_SLOTS + (RING + k - 1))
                        a.sem_inc(S["passed"], 1)
                    w, whi, _ = in_parts(n)
                    for hf in range(2):
                        do(act(whi[hf], w[hf], ACT.Copy), "hi_in")

                split_hi(0)
                split_hi(1)
                a.wait_ge(S["dt_pre"], 1)
                do(act(dta[:, :, :], dts[:, :, :], ACT.Abs), "dt_sp")
                do(act(dta[:, :, :], dta[:, :, :], ACT.Exp, scale=-1.0), "dt_sp")
                do(act(dta[:, :, :], dta[:, :, :], ACT.Ln, bias=1.0), "dt_sp")
                a.wait_ge(S["conv_raw"], 1)
                for n, slot_ in enumerate(IN_SLOTS):
                    for name, _ in slot_:
                        if name == "va":
                            b = filled("va0")
                            do(act(vat[:, 0:2, :], b[:, :].rearrange("p (t n) -> p t n", t=2), ACT.Copy), "emptied_a")
                            b = filled("va1")
                            do(act(vat[:, 2, :], b[:, 0:256], ACT.Copy), "emptied_a")
                            continue
                        b = filled(name)
                        if name in ("xs0", "xs1", "xs2", "B", "C"):
                            c = ("xs0", "xs1", "xs2", "B", "C").index(name)
                            do(act(xbcp[:, c, 2:130], b[:, 0:P], ACT.Copy))
                            do(act(xbcp[:, c, 134:390], b[:, P:NT], ACT.Copy), "emptied_a")
                        elif name[0] == "z":
                            do(act(zz[:, int(name[1]), :], b[:, 0:NT], ACT.Silu), "emptied_a")
                        elif name == "xwa":
                            do(act(xwa[0:64, :], b[0:64, 0:NT], ACT.Tanh))
                            do(act(xwa[64:128, :], b[64:128, 0:NT], ACT.Copy), "emptied_a")
                        elif name == "xg":
                            do(act(xg[:, :], b[:, 0:NT], ACT.Sigmoid), "emptied_a")
                        else:
                            if name[0] == "q":
                                dst = qk[:, int(name[1]), :]
                            elif name[0] == "k":
                                dst = qk[:, 2 + int(name[1]), :]
                            else:
                                dst = rkv[:, {"r": 0, "v": 6}[name[0]] + int(name[1]) if name[:2] != "rk" else 3 + int(name[2]), :]
                            do(act(dst, b[:, 0:NT], ACT.Copy), "emptied_a")
                    if n + 2 < N_INS:
                        split_hi(n + 2)
                for c in range(5):
                    a.wait_ge(S["conv_in"], c + 1)
                    do(act(conv[:, c, :], conv[:, c, :], ACT.Silu, bias=col("conv_b", c)), "conv_done")
                exp_ln_tables()
                a.wait_ge(S["cs_pre"], 1)
                do(act(wst[:, :, :], wst[:, :, :], ACT.Exp), "cs_exp")
                do(act(dec[:, :, :], csc[:, 1], ACT.Exp), "cs_exp")
                ada_copy(4)
                for t in range(TT):
                    b = filled(f"xtr{t}")
                    do(act(tok[:, t, :], b[:, :], ACT.Copy), "emptied_a")
                ada_copy(5)
                for t in range(TT):
                    if t > 0:
                        a.wait_ge(S["cd_ready"], 4 * t)
                    for q in range(3):
                        b = filled(f"csr{t}{q}")
                        a.wait_ge(S["csr_read"], 3 * t + q + 1)
                        do(act(ecs[:, 4 * q:4 * q + 4, :], b[:, :].rearrange("p (u t) -> p u t", u=4), ACT.Exp), "emptied_a")
                        tell("ec_ready")
                    for d in range(2):
                        a.wait_ge(S["d_ready"], 2 * t + d + 1)
                        dv = diff[:, 6 * d:6 * d + 6, :]
                        do(act(dv, dv, ACT.Exp), "e_ready")
                    ada_copy(6 + t)
                for d in range(2):
                    b = filled(f"sfin{d}")
                    do(act(stg[0:64, 384 * d:384 * d + 384], b[0:64, 0:384], ACT.Copy), "emptied_a")
                    tell("stage_ssd")
                for j in range(NJ):
                    a.wait_ge(S["ssd_y"], j + 1)
                    do(act(rs_at[:, j, :], yv[:, j, :], ACT.Square), "yssd_sq")
                ada_copy(9)
                b = filled("sn")
                do(act(rs[:, :], b[:, 0:NT], ACT.Ln, scale=1.0 / 384, bias=eps), "emptied_a")
                do(act(rs[:, :], rs[:, :], ACT.Exp, scale=-0.5), "sn_rs")
                do(act(sq_at[:, :, :], qk[:, :, :], ACT.Square), "qk_sq")
                for c in range(4):
                    b = filled(f"qn{c}")
                    do(act(rs_at[:, c, :], b[:, 0:NT], ACT.Ln, bias=eps), "emptied_a")
                    do(act(rs_at[:, c, :], rs_at[:, c, :], ACT.Exp, scale=-0.5), "qk_sq")
                b = filled("kout")
                do(act(stg[:, 768:1024], b[:, 0:256], ACT.Copy), "emptied_a")
                tell("stage_kv")
                for j in range(NJ):
                    do(act(kkn[:, j, :], rkv[:, 3 + j, :], ACT.Copy, scale=col("kk", j)))
                    do(act(kxa[:, j, :], rkv[:, 3 + j, :], ACT.Copy, scale=col("ka", j)), "kx_ready")
                sc = 32 ** -0.5

                def score_exp(u):
                    t, j = divmod(u, 2)
                    nk = P if t == 0 else NT
                    if u > 1:
                        a.wait_ge(S["w_ready"], 2 * (u - 1))
                    for i4 in range(4):
                        b = filled(f"sc{t}{j}{i4}")
                        a.wait_ge(S["sc_max"], 4 * u + i4 + 1)
                        do(act(e_at2[u % 2][:, i4, 0:nk], b[:, 0:nk], ACT.Exp, scale=sc, bias=nmx2[u % 2][:, i4:i4 + 1],
                               accum_out=ssm2[u % 2][:, i4:i4 + 1]), "emptied_a")
                        tell("sc_exp")

                score_exp(0)
                for u in range(2 * TT):
                    if u + 1 < 2 * TT:
                        score_exp(u + 1)
                    t, j = divmod(u, 2)
                    nk = P if t == 0 else NT
                    for hh in range(2):
                        b = filled(f"wt{t}{j}{hh}")
                        do(act(wt_at[:, hh, 0:nk], b[:, 0:nk], ACT.Copy), "emptied_a")
                for j in range(2):
                    b = filled(f"on{j}")
                    do(act(rs_at[:, j, :], b[:, 0:NT], ACT.Ln, scale=1.0 / 64, bias=eps), "emptied_a")
                    do(act(rs_at[:, j, :], rs_at[:, j, :], ACT.Exp, scale=-0.5), "on_rs")
                a.wait_ge(S["att_done"], 2)
                do(act(en[:, :, :], kkn[:, :, :], ACT.Square), "kk_sq")
                a.wait_ge(S["kk_max"], 1)
                do(act(ep[:, :, :], ep[:, :, :], ACT.Ln, scale=65536.0))
                do(act(ep[:, :, :], ep[:, :, :], ACT.Exp, scale=-0.5, bias=cst[:, C_KKB:C_KKB + 1]), "kk_rs")
                for d in range(2):
                    if d == 1:
                        a.wait_ge(S["f_ready"], 1)
                        a.wait_ge(S["rho_ready"], 1)
                    for j in range(NJ):
                        b = filled(f"lw{d}{j}")
                        do(act(sig[:, j, :], b[:, 0:NT], ACT.Sigmoid, bias=col("w0", 3 * d + j)), "emptied_a")
                        tell("lora_ready")
                        b = filled(f"la{d}{j}")
                        do(act(aa[:, j, :], b[:, 0:NT], ACT.Sigmoid, bias=col("a0", 3 * d + j)), "emptied_a")
                        tell("lora_ready")
                    ada_copy(10 + d)
                    exp_ln_tables()
                    a.wait_ge(S["decay_pre"], d + 1)
                    pr = pre[d].rearrange("p j t -> p (j t)")
                    if d == 0:
                        do(act(pr, mref[:, 0:9], ACT.Exp, scale=-G), "decay_exp")
                        do(act(en[:, :, :], dd[:, :, :], ACT.Exp, scale=-G), "decay_exp")
                        do(act(ep[:, :, :], dd[:, :, :], ACT.Exp, scale=G), "decay_exp")
                        do(act(dx[:, :, :], dx[:, :, :], ACT.Exp, scale=-G), "decay_exp")
                    else:
                        do(act(pr, dd[:, :, :].rearrange("p j (t c) -> p (j t) c", c=P)[:, :, 127], ACT.Exp, scale=-G), "decay_exp")
                        do(act(en[:, :, :], dx[:, :, :], ACT.Exp, scale=G), "decay_exp")
                        do(act(ep[:, :, :], dx[:, :, :], ACT.Exp, scale=-G), "decay_exp")
                        do(act(dx[:, :, :], dd[:, :, :], ACT.Exp, scale=G), "decay_exp")
                for t in range(TT):
                    b = filled(f"vt{t}")
                    do(act(vtok[:, t, :], b[:, 0:NT], ACT.Copy), "emptied_a")
                for s in range(3):
                    if s > 0:
                        a.wait_ge(S["bank_full"], table[f"rs{s - 1}1"].n + 1)
                    for d in range(2):
                        for w in range(2):
                            b = filled(f"{'bk'[w]}t{s}{d}")
                            do(act(bktok[:, d, w, :], b[:, 0:NT], ACT.Copy), "emptied_a")
                    for g4 in range(4):
                        for name, dst in (("L2", m_l2), ("M1", m_m1), ("M2", m_m2)):
                            b = filled(f"{name}{s}{g4}")
                            do(act(dst[:, g4], b[:, 0:384].rearrange("p (i t) -> p i t", i=3), ACT.Copy), "emptied_a")
                            tell("mask_in")
                    for lv in range(1, 7):
                        for g4 in range(4):
                            if lv < 6:
                                b = filled(f"X{s}{lv}{g4}")
                                do(act(m_x[:, g4], b[:, 0:384].rearrange("p (i t) -> p i t", i=3), ACT.Copy), "emptied_a")
                            b = filled(f"T{s}{lv}{g4}")
                            do(act(m_xt[:, g4], b[:, 0:384].rearrange("p (i t) -> p i t", i=3), ACT.Copy), "emptied_a")
                    if s == 0:
                        a.wait_ge(S["out_free"], 1)
                        for d in range(2):
                            b = filled(f"rfin{d}")
                            do(act(stg[0:64, 384 * d:384 * d + 384], b[0:64, 0:384], ACT.Copy), "emptied_a")
                            tell("stage_rwkv")
                for j in range(NJ):
                    b = filled(f"var{j}")
                    do(act(dx[:, j, :], b[:, 0:NT], ACT.Ln, scale=1.0 / 64, bias=cst[:, C_GN:C_GN + 1]), "emptied_a")
                    do(act(dx[:, j, :], dx[:, j, :], ACT.Exp, scale=-0.5), "gn_rs")
                a.wait_ge(S["mod_ready"], 2)
                b = filled("sum2")
                do(act(rs[:, :], b[:, 0:NT], ACT.Ln, scale=1.0 / D, bias=eps), "emptied_a")
                do(act(rs[:, :], rs[:, :], ACT.Exp, scale=-0.5), "h2_part")
                for c in range(KD):
                    a.wait_ge(S["x2_ready"], KD + c + 1)
                    do(act(hv[:, c, P:NT], hv[:, c, P:NT], ACT.Identity, scale=gs[:, 8 + c, 0:1], bias=mod[:, SH2 + c, 0:1]), "h2_ready")
                a.wait_ge(S["hc2_ready"], KD)
                do(act(h_hi, hv, ACT.Copy), "hhi_moe")
                a.wait_ge(S["rt_pre"], 2)
                do(act(rg2, rg2, ACT.Exp), "rt_exp")
                do(act(r3, r3, ACT.Exp), "rt_exp")
                for e in range(EXPERTS):
                    b = filled(f"gb{e}")
                    do(act(gates[:, e, :], b[:, 0:NT], ACT.Copy), "emptied_a")
                tell("s_moe")
                with a.Fori(0, EXPERTS // 2) as jj:
                    for e in range(2):
                        for i3 in range(3):
                            k = PRE_SLOTS + 3 * e + i3
                            a.wait_ge(ring_full[k % RING], jj * 16 + (lring(l, k % RING) + ring_value(k)))
                            a.sem_inc(S["passed"], 1)
                            a.wait_ge(ring_free, jj * 6 + (l * LAYER_SLOTS + (RING + k - 2)))
                            for hf in range(2):
                                act(w_hi[i3][hf], slot(k)[:, 1024 * hf:1024 * hf + 1024], ACT.Copy).then_inc(S["hi_moe"], 1)
                        for m in range(2):
                            n = 2 * e + m
                            a.wait_ge(S["hp_moe"], jj * 8 + (2 * n + 1))
                            act(sh[:, m, :], ps[:, 6, 0:NT], ACT.Silu).then_inc(S["s_moe"], 1)
                meet(a, l + 1)
                cnt.clear()
            tb[0] = post_table
            for t in range(TT):
                for hf in range(2):
                    b = filled(f"o{t}{hf}")
                    do(act(xin[:, t, 512 * hf:512 * hf + 512], b[:, :], ACT.Copy), "emptied_a")
                    tell("tok_done")


_OUTS = [(1, CTX, D), (1, LAT, D), (1, DEPTH, CTX, 4, 2, 32), (1, DEPTH, CTX, 4, 64), (1, DEPTH, 2, HEADS, 64, 64), (1, DEPTH, 2, HEADS, 64, 64)]


def kernel(**inputs):
    import numpy as _np
    import concourse.bacc as _bacc
    from concourse import mybir as _mybir
    from concourse.bass_utils import run_bass_kernel_spmd as _run

    nc = _bacc.Bacc("TRN2", target_bir_lowering=False, num_devices=1)
    arrays, aps = {}, {}
    for name, value in inputs.items():
        value = _np.ascontiguousarray(value)
        arrays["in_" + name] = value
        aps[name] = nc.dram_tensor("in_" + name, value.shape, _mybir.dt.float32, kind="ExternalInput").ap()
    arrays["shape_constants"] = shape_constants()
    arrays["layer_constants"] = layer_constants()
    consts = nc.dram_tensor("shape_constants", (P, C_N), _mybir.dt.float32, kind="ExternalInput").ap()
    lconst = nc.dram_tensor("layer_constants", (DEPTH, 2), _mybir.dt.float32, kind="ExternalInput").ap()
    outs = [nc.dram_tensor(f"out_{i}", s, _mybir.dt.float32, kind="ExternalOutput").ap() for i, s in enumerate(_OUTS)]
    build(nc, aps, outs, consts, lconst)
    r = _run(nc, [arrays], core_ids=[0])
    return tuple(r.results[0][f"out_{i}"] for i in range(len(_OUTS)))
```
